# Optimizing a Trainium2 kernel written in Bass

```python
import jax, jax.numpy as jnp
from jax import lax
import numpy as np

D_MODEL = 1024
BATCH = 1
SEQ = 256
DEPTH = 1

SSD_HEADS = 8
SSD_HEAD_DIM = 64
SSD_D = SSD_HEADS * SSD_HEAD_DIM
SSD_GROUPS = 2
SSD_STATE = 128
SSD_CONV = 4
SSD_CHUNK = 128
SSD_CONV_DIM = SSD_D + 2 * SSD_GROUPS * SSD_STATE
SSD_COLS = SSD_D + SSD_CONV_DIM + SSD_HEADS

RWKV_HEADS = 8
RWKV_HEAD_DIM = 64
RWKV_D = RWKV_HEADS * RWKV_HEAD_DIM
DECAY_LORA = 64
AAA_LORA = 64
GATE_LORA = 128
RWKV_COLS = 3 * RWKV_D + DECAY_LORA + AAA_LORA + GATE_LORA
RWKV_GN_EPS = 64e-5

D_MIX = SSD_D + RWKV_D
D_IN = SSD_COLS + RWKV_COLS

D_FF = 2816
FFN_CONV = 3
NORM_EPS = 1e-6


def _rms_norm(x, g):
    xf = x.astype(jnp.float32)
    y = xf * lax.rsqrt(jnp.mean(xf * xf, axis=-1, keepdims=True) + NORM_EPS)
    return (y * g.astype(jnp.float32)).astype(x.dtype)

def _causal_dwconv(x, w, b):
    K, C = w.shape
    y = lax.conv_general_dilated(
        x, w[:, None, :].astype(x.dtype), window_strides=(1,), padding=[(K - 1, 0)],
        dimension_numbers=("NWC", "WIO", "NWC"), feature_group_count=C)
    return y + b.astype(x.dtype)

def _token_shift(x):
    return jnp.pad(x, ((0, 0), (1, 0), (0, 0)))[:, :-1]

def _segsum(a):
    cs = jnp.cumsum(a, axis=-1)
    diff = cs[..., :, None] - cs[..., None, :]
    L = a.shape[-1]
    mask = jnp.tril(jnp.ones((L, L), dtype=bool))
    return jnp.where(mask, diff, -jnp.inf)

def _ssd_chunked(xh, dt, A, Bg, Cg):
    b, T, h, p = xh.shape
    g, n = Bg.shape[2], Bg.shape[3]
    c, L = T // SSD_CHUNK, SSD_CHUNK
    Bh = jnp.repeat(Bg, h // g, axis=2).reshape(b, c, L, h, n)
    Ch = jnp.repeat(Cg, h // g, axis=2).reshape(b, c, L, h, n)
    X = (xh * dt[..., None]).reshape(b, c, L, h, p)
    a = (dt * A).reshape(b, c, L, h).transpose(0, 3, 1, 2)
    a_cs = jnp.cumsum(a, axis=-1)
    decay_in = jnp.exp(_segsum(a))
    scores = jnp.einsum("bclhn,bcshn->bhcls", Ch, Bh)
    y_diag = jnp.einsum("bhcls,bcshp->bclhp", scores * decay_in, X)
    decay_states = jnp.exp(a_cs[..., -1:] - a_cs)
    states = jnp.einsum("bclhn,bhcl,bclhp->bchpn", Bh, decay_states, X)
    chunk_decay = jnp.pad(a_cs[..., -1], ((0, 0), (0, 0), (1, 0)))
    decay_chunk = jnp.exp(_segsum(chunk_decay))
    states_p = jnp.concatenate([jnp.zeros_like(states[:, :1]), states], axis=1)
    states_in = jnp.einsum("bhzc,bchpn->bzhpn", decay_chunk, states_p)[:, :-1]
    y_off = jnp.einsum("bclhn,bchpn,bhcl->bclhp", Ch, states_in, jnp.exp(a_cs))
    return (y_diag + y_off).reshape(b, T, h, p)

def _ssd_mixer(p, conv_w, conv_b, dt_bias, a_log, d_skip, norm_g):
    b, T, _ = p.shape
    z, xbc, dt = jnp.split(p, [SSD_D, SSD_D + SSD_CONV_DIM], axis=-1)
    xbc = jax.nn.silu(_causal_dwconv(xbc, conv_w.astype(jnp.float32), conv_b.astype(jnp.float32)))
    xs, Bm, Cm = jnp.split(xbc, [SSD_D, SSD_D + SSD_GROUPS * SSD_STATE], axis=-1)
    xh = xs.reshape(b, T, SSD_HEADS, SSD_HEAD_DIM)
    Bm = Bm.reshape(b, T, SSD_GROUPS, SSD_STATE)
    Cm = Cm.reshape(b, T, SSD_GROUPS, SSD_STATE)
    dt = jax.nn.softplus(dt + dt_bias.astype(jnp.float32))
    A = -jnp.exp(a_log.astype(jnp.float32))
    y = _ssd_chunked(xh, dt, A, Bm, Cm) + d_skip.astype(jnp.float32)[:, None] * xh
    y = y.reshape(b, T, SSD_D) * jax.nn.silu(z)
    y = y.reshape(b, T, SSD_GROUPS, SSD_D // SSD_GROUPS)
    y = y * lax.rsqrt(jnp.mean(y * y, axis=-1, keepdims=True) + NORM_EPS)
    return y.reshape(b, T, SSD_D) * norm_g.astype(jnp.float32)

def _rwkv7_scan(r, w, k, v, za, zb):
    b, T, h, n = r.shape

    def step(S, inp):
        r_t, w_t, k_t, v_t, a_t, b_t = inp
        sa = jnp.einsum("bhij,bhj->bhi", S, a_t)
        S = S * w_t[:, :, None, :] + sa[..., None] * b_t[:, :, None, :] + v_t[..., None] * k_t[:, :, None, :]
        return S, jnp.einsum("bhij,bhj->bhi", S, r_t)

    xs = tuple(jnp.moveaxis(t, 1, 0) for t in (r, w, k, v, za, zb))
    S0 = jnp.zeros((b, h, n, n), dtype=r.dtype)
    _, ys = lax.scan(step, S0, xs)
    return jnp.moveaxis(ys, 0, 1)

def _rwkv7_mixer(p, mu, w0, w2, a0, a2, g2, k_k, k_a, r_k, ln_w, ln_b):
    b, T, _ = p.shape
    f32 = lambda t: t.astype(jnp.float32)
    p = p + (_token_shift(p) - p) * f32(mu)
    i1 = RWKV_D
    i2 = i1 + DECAY_LORA
    i3 = i2 + RWKV_D
    i4 = i3 + RWKV_D
    i5 = i4 + AAA_LORA
    r, w_lo, k, v, a_lo, g_lo = jnp.split(p, [i1, i2, i3, i4, i5], axis=-1)
    w_log = -jax.nn.softplus(-(f32(w0) + jnp.tanh(w_lo) @ f32(w2))) - 0.5
    decay = jnp.exp(-jnp.exp(w_log))
    a = jax.nn.sigmoid(f32(a0) + a_lo @ f32(a2))
    g = jax.nn.sigmoid(g_lo) @ f32(g2)
    heads = lambda t: t.reshape(b, T, RWKV_HEADS, RWKV_HEAD_DIM)
    kk = heads(k * f32(k_k))
    kk = kk / jnp.maximum(jnp.sqrt(jnp.sum(kk * kk, axis=-1, keepdims=True)), 1e-12)
    k = k * (1.0 + (a - 1.0) * f32(k_a))
    rh, kh, vh, ah = heads(r), heads(k), heads(v), heads(a)
    y = _rwkv7_scan(rh, heads(decay), kh, vh, -kk, kk * ah)
    mean = jnp.mean(y, axis=-1, keepdims=True)
    var = jnp.mean(jnp.square(y - mean), axis=-1, keepdims=True)
    y = ((y - mean) * lax.rsqrt(var + RWKV_GN_EPS)).reshape(b, T, RWKV_D) * f32(ln_w) + f32(ln_b)
    bonus = jnp.sum(rh * kh * f32(r_k), axis=-1, keepdims=True) * vh
    return (y + bonus.reshape(b, T, RWKV_D)) * g

def first_inputs(seed: int = 0) -> dict:
    key = jax.random.key(seed)
    ks = jax.random.split(key, 32)
    nrm = lambda k, shape, s: jax.random.normal(k, shape, jnp.float32) * s
    L = DEPTH
    dt = jnp.exp(jax.random.uniform(ks[5], (L, SSD_HEADS), jnp.float32) * (np.log(0.1) - np.log(0.001)) + np.log(0.001))
    dt = jnp.clip(dt, 1e-4)
    return {
        "x": nrm(ks[0], (BATCH, SEQ, D_MODEL), 1.0),
        "pre_mix_norm": 1.0 + nrm(ks[1], (L, D_MODEL), 0.05),
        "w_in": nrm(ks[2], (L, D_MODEL, D_IN), D_MODEL ** -0.5),
        "ssd_conv_w": nrm(ks[3], (L, SSD_CONV, SSD_CONV_DIM), SSD_CONV ** -0.5),
        "ssd_conv_b": nrm(ks[4], (L, SSD_CONV_DIM), 0.02),
        "ssd_dt_bias": dt + jnp.log(-jnp.expm1(-dt)),
        "ssd_a_log": jnp.log(jax.random.uniform(ks[6], (L, SSD_HEADS), jnp.float32, 1.0, 16.0)),
        "ssd_d": 1.0 + nrm(ks[7], (L, SSD_HEADS), 0.1),
        "ssd_norm": 1.0 + nrm(ks[8], (L, SSD_D), 0.05),
        "rwkv_mu": jax.random.uniform(ks[9], (L, RWKV_COLS), jnp.float32),
        "rwkv_w0": jax.random.uniform(ks[10], (L, RWKV_D), jnp.float32, -6.0, 1.0),
        "rwkv_w2": nrm(ks[11], (L, DECAY_LORA, RWKV_D), 0.1 * DECAY_LORA ** -0.5),
        "rwkv_a0": nrm(ks[12], (L, RWKV_D), 0.1),
        "rwkv_a2": nrm(ks[13], (L, AAA_LORA, RWKV_D), 0.5 * AAA_LORA ** -0.5),
        "rwkv_g2": nrm(ks[14], (L, GATE_LORA, RWKV_D), GATE_LORA ** -0.5),
        "rwkv_k_k": 0.85 + nrm(ks[15], (L, RWKV_D), 0.05),
        "rwkv_k_a": 1.0 + nrm(ks[16], (L, RWKV_D), 0.05),
        "rwkv_r_k": nrm(ks[17], (L, RWKV_HEADS, RWKV_HEAD_DIM), 0.1),
        "rwkv_ln_w": 1.0 + nrm(ks[18], (L, RWKV_D), 0.05),
        "rwkv_ln_b": nrm(ks[19], (L, RWKV_D), 0.02),
        "w_out": nrm(ks[20], (L, D_MIX, D_MODEL), D_MIX ** -0.5),
        "post_mix_norm": 1.0 + nrm(ks[21], (L, D_MODEL), 0.05),
        "pre_ffn_norm": 1.0 + nrm(ks[22], (L, D_MODEL), 0.05),
        "ffn_w_up": nrm(ks[23], (L, D_MODEL, 2 * D_FF), D_MODEL ** -0.5),
        "ffn_conv_w": nrm(ks[24], (L, FFN_CONV, 2 * D_FF), FFN_CONV ** -0.5),
        "ffn_conv_b": nrm(ks[25], (L, 2 * D_FF), 0.02),
        "ffn_w_down": nrm(ks[26], (L, D_FF, D_MODEL), D_FF ** -0.5),
        "post_ffn_norm": 1.0 + nrm(ks[27], (L, D_MODEL), 0.05),
    }

def first_block(x, pre_mix_norm, w_in, ssd_conv_w, ssd_conv_b, ssd_dt_bias, ssd_a_log, ssd_d, ssd_norm,
              rwkv_mu, rwkv_w0, rwkv_w2, rwkv_a0, rwkv_a2, rwkv_g2, rwkv_k_k, rwkv_k_a, rwkv_r_k,
              rwkv_ln_w, rwkv_ln_b, w_out, post_mix_norm, pre_ffn_norm, ffn_w_up, ffn_conv_w,
              ffn_conv_b, ffn_w_down, post_ffn_norm):
    h = x
    for l in range(DEPTH):
        xn = _rms_norm(h, pre_mix_norm[l])
        proj = (xn @ w_in[l]).astype(jnp.float32)
        p_ssd, p_rwkv = jnp.split(proj, [SSD_COLS], axis=-1)
        y_ssd = _ssd_mixer(p_ssd, ssd_conv_w[l], ssd_conv_b[l], ssd_dt_bias[l], ssd_a_log[l],
                           ssd_d[l], ssd_norm[l])
        y_rwkv = _rwkv7_mixer(p_rwkv, rwkv_mu[l], rwkv_w0[l], rwkv_w2[l], rwkv_a0[l], rwkv_a2[l],
                              rwkv_g2[l], rwkv_k_k[l], rwkv_k_a[l], rwkv_r_k[l], rwkv_ln_w[l], rwkv_ln_b[l])
        mix = jnp.concatenate([y_ssd, y_rwkv], axis=-1).astype(h.dtype) @ w_out[l]
        h = h + _rms_norm(mix, post_mix_norm[l])
        hn = _rms_norm(h, pre_ffn_norm[l])
        u = _causal_dwconv(hn @ ffn_w_up[l], ffn_conv_w[l], ffn_conv_b[l])
        gate, val = jnp.split(u, 2, axis=-1)
        f = (jax.nn.silu(gate) * val) @ ffn_w_down[l]
        h = h + _rms_norm(f, post_ffn_norm[l])
    return h


MEM_LEN = 256
MIX_WIDTH = D_MODEL
HGRN_HEADS = 4
HGRN_WIDTH = MIX_WIDTH // 2
HGRN_HEAD_DIM = HGRN_WIDTH // HGRN_HEADS
HGRN_CHUNK = 32
MOBA_HEADS = 4
MOBA_WIDTH = MIX_WIDTH - HGRN_WIDTH
MOBA_HEAD_DIM = MOBA_WIDTH // MOBA_HEADS
MOBA_BLOCK = 256
MOBA_TOP_K = 3
MOBA_QUERY_CHUNK = 64
ROPE_THETA = 500000.0
ROT_DIM = MOBA_HEAD_DIM // 4
XATTN_HEADS = 4
XATTN_HEAD_DIM = D_MODEL // XATTN_HEADS
D_FF_2 = 4 * D_MODEL
IN_SPLITS = (HGRN_WIDTH, 2 * HGRN_WIDTH, 3 * HGRN_WIDTH, 4 * HGRN_WIDTH,
             4 * HGRN_WIDTH + MOBA_WIDTH, 4 * HGRN_WIDTH + 2 * MOBA_WIDTH)
IN_COLS = 4 * HGRN_WIDTH + 3 * MOBA_WIDTH


def rms_norm(x, g):
    xf = x.astype(jnp.float32)
    y = xf * lax.rsqrt(jnp.mean(xf * xf, axis=-1, keepdims=True) + NORM_EPS)
    return (y * g.astype(jnp.float32)).astype(x.dtype)

def split_heads(t, n_heads):
    B, S, W = t.shape
    return t.reshape(B, S, n_heads, W // n_heads).transpose(0, 2, 1, 3)

def merge_heads(t):
    B, H, S, hd = t.shape
    return t.transpose(0, 2, 1, 3).reshape(B, S, H * hd)

def partial_rotary(t, positions):
    half = ROT_DIM // 2
    inv_freq = ROPE_THETA ** (-jnp.arange(half, dtype=jnp.float32) * 2.0 / ROT_DIM)
    ang = positions.astype(jnp.float32)[:, None] * inv_freq[None, :]
    cos, sin = jnp.cos(ang), jnp.sin(ang)
    tf = t.astype(jnp.float32)
    x1, x2 = tf[..., :half], tf[..., half:ROT_DIM]
    out = jnp.concatenate([x1 * cos - x2 * sin, x2 * cos + x1 * sin, tf[..., ROT_DIM:]], axis=-1)
    return out.astype(t.dtype)

def hgrn2_mixer(q, f_logit, inp, gate, lb, norm_g):
    B, S, _ = q.shape
    H, dh, C = HGRN_HEADS, HGRN_HEAD_DIM, HGRN_CHUNK
    n = S // C
    f = lb.astype(jnp.float32) + (1.0 - lb.astype(jnp.float32)) * jax.nn.sigmoid(f_logit.astype(jnp.float32))
    log_f = jnp.log(f)
    k = 1.0 - f

    def chunks(t):
        return split_heads(t.astype(jnp.float32), H).reshape(B, H, n, C, dh)

    qc, kc, vc, gc = chunks(q), chunks(k), chunks(inp), chunks(log_f)
    b = jnp.cumsum(gc, axis=3)
    b_last = b[..., -1:, :]
    q_t = qc * jnp.exp(b)
    k_t = kc * jnp.exp(-b)
    k_end = kc * jnp.exp(b_last - b)
    causal = jnp.tril(jnp.ones((C, C), dtype=bool))
    A = jnp.where(causal, jnp.einsum('bhncd,bhnsd->bhncs', q_t, k_t), 0.0)
    o_intra = jnp.einsum('bhncs,bhnsv->bhncv', A, vc)
    decay = jnp.exp(b_last[..., 0, :])

    def step(state, xs):
        q_n, k_n, v_n, dec_n = xs
        o_n = jnp.einsum('bhcd,bhdv->bhcv', q_n, state)
        new_state = dec_n[..., None] * state + jnp.einsum('bhsd,bhsv->bhdv', k_n, v_n)
        return new_state, o_n

    xs = (jnp.moveaxis(q_t, 2, 0), jnp.moveaxis(k_end, 2, 0),
          jnp.moveaxis(vc, 2, 0), jnp.moveaxis(decay, 2, 0))
    _, o_inter = lax.scan(step, jnp.zeros((B, H, dh, dh), jnp.float32), xs)
    o = (o_intra + jnp.moveaxis(o_inter, 0, 2)).reshape(B, H, S, dh)
    o = o * lax.rsqrt(jnp.mean(o * o, axis=-1, keepdims=True) + NORM_EPS)
    o = merge_heads(o) * norm_g.astype(jnp.float32) * jax.nn.silu(gate.astype(jnp.float32))
    return o.astype(q.dtype)

def moba_attention(q, k, v):
    B, H, S, hd = q.shape
    QC, BLK = MOBA_QUERY_CHUNK, MOBA_BLOCK
    n_blocks = -(-S // BLK)
    pad = n_blocks * BLK - S
    kb = jnp.pad(k, ((0, 0), (0, 0), (0, pad), (0, 0))).reshape(B, H, n_blocks, BLK, hd)
    vb = jnp.pad(v, ((0, 0), (0, 0), (0, pad), (0, 0))).reshape(B, H, n_blocks, BLK, hd)
    k_mean = jnp.mean(kb.astype(jnp.float32), axis=3)
    n_sel = min(MOBA_TOP_K, n_blocks)
    n_chunks = S // QC
    scale = hd ** -0.5
    b_idx = jnp.arange(B)[:, None, None, None]
    h_idx = jnp.arange(H)[None, :, None, None]
    block_ids = jnp.arange(n_blocks)
    slot_ids = jnp.arange(n_sel)
    q_chunks = jnp.moveaxis(q.reshape(B, H, n_chunks, QC, hd), 2, 0)

    def attend_chunk(args):
        qc, c = args
        start = c * QC
        blk = start // BLK
        q_pos = start + jnp.arange(QC)
        gate = jnp.einsum('bhqd,bhnd->bhqn', qc.astype(jnp.float32), k_mean)
        gate = jnp.where(block_ids < blk, gate, -jnp.inf)
        _, sel = lax.top_k(gate, n_sel)
        k_sel = kb[b_idx, h_idx, sel]
        v_sel = vb[b_idx, h_idx, sel]
        k_own = lax.dynamic_index_in_dim(kb, blk, axis=2, keepdims=False)
        v_own = lax.dynamic_index_in_dim(vb, blk, axis=2, keepdims=False)
        s_sel = jnp.einsum('bhqd,bhqnkd->bhqnk', qc, k_sel,
                           preferred_element_type=jnp.float32) * scale
        s_sel = jnp.where((slot_ids < blk)[:, None], s_sel, -jnp.inf)
        s_own = jnp.einsum('bhqd,bhkd->bhqk', qc, k_own,
                           preferred_element_type=jnp.float32) * scale
        k_pos = blk * BLK + jnp.arange(BLK)
        s_own = jnp.where(k_pos[None, :] <= q_pos[:, None], s_own, -jnp.inf)
        scores = jnp.concatenate([s_sel.reshape(B, H, QC, n_sel * BLK), s_own], axis=-1)
        p = jax.nn.softmax(scores, axis=-1).astype(v.dtype)
        p_sel = p[..., :n_sel * BLK].reshape(B, H, QC, n_sel, BLK)
        p_own = p[..., n_sel * BLK:]
        return (jnp.einsum('bhqnk,bhqnkd->bhqd', p_sel, v_sel)
                + jnp.einsum('bhqk,bhkd->bhqd', p_own, v_own))

    out = lax.map(attend_chunk, (q_chunks, jnp.arange(n_chunks)))
    return jnp.moveaxis(out, 0, 2).reshape(B, H, S, hd)

def cross_attention(h, mem_n, w_q, w_k, w_v, w_o):
    B, S, _ = h.shape
    q = split_heads(h @ w_q, XATTN_HEADS)
    k = split_heads(mem_n @ w_k, XATTN_HEADS)
    v = split_heads(mem_n @ w_v, XATTN_HEADS)
    s = jnp.einsum('bhsd,bhmd->bhsm', q, k, preferred_element_type=jnp.float32) * XATTN_HEAD_DIM ** -0.5
    p = jax.nn.softmax(s, axis=-1).astype(v.dtype)
    o = jnp.einsum('bhsm,bhmd->bhsd', p, v)
    return merge_heads(o) @ w_o

def second_inputs(seed: int = 0) -> dict:
    key = jax.random.key(seed)
    ks = jax.random.split(key, 20)

    def normal(k, shape, scale):
        return jax.random.normal(k, shape, jnp.float32) * scale

    def gain(k, shape):
        return 1.0 + 0.05 * jax.random.normal(k, shape, jnp.float32)

    return {
        "x": normal(ks[0], (BATCH, SEQ, D_MODEL), 1.0),
        "mem": normal(ks[1], (BATCH, MEM_LEN, D_MODEL), 1.0),
        "norm_mix": gain(ks[2], (DEPTH, D_MODEL)),
        "w_in": normal(ks[3], (DEPTH, D_MODEL, IN_COLS), D_MODEL ** -0.5),
        "lb_logits": gain(ks[4], (DEPTH + 1, HGRN_WIDTH)),
        "hgrn_norm": gain(ks[5], (DEPTH, HGRN_WIDTH)),
        "w_out": normal(ks[6], (DEPTH, MIX_WIDTH, D_MODEL), MIX_WIDTH ** -0.5),
        "norm_xattn": gain(ks[7], (DEPTH, D_MODEL)),
        "norm_mem": gain(ks[8], (DEPTH, D_MODEL)),
        "w_xq": normal(ks[9], (DEPTH, D_MODEL, D_MODEL), D_MODEL ** -0.5),
        "w_xk": normal(ks[10], (DEPTH, D_MODEL, D_MODEL), D_MODEL ** -0.5),
        "w_xv": normal(ks[11], (DEPTH, D_MODEL, D_MODEL), D_MODEL ** -0.5),
        "w_xo": normal(ks[12], (DEPTH, D_MODEL, D_MODEL), D_MODEL ** -0.5),
        "norm_mlp": gain(ks[13], (DEPTH, D_MODEL)),
        "w_ff1": normal(ks[14], (DEPTH, D_MODEL, D_FF_2), D_MODEL ** -0.5),
        "w_ff2": normal(ks[15], (DEPTH, D_FF_2, D_MODEL), D_FF_2 ** -0.5),
        "norm_final": gain(ks[16], (D_MODEL,)),
    }

def second_block(x, mem, norm_mix, w_in, lb_logits, hgrn_norm, w_out, norm_xattn, norm_mem,
              w_xq, w_xk, w_xv, w_xo, norm_mlp, w_ff1, w_ff2, norm_final):
    S = x.shape[1]
    positions = jnp.arange(S, dtype=jnp.int32)
    lb_table = jnp.cumsum(jax.nn.softmax(lb_logits.astype(jnp.float32), axis=0), axis=0)
    for l in range(DEPTH):
        h = rms_norm(x, norm_mix[l])
        proj = h @ w_in[l]
        hq, hf, hi, hg, mq, mk, mv = jnp.split(proj, IN_SPLITS, axis=-1)
        o_hgrn = hgrn2_mixer(hq, hf, hi, hg, lb_table[l], hgrn_norm[l])
        mq = partial_rotary(split_heads(mq, MOBA_HEADS), positions)
        mk = partial_rotary(split_heads(mk, MOBA_HEADS), positions)
        mv = split_heads(mv, MOBA_HEADS)
        o_moba = merge_heads(moba_attention(mq, mk, mv))
        mixed = jnp.concatenate([o_hgrn, o_moba.astype(o_hgrn.dtype)], axis=-1)
        x = x + mixed @ w_out[l]
        h = rms_norm(x, norm_xattn[l])
        mem_n = rms_norm(mem, norm_mem[l])
        x = x + cross_attention(h, mem_n, w_xq[l], w_xk[l], w_xv[l], w_xo[l])
        h = rms_norm(x, norm_mlp[l])
        x = x + jnp.square(jax.nn.relu(h @ w_ff1[l])) @ w_ff2[l]
    return rms_norm(x, norm_final)


def setup_inputs(seed=0):
    out = dict(first_inputs(seed))
    for name, value in second_inputs(seed + 1).items():
        if name != "x":
            out[name + "_2"] = value
    return out


def reference(
    x, pre_mix_norm, w_in, ssd_conv_w, ssd_conv_b, ssd_dt_bias, ssd_a_log, ssd_d, ssd_norm,
    rwkv_mu, rwkv_w0, rwkv_w2, rwkv_a0, rwkv_a2, rwkv_g2, rwkv_k_k, rwkv_k_a, rwkv_r_k,
    rwkv_ln_w, rwkv_ln_b, w_out, post_mix_norm, pre_ffn_norm, ffn_w_up, ffn_conv_w, ffn_conv_b,
    ffn_w_down, post_ffn_norm, mem_2, norm_mix_2, w_in_2, lb_logits_2, hgrn_norm_2, w_out_2,
    norm_xattn_2, norm_mem_2, w_xq_2, w_xk_2, w_xv_2, w_xo_2, norm_mlp_2, w_ff1_2, w_ff2_2,
    norm_final_2,
):
    x = first_block(
        x, pre_mix_norm, w_in, ssd_conv_w, ssd_conv_b, ssd_dt_bias, ssd_a_log, ssd_d, ssd_norm,
        rwkv_mu, rwkv_w0, rwkv_w2, rwkv_a0, rwkv_a2, rwkv_g2, rwkv_k_k, rwkv_k_a, rwkv_r_k,
        rwkv_ln_w, rwkv_ln_b, w_out, post_mix_norm, pre_ffn_norm, ffn_w_up, ffn_conv_w,
        ffn_conv_b, ffn_w_down, post_ffn_norm,
    )
    return second_block(
        x, mem_2, norm_mix_2, w_in_2, lb_logits_2, hgrn_norm_2, w_out_2, norm_xattn_2,
        norm_mem_2, w_xq_2, w_xk_2, w_xv_2, w_xo_2, norm_mlp_2, w_ff1_2, w_ff2_2, norm_final_2,
    )


_drawn_inputs = setup_inputs


def setup_inputs(seed=0):
    import zlib

    import numpy as np

    out = dict(_drawn_inputs(seed))
    spreads = {}
    factors = {'rwkv_w2': 8.0,
     'rwkv_a0': 3.108,
     'rwkv_k_k': 3.71,
     'rwkv_ln_w': 2.854,
     'rwkv_ln_b': 6.49,
     'ffn_conv_b': 2.851,
     'lb_logits_2': 5.416,
     'hgrn_norm_2': 4.639,
     'norm_xattn_2': 8.0,
     'norm_mem_2': 8.0,
     'norm_mlp_2': 6.536}
    for name, (base, spread) in spreads.items():
        noise = np.random.default_rng([zlib.crc32(name.encode()), seed]).standard_normal(out[name].shape)
        drawn = base * np.exp(spread * noise) if base else spread * noise
        out[name] = __import__('jax').numpy.asarray(drawn.astype(out[name].dtype))
    for name, factor in factors.items():
        out[name] = (out[name] * factor).astype(out[name].dtype)
    return out
```

```python
from contextlib import ExitStack

import numpy as np

import concourse.bass as bass
from concourse import mybir

ALU = mybir.AluOpType
ACT = mybir.ActivationFunctionType
AX = mybir.AxisListType
F32 = mybir.dt.float32

P = 128
T = 256
D = 1024
KT = D // P
C = 128
NC_ = T // C
EPS = 1e-6

SSD_D, SSD_HEADS, SSD_GROUPS, SSD_STATE, SSD_CONV = 512, 8, 2, 128, 4
SSD_CONV_DIM = SSD_D + 2 * SSD_GROUPS * SSD_STATE
SSD_COLS = SSD_D + SSD_CONV_DIM + SSD_HEADS
RW_D, RW_HEADS, RW_HD = 512, 8, 64
GN_EPS = 64e-5
DECAY_SCALE = float(np.exp(-0.5))
D_FF = 2816
FFT = D_FF // P
HG_D, HG_HEADS, HG_CHUNK = 512, 4, 32
MB_HEADS, MB_HD, ROT, ROPE_THETA = 4, 128, 32, 500000.0
XA_HEADS, XA_HD = 4, 256
D_FF2 = 4096
FF2T = D_FF2 // P

RING = 4
SLOT = 4096


PARAM_TILES = [
    ("pre_mix_norm", KT), ("post_mix_norm", KT), ("pre_ffn_norm", KT), ("post_ffn_norm", KT),
    ("norm_mix_2", KT), ("norm_xattn_2", KT), ("norm_mem_2", KT), ("norm_mlp_2", KT),
    ("norm_final_2", KT),
    ("ssd_conv_w", 4 * 8), ("ssd_conv_b", 8), ("ssd_norm", 4), ("ssd_d", 4),
    ("ssd_dt_bias", 1), ("ssd_a_log", 1),
    ("rwkv_mu", 14), ("rwkv_w0", 4), ("rwkv_a0", 4), ("rwkv_k_k", 4), ("rwkv_k_a", 4),
    ("rwkv_r_k", 4), ("rwkv_ln_w", 4), ("rwkv_ln_b", 4),
    ("ffn_conv_w", 3 * 2 * FFT), ("ffn_conv_b", 2 * FFT),
    ("lb_logits_2", 8), ("hgrn_norm_2", 4),
]
PARAM_AT = {}
_n = 0
for _name, _tiles in PARAM_TILES:
    PARAM_AT[_name] = _n
    _n += _tiles
PARAM_COLS = _n

LEVELS = (2, 4, 8, 16, 32)
CONST_WIDTHS = [
    ("ident", P), ("ones", P), ("head_ones", P),
    ("incl", P), ("strict", P), ("neg_incl", P), ("neg_strict", P),
    ("pair", P), ("pair_t", P),
    ("levels", 64 * len(LEVELS)),
    ("chunk32", P), ("causal", T), ("swap", P), ("cos", T), ("sin", T),
    ("reset128", T), ("reset32", T),
]
CONST_AT = {}
_n = 0
for _name, _w in CONST_WIDTHS:
    CONST_AT[_name] = (_n, _w)
    _n += _w
CONST_COLS = _n


def constant_table():
    out = np.zeros((P, CONST_COLS), np.float32)

    def put(name, value):
        at, w = CONST_AT[name]
        out[:value.shape[0], at:at + w] = value

    r, c = np.arange(P)[:, None], np.arange(P)[None, :]
    put("ident", np.eye(P))
    put("ones", np.ones((P, P)))
    put("head_ones", (r // RW_HD == c // RW_HD) * 1.0)
    put("incl", (r <= c) * 1.0)
    put("strict", (r < c) * 1.0)
    put("neg_incl", (r <= c) * -1.0)
    put("neg_strict", (r < c) * -1.0)
    put("pair", ((r == c + 1) & (r % 2 == 1)) * -1.0)
    put("pair_t", ((c == r + 1) & (c % 2 == 1)) * 1.0)
    levels = []
    for m in LEVELS:
        mask = ((r // (2 * m) == c // (2 * m)) & (r % (2 * m) >= m) & (c % (2 * m) < m)) * 1.0
        levels.append(mask.reshape(P, P // (2 * m), 2, m)[:, :, 0, :].reshape(P, 64))
    put("levels", np.concatenate(levels, axis=1))
    put("chunk32", ((r <= c) & (r // HG_CHUNK == c // HG_CHUNK)) * 1.0)
    q, k = np.arange(P)[:, None], np.arange(T)[None, :]
    put("causal", np.where(k - P <= q, 0.0, -3e38))
    half = ROT // 2
    swap = np.zeros((P, P))
    for i in range(half):
        swap[i + half, i] = 1.0
        swap[i, i + half] = 1.0
    put("swap", swap)
    inv = np.float32(ROPE_THETA) ** (-np.arange(half, dtype=np.float32) * np.float32(2.0) / np.float32(ROT))
    ang = np.arange(T, dtype=np.float32)[:, None] * inv[None, :].astype(np.float32)
    cos, sin = np.cos(ang).T, np.sin(ang).T
    put("cos", np.concatenate([cos, cos]))
    put("sin", np.concatenate([-sin, sin]))
    t = np.arange(T)[None, :].repeat(P, 0)
    put("reset128", (t % C != 0) * 1.0)
    put("reset32", (t % HG_CHUNK != 0) * 1.0)
    return out


def parameter_table(inputs):
    def tiles(a):
        return np.asarray(a).reshape(-1, P).T

    def column(a):
        out = np.zeros((P, 1), np.float32)
        out[:a.shape[0], 0] = a
        return out

    a = {k: np.asarray(v) for k, v in inputs.items()}
    mu = a["rwkv_mu"][0]
    cols = {name: None for name, _ in PARAM_TILES}
    for name in cols:
        if name == "rwkv_mu":
            k0 = RW_D + 64
            al = 3 * RW_D + 64
            order = [mu[k0:k0 + RW_D], mu[RW_D:k0], mu[al:al + 64], mu[al + 64:], mu[:RW_D],
                     mu[k0 + RW_D:k0 + 2 * RW_D]]
            cols[name] = tiles(np.concatenate(order))
        elif name == "ssd_conv_w":
            cols[name] = np.concatenate([tiles(a[name][0, i]) for i in range(4)], axis=1)
        elif name == "ffn_conv_w":
            cols[name] = np.concatenate([tiles(a[name][0, i]) for i in range(3)], axis=1)
        elif name == "lb_logits_2":
            cols[name] = np.concatenate([tiles(a[name][i]) for i in range(2)], axis=1)
        elif name == "ssd_d":
            cols[name] = tiles(np.repeat(a[name][0], SSD_D // SSD_HEADS))
        elif name in ("ssd_dt_bias", "ssd_a_log"):
            cols[name] = column(a[name][0])
        else:
            cols[name] = tiles(a[name].reshape(-1))
        assert cols[name].shape[1] == dict(PARAM_TILES)[name], name
    return np.ascontiguousarray(np.concatenate(list(cols.values()), axis=1))


def weight_stream():
    out = []
    out += [("w_in", "k", 0), ("w_in", "lora", 0), ("w_in", "r", 0), ("w_in", "v", 0),
            ("w_in", "xs", 0), ("w_in", "bc", 0), ("w_in", "z", 0)]
    out += [("w_xk_2", "cols", i) for i in range(2)] + [("w_xv_2", "cols", i) for i in range(2)]
    out += [("w_out", "rows", i) for i in range(2)]
    out += [("ffn_w_up", "pair", i) for i in range(FFT // 2)]
    out += [("ffn_w_down", "rows", i) for i in range((FFT + 3) // 4)]
    out += [("w_in_2", "cols", i) for i in (1, 0, 2, 3, 4, 5, 6)]
    out += [("w_out_2", "rows", i) for i in range(2)]
    out += [("w_xq_2", "cols", i) for i in range(2)]
    out += [("w_xo_2", "rows", i) for i in range(2)]
    out += [("w_ff1_2", "cols", i) for i in range(D_FF2 // 512)]
    out += [("w_ff2_2", "rows", i) for i in range(FF2T // 4)]
    return out


STREAM = weight_stream()
CHUNK_NO = {c: n for n, c in enumerate(STREAM)}
W_IN_COLS = {"z": 0, "xs": SSD_D, "bc": 2 * SSD_D, "dt": SSD_D + SSD_CONV_DIM,
             "r": SSD_COLS, "w_lo": SSD_COLS + RW_D, "k": SSD_COLS + RW_D + 64,
             "v": SSD_COLS + 2 * RW_D + 64, "a_lo": SSD_COLS + 3 * RW_D + 64}


def chunk_pieces(w, chunk):
    name, kind, i = chunk
    if kind == "rows":
        rows = w[name].rearrange("(k p) n -> p k n", p=P)
        k = rows.shape[1]
        return [(j, rows[:, 4 * i + j:4 * i + j + 2, :]) for j in (0, 2) if 4 * i + j < k]
    cols = w[name].rearrange("(k p) n -> p k n", p=P)
    if kind == "cols":
        return [(0, cols[:, :, 512 * i:512 * i + 512])]
    if kind == "pair":
        return [(0, cols[:, :, 256 * i:256 * i + 256]),
                (256, cols[:, :, D_FF + 256 * i:D_FF + 256 * i + 256])]
    if kind == "lora":
        at = W_IN_COLS
        return [(0, cols[:, :, at["w_lo"]:at["w_lo"] + 64]),
                (64, cols[:, :, at["a_lo"]:at["a_lo"] + 192]),
                (256, cols[:, :, at["dt"]:at["dt"] + SSD_HEADS])]
    return [(0, cols[:, :, W_IN_COLS[kind]:W_IN_COLS[kind] + 512])]


class Ledger:

    def __init__(self, known, sem):
        self.known, self.sem, self.count, self.steps = known, sem, {}, {}

    def mark(self, name, *step, by=1):
        self.count[name] = self.count.get(name, 0) + by
        if step:
            assert step not in self.steps, step
            self.steps[step] = (name, self.count[name])
        return self.sem(name), by

    def same(self, step, as_step):
        self.steps[step] = self.steps[as_step]

    def at(self, *step):
        if self.known is None:
            return self.sem("first_pass"), 1
        name, value = self.known[step]
        assert value > 0
        return self.sem(name), value

    def so_far(self, name):
        return self.sem(name), self.count[name]


def build(nc, w, out, known, dump=None):
    with ExitStack() as ctx:
        sems = {}

        def sem(name):
            if name not in sems:
                sems[name] = ctx.enter_context(nc.semaphore(name))
            return sems[name]

        steps = Ledger(known, sem)
        mark, at, same, so_far = steps.mark, steps.at, steps.same, steps.so_far

        def sb(name, *dims):
            return ctx.enter_context(nc.sbuf_tensor(name, [P, *dims], F32))

        banks = [ctx.enter_context(nc.psum_tensor(f"bank{i}", [P, 512], F32)) for i in range(8)]

        def halves(b):
            return banks[b][:, :].rearrange("p (i t) -> p i t", i=2)

        def quarters(b):
            return banks[b][:, :].rearrange("p (i t) -> p i t", i=4)

        consts = sb("consts", CONST_COLS)
        params = sb("params", PARAM_COLS)
        ring = sb("ring", RING, SLOT)
        h = sb("h", KT, T)
        hg = sb("hg", KT, T)
        mix = sb("mix", KT, T)
        xk = sb("xk", KT, T)
        xv = sb("xv", NC_, D)
        sqs = sb("sqs", 2, 512)
        ssum = sb("ssum", 512)
        rms = sb("rms", T)
        rstd = sb("rstd", T)
        rcol = sb("rcol", NC_)
        eps = sb("eps", 4)
        ARENA = 20480
        arena = sb("arena", ARENA)

        def const(name):
            a, n = CONST_AT[name]
            return consts[:, a:a + n]

        def par(name, i):
            a = PARAM_AT[name] + i
            return params[:, a:a + 1]

        def view(a, *dims):
            n = int(np.prod(dims))
            assert a + n <= ARENA, (a, dims)
            v = arena[:, a:a + n]
            if len(dims) == 2:
                v = v.rearrange("p (a b) -> p a b", a=dims[0])
            elif len(dims) == 3:
                v = v.rearrange("p (a b c) -> p a b c", a=dims[0], b=dims[1])
            return v

        ident, ones, head_ones = const("ident"), const("ones"), const("head_ones")

        def over(ap, n):
            return ap.unsqueeze(1).broadcast_to([ap.shape[0], n, ap.shape[1]])

        def along(ap, n):
            return ap.unsqueeze(2).broadcast_to([ap.shape[0], ap.shape[1], n])

        raw = view(0, 14, T + 1)
        shf = view(3600, 14, T)
        K_, R_, V_ = shf[:, 0:4, :], shf[:, 6:10, :], shf[:, 10:14, :]
        WA, GLO = shf[:, 4, :], shf[:, 5, :]
        SW, CS, E0 = view(0, 4, T), view(1024, 4, T), view(2048, 4, T)
        A_, KK, E1, E2, BT = (view(7184 + 1024 * i, 4, T) for i in range(5))
        KSQ = xk[:, 0:4, :]
        VTOK = view(0, NC_, RW_D)
        KTOK, BTOK = view(1024, RW_D), view(1536, RW_D)
        P64 = [view(3072 + 256 * i, 4, 64) for i in range(2)]
        SOLVE = 7184 + 5 * 1024
        Y, BONUS = KK, R_
        small = sb("small", 64)
        s0c = view(SOLVE + 7168, 4, 64)
        lora_w = view(SOLVE + 7168 - 400, RW_D)
        gate_w = ssum

        def solve_set(i):
            a = SOLVE + 3584 * i
            q = [view(a + 512 * n, 4, C) for n in range(6)]

            def grown(m):
                both = arena[:, a + 512:a + 512 + 2 * (512 + m)].rearrange("p (w x) -> p w x", w=2)
                return both[:, :, 0:512].rearrange("p w (jb two m) -> p w jb two m", two=2, m=m)[:, :, :, 0, :]

            return dict(LT=q[0], X=q[1], XT=q[2], PA=q[3], PB=q[4], ARB=q[5], XX=view(a + 512, 8, C), grown=grown,
                        G=view(a + 3072, 4, 64), U=view(a + 3328, 4, 64))

        sets = [solve_set(0), solve_set(1)]
        rawx = view(SOLVE, 8, T + 3)
        xbc = view(SOLVE + 2080, 8, T)
        EX = [view(SOLVE + 2080 + 512 * i, 4, C) for i in range(2)]
        MT = [view(SOLVE + 3104 + 512 * i, 4, C) for i in range(2)]
        zs = view(SOLVE + 4128, 4, T)
        BTOKS = view(SOLVE + 5152, 2, SSD_STATE)
        dtT, aT, dtmp = view(SOLVE + 5408, T), view(SOLVE + 5664, T), view(SOLVE + 5920, T)
        dtok = view(SOLVE + 6176, NC_, 8)
        atok = view(SOLVE + 6192, NC_, 8)
        cstok = view(SOLVE + 6208, NC_, 8)
        dect = view(SOLVE + 6224, 8)
        acol = view(SOLVE + 6232, 2)
        GT = A_[:, 0:2, :].rearrange("p a (b t) -> p (a b) t", t=C)
        CEX = mix[:, 4:8, :].rearrange("p a (b t) -> p (a b) t", t=C)
        YS = mix[:, 0:4, :]
        XDT = xv[:, 0, :].rearrange("p (c d) -> p c d", c=NC_)
        XDEC, ST = xv[:, 1, 0:SSD_D], xv[:, 1, SSD_D:2 * SSD_D]

        block = ctx.enter_context(nc.Block())

        def slot(name, kind, i=0):
            n = CHUNK_NO[(name, kind, i)]
            s = ring[:, n % RING, :]
            if kind == "rows":
                return s.rearrange("p (k n) -> p k n", k=4)
            if kind == "lora":
                return s[:, 0:8 * 264].rearrange("p (k n) -> p k n", k=KT)
            return s.rearrange("p (k n) -> p k n", k=KT)

        @block.sync
        def _(sp):
            sp.dma_start(consts[:, 0:3 * P], w["constants"][:, 0:3 * P]).then_inc(
                *mark("identity_landed", "identity landed", by=16))
            sp.dma_start(mix[:, :, :].rearrange("p a b -> p (a b)").rearrange("p (c d) -> p c d", c=2),
                         w["x"][0].rearrange("(c p) d -> p c d", p=P)).then_inc(*mark("x_landed", "x landed", by=16))
            for n, chunk in enumerate(STREAM):
                if n >= RING:
                    sp.wait_ge(*at("chunk used", n - RING))
                name, kind, i = chunk
                view_ = slot(name, kind, i)
                pieces = chunk_pieces(w, chunk)
                for j, (a, src) in enumerate(pieces):
                    dst = view_[:, a:a + src.shape[1], :] if kind == "rows" else view_[:, :, a:a + src.shape[2]]
                    last = j == len(pieces) - 1
                    sp.dma_start(dst, src).then_inc(
                        *mark(f"weights_landed_{n % RING}", *(("chunk", n) if last else ()), by=16))
            sp.wait_ge(*at("out stored"))

        def chunk_ready(pe, name, kind, i=0):
            pe.wait_ge(*at("chunk", CHUNK_NO[(name, kind, i)]))

        def chunk_used(name, kind, i, step):
            same(("chunk used", CHUNK_NO[(name, kind, i)]), step)

        def norm_act(act, n, src, gain, ready):
            for m in range(KT):
                act.wait_ge(*at(*ready(m)))
                if m >= 4:
                    act.wait_ge(*at(n, "summed", m // 2 - 2))
                nc.scalar.activation(sqs[:, m // 2 % 2, 256 * (m % 2):256 * (m % 2) + 256], src[:, m, :],
                                     ACT.Square).then_inc(*mark("norm_squares", n, "squares", m))
                nc.scalar.activation(hg[:, m, :], src[:, m, :], ACT.Copy,
                                     scale=par(gain, m)).then_inc(*mark("norm_gained", n, "gained", m))

        def norm_sum(dve, n):
            for b in range(4):
                dve.wait_ge(*at(n, "squares", 2 * b + 1))
                if b == 0:
                    nc.vector.tensor_copy(ssum[:, :], sqs[:, 0, :]).then_inc(*mark("norm_summed", n, "summed", 0))
                else:
                    dve.wait_ge(*at(n, "summed", b - 1))
                    nc.vector.tensor_tensor(ssum[:, :], ssum[:, :], sqs[:, b % 2, :], ALU.add).then_inc(
                        *mark("norm_summed", n, "summed", b))

        def norm_sum_post(dve, n):
            norm_sum(dve, n)

        def norm_total(pe, n, bank, free):
            if free:
                pe.wait_ge(*at(*free))
            pe.wait_ge(*at(n, "summed", 3))
            for i in range(2):
                mm = nc.tensor.matmul(banks[bank][:, 0:T], ones, ssum[:, 256 * i:256 * i + 256],
                                      start=(i == 0), stop=(i == 1))
            mm.then_inc(*mark("norm_total", n, "total"))

        def norm_root(act, n, bank, scale=1.0 / D):
            act.wait_ge(*at(n, "total"))
            nc.scalar.activation(rms[:, :], banks[bank][:, 0:T], ACT.Sqrt, bias=eps[:, 0:1],
                                 scale=scale).then_inc(*mark("norm_root", n, "root"))

        def norm_reciprocal(dve, n):
            dve.wait_ge(*at(n, "root"))
            nc.vector.reciprocal(rstd[:, :], rms[:, :]).then_inc(*mark("norm_rstd", n, "rstd"))

        def column_rstd(pe, n, bank, free):
            pe.wait_ge(*at(n, "rstd"))
            pe.wait_ge(*at(*free))
            for c in range(NC_):
                mm = nc.tensor.matmul(banks[bank][:, c:c + 1], rstd[:, c * C:(c + 1) * C], ident[:, 0:1],
                                      start=True, stop=True)
            mm.then_inc(*mark("column_rstd", n, "column"))

        def wide(pe, chunk, j, bank, half, mm_=None, src=None):
            s = slot(*chunk)
            for k in range(KT):
                mm = nc.tensor.matmul(halves(bank)[:, half, :], s[:, k, j * P:(j + 1) * P],
                                      (src or hg)[:, k, :], start=(k == 0), stop=(k == KT - 1))
            return mm

        def narrow(pe, name, ktiles, src, src_ready, last_in_turn, label, free):
            nchunks = (ktiles + 3) // 4
            for b in range(4):
                if free:
                    pe.wait_ge(*at(*free(b)))
            for i in range(nchunks):
                chunk_ready(pe, name, "rows", i)
                s = slot(name, "rows", i)
                n = min(4, ktiles - 4 * i)
                tail = i == nchunks - 1
                if not tail:
                    for kk in range(n):
                        k = 4 * i + kk
                        pe.wait_ge(*at(*src_ready(k)))
                        for m in range(KT):
                            mm = nc.tensor.matmul(halves(4 + m // 2)[:, m % 2, :], s[:, kk, m * P:(m + 1) * P],
                                                  src[:, k, :], start=(k == 0 and m % 2 == 0), stop=False,
                                                  skip_group_check=True)
                    mm.then_inc(*mark("rows_used", label, "rows", i))
                    chunk_used(name, "rows", i, (label, "rows", i))
                else:
                    for kk in range(n):
                        pe.wait_ge(*at(*src_ready(4 * i + kk)))
                    for m in range(KT):
                        for kk in range(n):
                            k = 4 * i + kk
                            mm = nc.tensor.matmul(halves(4 + m // 2)[:, m % 2, :], s[:, kk, m * P:(m + 1) * P],
                                                  src[:, k, :], start=(k == 0 and m % 2 == 0),
                                                  stop=(kk == n - 1), skip_group_check=True)
                        if m % 2:
                            mm.then_inc(*mark("projected_out", label, "bank", m // 2))
                    chunk_used(name, "rows", i, (label, "bank", 3))

        scaled_f = view(0, 2, 512)

        def post_norm_act(act, n, label):
            for b in range(4):
                act.wait_ge(*at(label, "bank", b))
                if b >= 2:
                    act.wait_ge(*at(n, "summed", b - 2))
                nc.scalar.activation(sqs[:, b % 2, :], banks[4 + b][:, :], ACT.Square).then_inc(
                    *mark("norm_squares", n, "squares", 2 * b + 1))

        def post_norm_apply(dve, n, label, gain):
            dve.wait_ge(*at(n, "rstd"))
            for m in range(KT):
                nc.vector.scalar_tensor_tensor(scaled_f[:, m // 2 % 2, 256 * (m % 2):256 * (m % 2) + 256],
                                               halves(4 + m // 2)[:, m % 2, :], par(gain, m), rstd[:, :],
                                               ALU.mult, ALU.mult).then_inc(*mark("post_scaled", n, "scaled", m))
                if m % 2:
                    dve.wait_ge(*at(n, "scaled", m))
                    for mm in (m - 1, m):
                        nc.vector.tensor_tensor(h[:, mm, :], h[:, mm, :],
                                                scaled_f[:, m // 2 % 2, 256 * (mm % 2):256 * (mm % 2) + 256],
                                                ALU.add).then_inc(*mark("residual", n, "added", mm))
            for b in range(4):
                same((label, "free", b), (n, "added", 7))

        PROJ = [("k", 4), ("lora", 2), ("r", 4), ("v", 4), ("xs", 4), ("bc", 4), ("z", 4)]
        TILE_OF = [(kind, j) for kind, n in PROJ for j in range(n)]
        PBANKS = len(TILE_OF) // 2

        def pe_load(pe):
            pe.wait_ge(*at("x landed"))
            pe.wait_ge(*at("identity landed"))
            xt = mix[:, :, :].rearrange("p a b -> p (a b)").rearrange("p (c d) -> p c d", c=2)
            for b in range(4):
                for m in (2 * b, 2 * b + 1):
                    for c in range(NC_):
                        mm = nc.tensor.transpose(halves(4 + b)[:, m % 2, c * C:(c + 1) * C],
                                                 xt[:, c, m * P:(m + 1) * P], ident)
                mm.then_inc(*mark("x_turned", "x turned", b))

        def dve_load(dve):
            for b in range(4):
                dve.wait_ge(*at("x turned", b))
                nc.vector.tensor_copy(h[:, 2 * b:2 * b + 2, :], halves(4 + b)).then_inc(*mark("h_written", "h", b))

        def pe_project1(pe):
            for i, (kind, j) in enumerate(TILE_OF):
                b = i // 2
                if j == 0:
                    chunk_ready(pe, "w_in", kind)
                if i % 2 == 0 and b >= 4:
                    pe.wait_ge(*at("proj1 out", b - 4))
                for k in range(KT):
                    if i == 0:
                        pe.wait_ge(*at("pre_mix", "gained", k))
                    mm = nc.tensor.matmul(halves(b % 4)[:, i % 2, :], slot("w_in", kind)[:, k, j * P:(j + 1) * P],
                                          hg[:, k, :], start=(k == 0), stop=(k == KT - 1))
                if i % 2:
                    mm.then_inc(*mark("proj1", "proj1", b))
                if i == 0:
                    norm_total(pe, "pre_mix", 4, ("h", 3))
                if i == 15:
                    pe_lora(pe)
                if i == 19:
                    pe_head_norm(pe)
                if i == 21:
                    pe_rwkv_turn_v(pe)
                if kind == "lora" and j == 1:
                    for k in range(KT):
                        mm = nc.tensor.matmul(banks[5][0:SSD_HEADS, 0:T], slot("w_in", "lora")[:, k, 256:264],
                                              hg[:, k, :], start=(k == 0), stop=(k == KT - 1))
                    mm.then_inc(*mark("proj1_dt", "proj1 dt"))
                    chunk_used("w_in", "lora", 0, ("proj1 dt",))
                elif j == dict(PROJ)[kind] - 1:
                    chunk_used("w_in", kind, 0, ("proj1", b))

        def dve_project1_rwkv(dve):
            norm_reciprocal(dve, "pre_mix")
            dve.wait_ge(*so_far("norm_rstd"))
            for b in range(7):
                dve.wait_ge(*at("proj1", b))
                if b == 0:
                    dve.wait_ge(*at("pads"))
                nc.vector.tensor_tensor(raw[:, 2 * b:2 * b + 2, 1:T + 1], halves(b % 4), over(rstd[:, :], 2),
                                        ALU.mult).then_inc(*mark("proj1_scaled", "proj1 out", b))
                if b == 2:
                    dve.wait_ge(*at("proj1 dt"))
                    nc.vector.tensor_tensor(dtT[0:8, :], banks[5][0:8, 0:T], rstd[0:8, :], ALU.mult).then_inc(
                        *mark("dt_raw", "dt raw"))
            for b in range(7):
                dve.wait_ge(*at("shift difference", b))
                for i in (2 * b, 2 * b + 1):
                    nc.vector.scalar_tensor_tensor(shf[:, i, :], shf[:, i, :], par("rwkv_mu", i),
                                                   raw[:, i, 1:T + 1], ALU.mult, ALU.add).then_inc(
                        *mark("shifted", "shifted", i))

        def pool_project1(pool):
            nc.gpsimd.memset(raw[:, :, 0:1], 0.0)
            nc.gpsimd.memset(eps[:, 0:1], EPS)
            nc.gpsimd.memset(eps[:, 1:2], GN_EPS)
            nc.gpsimd.memset(eps[:, 2:3], 1.0)
            nc.gpsimd.memset(rawx[:, :, 0:3], 0.0).then_inc(*mark("pads", "pads"))
            for b in range(7):
                pool.wait_ge(*at("proj1 out", b))
                nc.gpsimd.tensor_tensor(shf[:, 2 * b:2 * b + 2, :], raw[:, 2 * b:2 * b + 2, 0:T],
                                        raw[:, 2 * b:2 * b + 2, 1:T + 1], ALU.subtract).then_inc(
                    *mark("shift_difference", "shift difference", b))

        def dve_ssd_conv(dve, first, last):
            for b in range(first, last):
                dve.wait_ge(*at("proj1", b))
                if b < 11:
                    n = b - 7
                    nc.vector.tensor_tensor(rawx[:, 2 * n:2 * n + 2, 3:T + 3], halves(b % 4), over(rstd[:, :], 2),
                                            ALU.mult).then_inc(*mark("proj1_scaled", "proj1 out", b))
                    dve.wait_ge(*so_far("proj1_scaled"))
                    for i in (2 * n, 2 * n + 1):
                        nc.vector.tensor_scalar(xbc[:, i, :], rawx[:, i, 3:T + 3], par("ssd_conv_w", 24 + i),
                                                par("ssd_conv_b", i), ALU.mult, ALU.add).then_inc(*mark("ssd_conv"))
                    for tap in (2, 1, 0):
                        dve.wait_ge(*so_far("ssd_conv"))
                        for i in (2 * n, 2 * n + 1):
                            nc.vector.scalar_tensor_tensor(xbc[:, i, :], rawx[:, i, tap:tap + T],
                                                           par("ssd_conv_w", 8 * tap + i), xbc[:, i, :],
                                                           ALU.mult, ALU.add).then_inc(
                                *mark("ssd_conv", "ssd conv", tap, i))
                else:
                    n = b - 11
                    nc.vector.tensor_tensor(zs[:, 2 * n:2 * n + 2, :], halves(b % 4), over(rstd[:, :], 2),
                                            ALU.mult).then_inc(*mark("proj1_scaled", "proj1 out", b))

        def act_ssd_silu(act):
            act.wait_ge(*at("dt raw"))
            nc.scalar.activation(dtT[0:8, :], dtT[0:8, :], ACT.Identity, bias=par("ssd_dt_bias", 0)[0:8, :]).then_inc(
                *mark("dt_act", "dt biased"))
            act.wait_ge(*so_far("dt_act"))
            nc.scalar.activation(dtmp[0:8, :], dtT[0:8, :], ACT.Abs).then_inc(*mark("dt_act"))
            nc.scalar.preload_act_table_set("natural_log_exp_and_others")
            nc.scalar.activation(acol[0:8, 0:1], par("ssd_a_log", 0)[0:8, :], ACT.Exp).then_inc(*mark("dt_act"))
            act.wait_ge(*so_far("dt_act"))
            nc.scalar.activation(dtmp[0:8, :], dtmp[0:8, :], ACT.Exp, scale=-1.0).then_inc(*mark("dt_act", "dt exp"))
            act.wait_ge(*at("dt one plus"))
            nc.scalar.activation(rms[0:8, :], aT[0:8, :], ACT.Ln).then_inc(*mark("dt_act", "dt log"))
            for i in range(8):
                act.wait_ge(*at("ssd conv", 0, i))
                nc.scalar.activation(rawx[:, i, 3:T + 3], xbc[:, i, :], ACT.Silu).then_inc(
                    *mark("ssd_silu", "ssd silu", i))
            for n in range(2):
                act.wait_ge(*at("proj1 out", 11 + n))
                nc.scalar.activation(zs[:, 2 * n:2 * n + 2, :], zs[:, 2 * n:2 * n + 2, :], ACT.Silu).then_inc(
                    *mark("z_silu", "z silu", n))

        def dve_dt(dve):
            dve.wait_ge(*at("dt exp"))
            nc.vector.tensor_scalar(aT[0:8, :], dtmp[0:8, :], 1.0, None, ALU.add).then_inc(
                *mark("dt_vector", "dt one plus"))
            dve.wait_ge(*so_far("dt_vector"))
            nc.vector.scalar_tensor_tensor(dtmp[0:8, :], aT[0:8, :], -1.0, dtmp[0:8, :], ALU.add,
                                           ALU.subtract).then_inc(*mark("dt_vector"))
            dve.wait_ge(*so_far("dt_vector"))
            nc.vector.scalar_tensor_tensor(dtT[0:8, :], dtT[0:8, :], 0.0, dtmp[0:8, :], ALU.max,
                                           ALU.subtract).then_inc(*mark("dt_vector"))
            dve.wait_ge(*so_far("dt_vector"))
            dve.wait_ge(*at("dt log"))
            nc.vector.tensor_tensor(dtT[0:8, :], dtT[0:8, :], rms[0:8, :], ALU.add).then_inc(*mark("dt_vector"))
            dve.wait_ge(*so_far("dt_vector"))
            nc.vector.tensor_scalar(aT[0:8, :], dtT[0:8, :], acol[0:8, 0:1], -1.0, ALU.mult, ALU.mult).then_inc(
                *mark("dt_vector", "dt done"))

        XS = lambda i: rawx[:, i, 3:T + 3]

        def pe_ssd(pe):
            pe.wait_ge(*at("mem", "gained", 7))
            pe.wait_ge(*at("k token-major"))
            pe.wait_ge(*at("dt done"))
            for c in range(NC_):
                nc.tensor.transpose(banks[4][:, 8 * c:8 * c + 8], dtT[0:8, c * C:(c + 1) * C], ident[0:8, 0:8])
                mm = nc.tensor.transpose(banks[4][:, 16 + 8 * c:24 + 8 * c], aT[0:8, c * C:(c + 1) * C],
                                         ident[0:8, 0:8])
            mm.then_inc(*mark("ssd_pe", "ssd dt turned"))
            for c in range(NC_):
                for i in range(4):
                    if c == 0:
                        pe.wait_ge(*at("ssd silu", i))
                    mm = nc.tensor.transpose(quarters(5 + c)[:, i, :], XS(i)[:, c * C:(c + 1) * C], ident)
                mm.then_inc(*mark("ssd_pe", "ssd x turned", c))
            for g in range(2):
                pe.wait_ge(*at("ssd silu", 4 + g))
                mm = nc.tensor.transpose(quarters(7)[:, g, :], XS(4 + g)[:, 0:C], ident)
            mm.then_inc(*mark("ssd_pe", "ssd b turned"))
            pe.wait_ge(*at("ssd dt token-major"))
            for c in range(NC_):
                mm = nc.tensor.matmul(banks[4][:, 32 + 8 * c:40 + 8 * c], const("incl"), atok[:, c, :],
                                      start=True, stop=True)
            mm.then_inc(*mark("ssd_pe", "ssd cumulative"))
            pe.wait_ge(*at("proj1 out", 12))
            for g in range(2):
                pe.wait_ge(*at("ssd silu", 6 + g))
                for c in range(NC_):
                    mm = nc.tensor.matmul(quarters(0)[:, 2 * g + c, :], XS(4 + g)[:, c * C:(c + 1) * C],
                                          XS(6 + g)[:, c * C:(c + 1) * C], start=True, stop=True)
            mm.then_inc(*mark("ssd_pe", "ssd bc"))
            for c in range(NC_):
                for g in range(2):
                    b = (1, 2, 3, 7)[2 * c + g]
                    if b == 7:
                        pe.wait_ge(*at("ssd b token-major"))
                    for i in range(4):
                        mm = nc.tensor.matmul(quarters(b)[:, i, :],
                                              atok[:, c, 4 * g + i:4 * g + i + 1].broadcast_to([P, P]),
                                              const("incl"), start=True, stop=True)
                    mm.then_inc(*mark("ssd_pe", "ssd sums", c, g))
            pe.wait_ge(*at("ssd decayed"))
            pe.wait_ge(*at("ssd cumulative column"))
            for g in range(2):
                mm = nc.tensor.matmul(banks[4][:, 256 * g:256 * g + 256], BTOKS[:, g, :],
                                      XDEC[:, 256 * g:256 * g + 256], start=True, stop=True)
            mm.then_inc(*mark("ssd_pe", "ssd state"))
            for c in range(NC_):
                for g in range(2):
                    pe.wait_ge(*at("ssd mt", c, g))
                    if c == 1:
                        pe.wait_ge(*at("ssd cex", g))
                        pe.wait_ge(*at("ssd state out"))
                    elif g == 0:
                        pe.wait_ge(*at("ssd x token-major", 1))
                    for i in range(4):
                        hd = 4 * g + i
                        o = halves(5 + g)[64 * (hd % 2):64 * (hd % 2) + 64, (hd // 2) % 2, c * C:(c + 1) * C]
                        mm = nc.tensor.matmul(o, XDT[:, c, 64 * hd:64 * hd + 64], MT[g][:, i, :],
                                              start=True, stop=(c == 0), skip_group_check=True)
                        if c == 1:
                            mm = nc.tensor.matmul(o, ST[:, 64 * hd:64 * hd + 64], CEX[:, hd, :],
                                                  start=False, stop=True, skip_group_check=True)
                    mm.then_inc(*mark("ssd_pe", "ssd y", c, g))

        def dve_ssd(dve):
            dve.wait_ge(*at("ssd dt turned"))
            nc.vector.tensor_copy(view(SOLVE + 6176, 32), banks[4][:, 0:32]).then_inc(
                *mark("ssd_vector", "ssd dt token-major"))
            dve.wait_ge(*so_far("ssd_vector"))
            for c in range(NC_):
                dve.wait_ge(*at("ssd x turned", c))
                nc.vector.tensor_tensor(XDT[:, c, :].rearrange("p (h d) -> p h d", h=8),
                                        banks[5 + c][:, :].rearrange("p (h d) -> p h d", h=8),
                                        along(dtok[:, c, :], 64), ALU.mult).then_inc(
                    *mark("ssd_vector", "ssd x token-major", c))
            dve.wait_ge(*at("ssd b turned"))
            nc.vector.tensor_copy(BTOKS, quarters(7)[:, 0:2, :]).then_inc(*mark("ssd_vector", "ssd b token-major"))
            dve.wait_ge(*at("ssd cumulative"))
            nc.vector.tensor_copy(cstok.rearrange("p c h -> p (c h)"), banks[4][:, 32:48]).then_inc(
                *mark("ssd_vector", "ssd cumulative column"))
            dve.wait_ge(*at("ssd bc"))
            nc.vector.tensor_tensor(GT, quarters(0), over(const("incl"), 4), ALU.mult).then_inc(*mark("ssd_vector"))
            for c in range(NC_):
                for g in range(2):
                    b = (1, 2, 3, 7)[2 * c + g]
                    dve.wait_ge(*at("ssd sums", c, g))
                    dve.wait_ge(*so_far("ssd_vector"))
                    if c == 0:
                        nc.vector.tensor_tensor(dect[:, 4 * g:4 * g + 4], quarters(b)[:, :, C - 1],
                                                cstok[:, 0, 4 * g:4 * g + 4], ALU.subtract).then_inc(
                            *mark("ssd_vector", "ssd decay exponent", g))
                    else:
                        dve.wait_ge(*at("ssd cexp", g))
                        dve.wait_ge(*at("ssd cex", g))
                    if c == 0 and g == 0:
                        dve.wait_ge(*at("ssd silu", 7))
                    for i in range(4):
                        hd = 4 * g + i
                        nc.vector.tensor_scalar(EX[g][:, i, :], quarters(b)[:, i, :], cstok[:, c, hd:hd + 1], 0.0,
                                                ALU.subtract, ALU.min).then_inc(
                            *mark("ssd_vector", "ssd exponent", c, g, i))
                    if c == 0 and g == 1:
                        dve.wait_ge(*at("ssd decay"))
                        nc.vector.tensor_tensor(XDEC.rearrange("p (h d) -> p h d", h=8),
                                                XDT[:, 0, :].rearrange("p (h d) -> p h d", h=8),
                                                along(dect, 64), ALU.mult).then_inc(*mark("ssd_vector", "ssd decayed"))
                    if c == 0 and g == 1:
                        for gg in range(2):
                            dve.wait_ge(*at("ssd decays", 0, gg))
                            nc.vector.tensor_tensor(MT[gg], EX[gg], over(GT[:, 2 * gg, :], 4), ALU.mult).then_inc(
                                *mark("ssd_vector", "ssd mt", 0, gg))
            dve.wait_ge(*at("ssd state"))
            nc.vector.tensor_copy(ST, banks[4][:, :]).then_inc(*mark("ssd_vector", "ssd state out"))
            for gg in range(2):
                dve.wait_ge(*at("ssd decays", 1, gg))
                dve.wait_ge(*at("ssd y", 0, gg))
                nc.vector.tensor_tensor(MT[gg], EX[gg], over(GT[:, 2 * gg + 1, :], 4), ALU.mult).then_inc(
                    *mark("ssd_vector", "ssd mt", 1, gg))
            for g in range(2):
                dve.wait_ge(*at("ssd y", 1, g))
                for j in range(2):
                    i = 2 * g + j
                    nc.vector.scalar_tensor_tensor(YS[:, i, :], XS(i), par("ssd_d", i), halves(5 + g)[:, j, :],
                                                   ALU.mult, ALU.add).then_inc(*mark("ssd_vector"))
                dve.wait_ge(*so_far("ssd_vector"))
                dve.wait_ge(*at("z silu", g))
                nc.vector.tensor_tensor(YS[:, 2 * g:2 * g + 2, :], YS[:, 2 * g:2 * g + 2, :],
                                        zs[:, 2 * g:2 * g + 2, :], ALU.mult).then_inc(
                    *mark("ssd_vector", "ssd gated", g))
            for g in range(2):
                dve.wait_ge(*at("ssd group root", g))
                nc.vector.reciprocal(GT[:, 2 * g:2 * g + 2, :].rearrange("p a b -> p (a b)"),
                                     zs[:, 2 * g, :]).then_inc(*mark("ssd_vector"))
                dve.wait_ge(*so_far("ssd_vector"))
                for j in range(2):
                    i = 2 * g + j
                    nc.vector.scalar_tensor_tensor(mix[:, i, :], YS[:, i, :], par("ssd_norm", i),
                                                   GT[:, 2 * g:2 * g + 2, :].rearrange("p a b -> p (a b)"),
                                                   ALU.mult, ALU.mult).then_inc(*mark("ssd_vector", "mix1", i))

        def act_ssd(act):
            for g in range(2):
                act.wait_ge(*at("ssd decay exponent", g))
            nc.scalar.activation(dect, dect, ACT.Exp).then_inc(*mark("ssd_act", "ssd decay"))
            for g in range(2):
                act.wait_ge(*at("ssd exponent", 0, g, 3))
                nc.scalar.activation(EX[g], EX[g], ACT.Exp).then_inc(*mark("ssd_act", "ssd decays", 0, g))
            for g in range(2):
                act.wait_ge(*at("ssd sums", 1, g))
                nc.scalar.activation(CEX[:, 4 * g:4 * g + 4, :], quarters((3, 7)[g]), ACT.Exp).then_inc(
                    *mark("ssd_act", "ssd cexp", g))
            for g in range(2):
                act.wait_ge(*at("ssd exponent", 1, g, 3))
                nc.scalar.activation(EX[g], EX[g], ACT.Exp).then_inc(*mark("ssd_act", "ssd decays", 1, g))
            for g in range(2):
                act.wait_ge(*at("ssd gated", g))
                nc.scalar.activation(xbc[:, 2 * g:2 * g + 2, :], YS[:, 2 * g:2 * g + 2, :], ACT.Square).then_inc(
                    *mark("ssd_act", "ssd squares", g))
            for g in range(2):
                act.wait_ge(*at("ssd group total", g))
                nc.scalar.activation(zs[:, 2 * g, :], banks[g][:, 0:T], ACT.Sqrt, bias=eps[:, 0:1],
                                     scale=1.0 / 256).then_inc(*mark("ssd_act", "ssd group root", g))

        def pool_ssd(pool):
            for g in range(2):
                pool.wait_ge(*at("ssd cexp", g))
                nc.gpsimd.tensor_tensor(CEX[:, 4 * g:4 * g + 4, :], CEX[:, 4 * g:4 * g + 4, :],
                                        over(XS(6 + g)[:, C:2 * C], 4), ALU.mult).then_inc(
                    *mark("ssd_pool", "ssd cex", g))

        def pe_ssd_norm(pe):
            for g in range(2):
                pe.wait_ge(*at("ssd squares", g))
                pe.wait_ge(*at("ssd exponent", 0, 1, 3))
                for j in range(2):
                    mm = nc.tensor.matmul(banks[g][:, 0:T], ones, xbc[:, 2 * g + j, :], start=(j == 0), stop=(j == 1))
                mm.then_inc(*mark("ssd_pe", "ssd group total", g))

        def sync_mem(sp):
            sp.wait_ge(*at("x turned", 3))
            sp.dma_start(mix[:, :, :].rearrange("p a b -> p (a b)").rearrange("p (c d) -> p c d", c=2),
                         w["mem_2"][0].rearrange("(c p) d -> p c d", p=P)).then_inc(
                *mark("mem_landed", "mem landed", by=16))

        def pe_mem_turn(pe):
            pe.wait_ge(*at("mem landed"))
            xt = mix[:, :, :].rearrange("p a b -> p (a b)").rearrange("p (c d) -> p c d", c=2)
            for b in range(4):
                if b >= 2:
                    pe.wait_ge(*at("mem", "gained", 2 * b - 3))
                if b < 2:
                    pe.wait_ge(*at("v token-major", b))
                for m in (2 * b, 2 * b + 1):
                    for c in range(NC_):
                        mm = nc.tensor.transpose(halves(4 + b % 2)[:, m % 2, c * C:(c + 1) * C],
                                                 xt[:, c, m * P:(m + 1) * P], ident)
                mm.then_inc(*mark("mem_turned", "mem turned", b))

        def act_mem_norm(act):
            for m in range(KT):
                act.wait_ge(*at("mem turned", m // 2))
                if m >= 4:
                    act.wait_ge(*at("mem", "summed", m // 2 - 2))
                if m == 0:
                    act.wait_ge(*at("pre_mix", "summed", 3))
                src = halves(4 + m // 2 % 2)[:, m % 2, :]
                nc.scalar.activation(sqs[:, m // 2 % 2, 256 * (m % 2):256 * (m % 2) + 256], src,
                                     ACT.Square).then_inc(*mark("norm_squares", "mem", "squares", m))
                nc.scalar.activation(hg[:, m, :], src, ACT.Copy, scale=par("norm_mem_2", m)).then_inc(
                    *mark("norm_gained", "mem", "gained", m))

        MEM_PARTS = 32

        def pe_mem_part(pe, part):
            if part < 16:
                i, ks = part // 2, range(4 * (part % 2), 4 * (part % 2) + 4)
                b = 6 + (i // 2) % 2
                if part == 0:
                    pe.wait_ge(*at("mem", "gained", 7))
                    pe.wait_ge(*at("mem", "root"))
                if part % 8 == 0:
                    chunk_ready(pe, "w_xk_2", "cols", i // 4)
                if part == 4:
                    pe.wait_ge(*at("mem column"))
                if part >= 8 and part % 4 == 0:
                    pe.wait_ge(*at("keys", i // 2 - 2))
                for k in ks:
                    mm = nc.tensor.matmul(halves(b)[:, i % 2, :],
                                          slot("w_xk_2", "cols", i // 4)[:, k, (i % 4) * P:(i % 4 + 1) * P],
                                          hg[:, k, :], start=(k == 0), stop=(k == KT - 1))
                if part % 4 == 3:
                    mm.then_inc(*mark("mem_pe", "keys bank", i // 2))
                    if i % 4 == 3:
                        chunk_used("w_xk_2", "cols", i // 4, ("keys bank", i // 2))
            else:
                n, q = (part - 16) // 4, part % 4
                half, c = n // 2, n % 2
                b = 6 + n % 2
                if q == 0:
                    chunk_ready(pe, "w_xv_2", "cols", half)
                    pe.wait_ge(*(at("keys", 2 + n) if n < 2 else at("values", n - 2)))
                for k in (2 * q, 2 * q + 1):
                    mm = nc.tensor.matmul(banks[b][:, :], hg[:, k, c * C:(c + 1) * C],
                                          slot("w_xv_2", "cols", half)[:, k, :],
                                          start=(k == 0), stop=(k == KT - 1))
                if q == 3:
                    mm.then_inc(*mark("mem_pe", "values bank", n))
                    if n % 2:
                        chunk_used("w_xv_2", "cols", half, ("values bank", n))

        def dve_mem_keys(dve, b):
            dve.wait_ge(*at("keys bank", b))
            nc.vector.tensor_tensor(xk[:, 2 * b:2 * b + 2, :], halves(6 + b % 2), over(rstd[:, :], 2),
                                    ALU.mult).then_inc(*mark("mem_keys", "keys", b))

        def act_mem_column(act):
            act.wait_ge(*at("mem", "column"))
            nc.scalar.activation(rcol[:, :], banks[7][:, 0:2], ACT.Copy).then_inc(*mark("mem_act", "mem column"))

        def act_mem_values(act, n):
            if n == 0:
                act.wait_ge(*so_far("mem_act"))
            half, c = n // 2, n % 2
            act.wait_ge(*at("values bank", n))
            nc.scalar.activation(xv[:, c, 512 * half:512 * half + 512], banks[6 + n % 2][:, :], ACT.Copy,
                                 scale=rcol[:, c:c + 1]).then_inc(*mark("mem_act", "values", n))

        def act_lora(act):
            act.wait_ge(*at("shifted", 4))
            nc.scalar.activation(WA[0:64, :], WA[0:64, :], ACT.Tanh).then_inc(*mark("lora_in", "lora tanh"))
            act.wait_ge(*at("shifted", 5))
            nc.scalar.activation(GLO, GLO, ACT.Sigmoid).then_inc(*mark("lora_in", "lora gate"))

        def sync_lora(sp):
            sp.dma_start(lora_w[0:64, 0:RW_D], w["rwkv_w2"][0]).then_inc(*mark("lora_weights", by=16))
            sp.dma_start(lora_w[64:128, 0:RW_D], w["rwkv_a2"][0]).then_inc(
                *mark("lora_weights", "lora weights", by=16))

        def sync_gate(sp):
            sp.wait_ge(*at("mem", "total"))
            sp.dma_start(gate_w[:, :], w["rwkv_g2"][0]).then_inc(*mark("gate_weights", "gate weights", by=16))

        def pe_lora(pe):
            pe.wait_ge(*at("lora weights"))
            pe.wait_ge(*at("lora tanh"))
            pe.wait_ge(*at("h", 3))
            for j in range(4):
                mm = nc.tensor.matmul(halves(6 + j // 2)[:, j % 2, :], lora_w[0:64, j * P:(j + 1) * P], WA[0:64, :],
                                      start=True, stop=True)
                if j % 2:
                    mm.then_inc(*mark("lora_pe", "decay lora", j // 2))
            pe.wait_ge(*at("pre_mix", "root"))
            pe.wait_ge(*at("dt raw"))
            for j in range(4):
                mm = nc.tensor.matmul(halves(4 + j // 2)[:, j % 2, :], lora_w[64:128, j * P:(j + 1) * P],
                                      WA[64:128, :], start=True, stop=True)
                if j % 2:
                    mm.then_inc(*mark("lora_pe", "rate lora", j // 2))

        def pe_head_norm(pe):
            pe.wait_ge(*at("decay sigmoid", 3))
            pe.wait_ge(*at("k squares"))
            for i in range(2):
                mm = nc.tensor.matmul(banks[6 + i][:, :], head_ones, flat(KSQ)[:, 512 * i:512 * i + 512],
                                      start=True, stop=True)
                mm.then_inc(*mark("lora_pe", "k sums", i))

        def flat(v):
            return v.rearrange("p a b -> p (a b)")

        KP = K_

        def act_rwkv_prepare(act):
            act.wait_ge(*at("shifted", 13))
            for j in range(4):
                act.wait_ge(*at("decay lora", j // 2))
                nc.scalar.activation(SW[:, j, :], halves(6 + j // 2)[:, j % 2, :], ACT.Sigmoid,
                                     bias=par("rwkv_w0", j)).then_inc(*mark("rwkv_act", "decay sigmoid", j))
            for j in range(4):
                act.wait_ge(*at("rate lora", j // 2))
                nc.scalar.activation(A_[:, j, :], halves(4 + j // 2)[:, j % 2, :], ACT.Sigmoid,
                                     bias=par("rwkv_a0", j)).then_inc(*mark("rwkv_act", "rate", j))
            act.wait_ge(*at("kk"))
            nc.scalar.activation(flat(KSQ), flat(KK), ACT.Square).then_inc(*mark("rwkv_act", "k squares"))

        def act_rwkv_exponentials(act):
            for i in range(2):
                act.wait_ge(*at("k sums", i))
                nc.scalar.activation(flat(KSQ)[:, 512 * i:512 * i + 512], banks[6 + i][:, :], ACT.Sqrt).then_inc(
                    *mark("rwkv_act", "k norms", i))
            act.wait_ge(*at("cumulative"))
            nc.scalar.activation(flat(E1), flat(CS), ACT.Exp, scale=-DECAY_SCALE).then_inc(*mark("rwkv_act", "E1"))
            nc.scalar.activation(flat(E2), flat(CS), ACT.Exp, scale=DECAY_SCALE).then_inc(*mark("rwkv_act", "E2"))
            act.wait_ge(*at("cumulative before"))
            nc.scalar.activation(flat(E0), flat(E0), ACT.Exp, scale=-DECAY_SCALE).then_inc(*mark("rwkv_act", "E0"))
            act.wait_ge(*at("state exponent"))
            nc.scalar.activation(small[:, 8:12], small[:, 4:8], ACT.Exp, scale=-DECAY_SCALE).then_inc(
                *mark("rwkv_act", "state factor"))

        def dve_rwkv_prepare(dve):
            dve.wait_ge(*at("shifted", 13))
            for j in range(4):
                nc.vector.tensor_scalar(KK[:, j, :], K_[:, j, :], par("rwkv_k_k", j), None, ALU.mult).then_inc(
                    *mark("rwkv_vector", *(("kk",) if j == 3 else ())))
            for j in range(4):
                dve.wait_ge(*at("decay sigmoid", j))
                nc.vector.tensor_tensor_scan(CS[:, j, :], const("reset128"), SW[:, j, :], 0.0, ALU.mult,
                                             ALU.add).then_inc(*mark("rwkv_vector"))
            dve.wait_ge(*so_far("rwkv_vector"))
            cs4 = flat(CS).rearrange("p (j c t) -> p j c t", j=4, c=NC_)
            nc.vector.tensor_copy(small[:, 12:20].rearrange("p (j c) -> p j c", c=2), cs4[:, :, :, C // 2 - 1]).then_inc(
                *mark("rwkv_vector", "middles"))
            dve.wait_ge(*so_far("rwkv_vector"))
            mid = small[:, 12:20].rearrange("p (j c) -> p j c", c=2)
            nc.vector.tensor_tensor(small[:, 4:8], cs4[:, :, 0, C - 1], mid[:, :, 0], ALU.subtract).then_inc(
                *mark("rwkv_vector"))
            dve.wait_ge(*so_far("rwkv_vector"))
            nc.vector.tensor_tensor(small[:, 4:8], small[:, 4:8], mid[:, :, 1], ALU.add).then_inc(
                *mark("rwkv_vector", "state exponent"))
            jc = flat(CS).rearrange("p (jc t) -> p jc t", t=C)
            nc.vector.tensor_tensor(jc, jc, along(small[:, 12:20], C), ALU.subtract).then_inc(
                *mark("rwkv_vector", "cumulative"))
            nc.vector.tensor_scalar(small[:, 0:4], params[:, PARAM_AT["rwkv_k_a"]:PARAM_AT["rwkv_k_a"] + 4], -1.0,
                                    1.0, ALU.mult, ALU.add).then_inc(*mark("rwkv_vector"))
            dve.wait_ge(*so_far("rwkv_vector"))
            for j in range(4):
                dve.wait_ge(*at("rate", j))
                nc.vector.tensor_scalar(BT[:, j, :], A_[:, j, :], par("rwkv_k_a", j), small[:, j:j + 1],
                                        ALU.mult, ALU.add).then_inc(*mark("rwkv_vector"))
            dve.wait_ge(*so_far("rwkv_vector"))
            nc.vector.tensor_tensor(flat(KP), flat(K_), flat(BT), ALU.mult).then_inc(*mark("rwkv_vector", "k prime"))

        def dve_rwkv_scaled(dve):
            dve.wait_ge(*at("k norms", 1))
            nc.vector.tensor_scalar(flat(KSQ), flat(KSQ), 1e-12, None, ALU.max).then_inc(*mark("rwkv_vector"))
            dve.wait_ge(*so_far("rwkv_vector"))
            nc.vector.reciprocal(flat(KSQ), flat(KSQ)).then_inc(*mark("rwkv_vector"))
            dve.wait_ge(*so_far("rwkv_vector"))
            nc.vector.tensor_tensor(flat(KK), flat(KK), flat(KSQ), ALU.mult).then_inc(*mark("rwkv_vector", "kk unit"))
            dve.wait_ge(*so_far("rwkv_vector"))
            nc.vector.tensor_tensor(flat(BT), flat(KK), flat(A_), ALU.mult).then_inc(*mark("rwkv_vector"))
            dve.wait_ge(*so_far("rwkv_vector"))
            dve.wait_ge(*at("E2"))
            nc.vector.tensor_tensor(flat(BT), flat(BT), flat(E2), ALU.mult).then_inc(*mark("rwkv_vector", "BT"))
            dve.wait_ge(*at("E0"))
            nc.vector.tensor_tensor(flat(E0), flat(E0), flat(KK), ALU.mult).then_inc(*mark("rwkv_vector", "AT"))
            dve.wait_ge(*so_far("rwkv_vector"))
            nc.vector.tensor_tensor(flat(E2), flat(E2), flat(KP), ALU.mult).then_inc(*mark("rwkv_vector", "KT"))

        AT_, RT_, KT_ = E0, E1, E2

        def pool_rwkv_prepare(pool):
            pool.wait_ge(*at("cumulative"))
            pool.wait_ge(*at("decay sigmoid", 3))
            nc.gpsimd.tensor_tensor(flat(E0), flat(CS), flat(SW), ALU.subtract).then_inc(
                *mark("rwkv_pool", "cumulative before"))
            pool.wait_ge(*at("E1"))
            nc.gpsimd.tensor_tensor(flat(E1), flat(E1), flat(R_), ALU.mult).then_inc(*mark("rwkv_pool", "RT"))

        def pe_rwkv_turn_v(pe):
            pe.wait_ge(*at("rate", 3))
            for c in range(NC_):
                for j in range(4):
                    mm = nc.tensor.transpose(quarters(4 + c)[:, j, :], V_[:, j, c * C:(c + 1) * C], ident)
                mm.then_inc(*mark("rwkv_pe", "v turned", c))

        def pe_rwkv_turn(pe):
            pe.wait_ge(*at("k norms", 1))
            for n, (src, step) in enumerate(((BT, "BT"), (KT_, "KT"))):
                pe.wait_ge(*at(step))
                for j in range(4):
                    mm = nc.tensor.transpose(quarters(6 + n)[:, j, :], src[:, j, 0:C], ident)
                mm.then_inc(*mark("rwkv_pe", ("b turned", "k turned")[n]))

        def act_rwkv_turn_v(act):
            for c in range(NC_):
                act.wait_ge(*at("v turned", c))
                if c == 0:
                    act.wait_ge(*at("cumulative before"))
                nc.scalar.activation(VTOK[:, c, :], banks[4 + c][:, :], ACT.Copy).then_inc(
                    *mark("rwkv_act", "v token-major", c))

        def act_rwkv_turn(act):
            act.wait_ge(*at("b turned"))
            act.wait_ge(*so_far("rwkv_act"))
            nc.scalar.activation(BTOK, banks[6][:, :], ACT.Copy, scale=-1.0).then_inc(*mark("rwkv_act", "b token-major"))
            act.wait_ge(*at("k turned"))
            nc.scalar.activation(KTOK, banks[7][:, :], ACT.Copy).then_inc(*mark("rwkv_act", "k token-major"))

        def product(pe, g, c, bank, left, right):
            for j in range(4):
                lo = 64 * g
                mm = nc.tensor.matmul(quarters(bank)[:, j, :], left[lo:lo + 64, j, c * C:(c + 1) * C],
                                      right[lo:lo + 64, j, c * C:(c + 1) * C], start=True, stop=True)
            return mm

        def pe_rwkv_chunk(pe, c):
            def fill(n):
                pe_mem_part(pe, 16 * c + n)

            if c == 0:
                pe.wait_ge(*at("k token-major"))
                pe.wait_ge(*at("AT"))
                pe.wait_ge(*at("ssd group root", 1))
                pe.wait_ge(*at("ssd gated", 1))
            for g in range(2):
                b = 3 * g
                if c == 1:
                    pe.wait_ge(*at("y out", 0, g))
                    pe.wait_ge(*at("state out", g))
                product(pe, g, c, b, BT, AT_).then_inc(*mark("solve_pe", "LT bank", c, g))
                product(pe, g, c, b + 1, AT_, BT).then_inc(*mark("solve_pe", "L bank", c, g))
            fill(0)
            for n, m in enumerate(LEVELS):
                B = P // (2 * m)
                for g in range(2):
                    st = sets[g]
                    pe.wait_ge(*at("X", c, g, n))
                    for j in range(4):
                        x = st["X"][:, j, :].rearrange("p (b two m) -> p b two m", b=B, two=2)[:, :, 0, :]
                        mm = nc.tensor.matmul(banks[3 * g][:, 64 * j:64 * j + 64], st["LT"][:, j, :], x,
                                              start=True, stop=True)
                    mm.then_inc(*mark("solve_pe", "P bank", c, g, n))
                fill(1 + 2 * n)
                for g in range(2):
                    st = sets[g]
                    p = st["PA"] if n % 2 == 0 else st["PB"]
                    pe.wait_ge(*at("P", c, g, n))
                    for j in range(4):
                        x = p[:, j, :].rearrange("p (b two m) -> p b two m", b=B, two=2)[:, :, 0, :]
                        mm = nc.tensor.matmul(banks[3 * g + 1][:, 64 * j:64 * j + 64], st["XT"][:, j, :], x,
                                              start=True, stop=True)
                    for j in range(4):
                        x = st["XT"][:, j, :].rearrange("p (b two m) -> p b two m", b=B, two=2)[:, :, 1, :]
                        mm = nc.tensor.matmul(banks[3 * g + 1][:, 256 + 64 * j:320 + 64 * j], p[:, j, :], x,
                                              start=True, stop=True)
                    mm.then_inc(*mark("solve_pe", "dX bank", c, g, n))
                fill(2 + 2 * n)
            n = len(LEVELS)
            for g in range(2):
                st = sets[g]
                pe.wait_ge(*at("X", c, g, n))
                for j in range(4):
                    mm = nc.tensor.matmul(banks[3 * g][64:128, 64 * j:64 * j + 64], st["LT"][0:64, j, 64:128],
                                          st["X"][0:64, j, 0:64], start=True, stop=True)
                mm.then_inc(*mark("solve_pe", "P64 bank", c, g))
            for g in range(2):
                product(pe, g, c, 3 * g + 1, KT_, AT_).then_inc(*mark("solve_pe", "AK bank", c, g))
            fill(11)
            for g in range(2):
                st = sets[g]
                pe.wait_ge(*at("P64", c, g))
                for j in range(4):
                    mm = nc.tensor.matmul(banks[3 * g + 2][0:64, 64 * j:64 * j + 64], P64[g][64:128, j, :],
                                          st["XT"][64:128, j, 64:128], start=True, stop=True)
                mm.then_inc(*mark("solve_pe", "dXT64 bank", c, g))
            for g in range(2):
                if c == 0 and g == 0:
                    pe.wait_ge(*at("RT"))
                product(pe, g, c, 3 * g, KT_, RT_).then_inc(*mark("solve_pe", "RK bank", c, g))
            fill(12)
            for g in range(2):
                st = sets[g]
                lo = 64 * g
                pe.wait_ge(*at("AK", c, g))
                for j in range(4):
                    hd = 2 * j + g
                    mm = nc.tensor.matmul(banks[3 * g + 1][:, 64 * j:64 * j + 64], st["LT"][:, j, :],
                                          VTOK[:, c, 64 * hd:64 * hd + 64], start=True, stop=(c == 0))
                    if c:
                        mm = nc.tensor.matmul(banks[3 * g + 1][:, 64 * j:64 * j + 64],
                                              AT_[lo:lo + 64, j, C:2 * C], s0c[lo:lo + 64, j, :],
                                              start=False, stop=True)
                mm.then_inc(*mark("solve_pe", "G bank", c, g))
            for g in range(2):
                pe.wait_ge(*at("XT64", c, g))
                product(pe, g, c, 3 * g + 2, BT, RT_).then_inc(*mark("solve_pe", "RB bank", c, g))
            fill(13)
            for g in range(2):
                st = sets[g]
                pe.wait_ge(*at("G", c, g))
                for j in range(4):
                    mm = nc.tensor.matmul(banks[3 * g + 1][:, 256 + 64 * j:320 + 64 * j], st["XT"][:, j, :],
                                          st["G"][:, j, :], start=True, stop=True)
                mm.then_inc(*mark("solve_pe", "U bank", c, g))
            fill(14)
            for g in range(2):
                st = sets[g]
                lo = 64 * g
                pe.wait_ge(*at("U", c, g))
                pe.wait_ge(*at("RK", c, g))
                pe.wait_ge(*at("RB", c, g))
                if c == 0:
                    for j in range(4):
                        hd = 2 * j + g
                        o = banks[3 * g + 2][lo:lo + 64, 64 * j:64 * j + 64]
                        nc.tensor.matmul(o, KTOK[:, 64 * hd:64 * hd + 64], VTOK[:, 0, 64 * hd:64 * hd + 64],
                                         start=True, stop=False)
                        mm = nc.tensor.matmul(o, BTOK[:, 64 * hd:64 * hd + 64], st["U"][:, j, :],
                                              start=False, stop=True)
                    mm.then_inc(*mark("solve_pe", "state bank", g))
                for j in range(4):
                    hd = 2 * j + g
                    o = quarters(3 * g)[lo:lo + 64, j, :]
                    nc.tensor.matmul(o, VTOK[:, c, 64 * hd:64 * hd + 64], st["X"][:, j, :], start=True, stop=False)
                    mm = nc.tensor.matmul(o, st["U"][:, j, :], st["ARB"][:, j, :], start=False, stop=(c == 0))
                    if c:
                        mm = nc.tensor.matmul(o, s0c[lo:lo + 64, j, :], RT_[lo:lo + 64, j, C:2 * C],
                                              start=False, stop=True)
                mm.then_inc(*mark("solve_pe", "y bank", c, g))
            fill(15)

        def dve_rwkv_chunk(dve, c):
            for g in range(2):
                st = sets[g]
                b = 3 * g
                dve.wait_ge(*at("LT bank", c, g))
                if c:
                    dve.wait_ge(*at("y bank", 0, g))
                nc.vector.tensor_tensor(st["LT"], quarters(b), over(const("neg_strict"), 4), ALU.mult).then_inc(
                    *mark("solve_vector", "LT", c, g))
                dve.wait_ge(*at("L bank", c, g))
                nc.vector.tensor_tensor(st["X"], quarters(b + 1), over(const("pair"), 4), ALU.mult).then_inc(
                    *mark("solve_vector"))
                dve.wait_ge(*at("LT", c, g))
                nc.vector.tensor_tensor(st["XT"], st["LT"], over(const("pair_t"), 4), ALU.mult).then_inc(
                    *mark("solve_vector"))
                dve.wait_ge(*so_far("solve_vector"))
                both = st["XX"]
                nc.vector.tensor_tensor(both, both, over(ident, 8), ALU.add).then_inc(
                    *mark("solve_vector", "X", c, g, 0))
            for n, m in enumerate(LEVELS):
                B = P // (2 * m)
                mask = const("levels")[:, 64 * n:64 * n + 64].rearrange("p (b m) -> p b m", b=B)
                for g in range(2):
                    st = sets[g]
                    p = (st["PA"] if n % 2 == 0 else st["PB"]).rearrange("p j (b two m) -> p j b two m", b=B, two=2)
                    dve.wait_ge(*at("P bank", c, g, n))
                    dve.wait_ge(*at("P zeroed", c, g, n))
                    nc.vector.tensor_tensor(p[:, :, :, 0, :],
                                            banks[3 * g][:, 0:256].rearrange("p (j b m) -> p j b m", j=4, b=B),
                                            mask.unsqueeze(1).broadcast_to([P, 4, B, m]), ALU.mult).then_inc(
                        *mark("solve_vector", "P", c, g, n))
                for g in range(2):
                    grown = sets[g]["grown"](m)
                    dve.wait_ge(*at("dX bank", c, g, n))
                    nc.vector.tensor_tensor(grown, banks[3 * g + 1][:, :].rearrange("p (w jb m) -> p w jb m", w=2, m=m),
                                            grown, ALU.add).then_inc(*mark("solve_vector", "X", c, g, n + 1))
                if c == 0 and n in (1, 3):
                    dve_mem_keys(dve, n // 2)
            for g in range(2):
                dve.wait_ge(*at("P64 bank", c, g))
                nc.vector.tensor_copy(P64[g][64:128, :, :],
                                      banks[3 * g][64:128, 0:256].rearrange("p (j m) -> p j m", j=4)).then_inc(
                    *mark("solve_vector", "P64", c, g))
            for g in range(2):
                dve.wait_ge(*at("AK bank", c, g))
                nc.vector.tensor_tensor(sets[g]["LT"], quarters(3 * g + 1), over(const("strict"), 4),
                                        ALU.mult).then_inc(*mark("solve_vector", "AK", c, g))
            for g in range(2):
                dve.wait_ge(*at("dXT64 bank", c, g))
                nc.vector.tensor_copy(sets[g]["XT"][0:64, :, 64:128],
                                      banks[3 * g + 2][0:64, 0:256].rearrange("p (j m) -> p j m", j=4)).then_inc(
                    *mark("solve_vector", "XT64", c, g))
            for g in range(2):
                dve.wait_ge(*at("RK bank", c, g))
                nc.vector.tensor_tensor(sets[g]["X"], quarters(3 * g), over(const("incl"), 4), ALU.mult).then_inc(
                    *mark("solve_vector", "RK", c, g))
            if c == 0:
                dve_mem_keys(dve, 2)
            for g in range(2):
                dve.wait_ge(*at("RB bank", c, g))
                nc.vector.tensor_tensor(sets[g]["ARB"], quarters(3 * g + 2), over(const("neg_incl"), 4),
                                        ALU.mult).then_inc(*mark("solve_vector", "RB", c, g))
            if c == 0:
                for g in range(2):
                    lo = 64 * g
                    dve.wait_ge(*at("state bank", g))
                    dve.wait_ge(*at("state factor"))
                    nc.vector.tensor_tensor(s0c[lo:lo + 64], banks[3 * g + 2][lo:lo + 64, 0:256].rearrange(
                        "p (j m) -> p j m", j=4), along(small[lo:lo + 64, 8:12], 64), ALU.mult).then_inc(
                        *mark("solve_vector", "state out", g))
                dve_mem_keys(dve, 3)

        def act_rwkv_chunk(act, c):
            if c:
                for n in range(3):
                    act_mem_values(act, n)
            for g in range(2):
                st = sets[g]
                act.wait_ge(*at("G bank", c, g))
                nc.scalar.activation(st["G"], banks[3 * g + 1][:, 0:256].rearrange("p (j m) -> p j m", j=4),
                                     ACT.Copy).then_inc(*mark("solve_act", "G", c, g))
            for g in range(2):
                st = sets[g]
                act.wait_ge(*at("U bank", c, g))
                nc.scalar.activation(st["U"], banks[3 * g + 1][:, 256:512].rearrange("p (j m) -> p j m", j=4),
                                     ACT.Copy).then_inc(*mark("solve_act", "U", c, g))
            for g in range(2):
                lo = 64 * g
                act.wait_ge(*at("y bank", c, g))
                nc.scalar.activation(Y[lo:lo + 64, :, c * C:(c + 1) * C], quarters(3 * g)[lo:lo + 64],
                                     ACT.Copy).then_inc(*mark("solve_act", "y out", c, g))
            if c:
                act_mem_values(act, 3)

        def pool_rwkv_chunk(pool, c):
            for n in range(len(LEVELS)):
                for g in range(2):
                    p = sets[g]["PA"] if n % 2 == 0 else sets[g]["PB"]
                    if n >= 2:
                        pool.wait_ge(*at("dX bank", c, g, n - 2))
                    elif c:
                        pool.wait_ge(*at("dX bank", 0, g, 4 - n))
                    else:
                        pool.wait_ge(*at("mix1", 3))
                    nc.gpsimd.memset(p, 0.0).then_inc(*mark("solve_pool", "P zeroed", c, g, n))

        def pe_rwkv_end(pe):
            pe.wait_ge(*at("lora gate"))
            pe.wait_ge(*at("gate weights"))
            for g in range(2):
                pe.wait_ge(*at("y out", 1, g))
                pe.wait_ge(*at("RB", 1, g))
            pe.wait_ge(*at("values", 3))
            for j in range(4):
                mm = nc.tensor.matmul(halves(j // 2)[:, j % 2, :], gate_w[:, j * P:(j + 1) * P], GLO,
                                      start=True, stop=True)
            mm.then_inc(*mark("rwkv_end_pe", "gate bank"))
            for i in range(2):
                mm = nc.tensor.matmul(banks[4 + i][:, :], head_ones, flat(Y)[:, 512 * i:512 * i + 512],
                                      start=True, stop=True)
                mm.then_inc(*mark("rwkv_end_pe", "mean bank", i))
            pe.wait_ge(*at("bonus products"))
            for i in range(2):
                mm = nc.tensor.matmul(banks[2 + i][:, :], head_ones, flat(A_)[:, 512 * i:512 * i + 512],
                                      start=True, stop=True)
            mm.then_inc(*mark("rwkv_end_pe", "bonus bank"))
            for i in range(2):
                pe.wait_ge(*at("centred squares", i))
                mm = nc.tensor.matmul(banks[6 + i][:, :], head_ones, flat(BT)[:, 512 * i:512 * i + 512],
                                      start=True, stop=True)
                mm.then_inc(*mark("rwkv_end_pe", "variance bank", i))

        def pool_bonus(pool):
            pool.wait_ge(*at("k prime"))
            pool.wait_ge(*at("BT"))
            pool.wait_ge(*at("mix1", 3))
            nc.gpsimd.tensor_tensor(flat(A_), flat(R_), flat(KP), ALU.mult).then_inc(*mark("rwkv_pool", "rk"))

        def dve_bonus(dve):
            dve.wait_ge(*at("rk"))
            for j in range(4):
                nc.vector.tensor_scalar(A_[:, j, :], A_[:, j, :], par("rwkv_r_k", j), None, ALU.mult).then_inc(
                    *mark("bonus_vector", *(("bonus products",) if j == 3 else ())))

        def dve_rwkv_end(dve):
            for i in range(2):
                dve.wait_ge(*at("mean bank", i))
                nc.vector.scalar_tensor_tensor(flat(Y)[:, 512 * i:512 * i + 512], banks[4 + i][:, :], -1.0 / RW_HD,
                                               flat(Y)[:, 512 * i:512 * i + 512], ALU.mult, ALU.add).then_inc(
                    *mark("rwkv_end_vector", "centred", i))
            dve.wait_ge(*at("bonus bank"))
            for i in range(2):
                nc.vector.tensor_tensor(flat(BONUS)[:, 512 * i:512 * i + 512], banks[2 + i][:, :],
                                        flat(V_)[:, 512 * i:512 * i + 512], ALU.mult).then_inc(
                    *mark("rwkv_end_vector", "bonus", i))
            for i in range(2):
                s = slice(512 * i, 512 * i + 512)
                dve.wait_ge(*at("variance root", i))
                nc.vector.reciprocal(flat(E1)[:, s], flat(E1)[:, s]).then_inc(*mark("rwkv_end_vector"))
                dve.wait_ge(*so_far("rwkv_end_vector"))
                nc.vector.tensor_tensor(flat(Y)[:, s], flat(Y)[:, s], flat(E1)[:, s], ALU.mult).then_inc(
                    *mark("rwkv_end_vector"))
                dve.wait_ge(*so_far("rwkv_end_vector"))
                for j in (2 * i, 2 * i + 1):
                    nc.vector.tensor_scalar(Y[:, j, :], Y[:, j, :], par("rwkv_ln_w", j), par("rwkv_ln_b", j),
                                            ALU.mult, ALU.add).then_inc(*mark("rwkv_end_vector"))
                dve.wait_ge(*so_far("rwkv_end_vector"))
                nc.vector.tensor_tensor(flat(Y)[:, s], flat(Y)[:, s], flat(BONUS)[:, s], ALU.add).then_inc(
                    *mark("rwkv_end_vector"))
                dve.wait_ge(*so_far("rwkv_end_vector"))
                nc.vector.tensor_tensor(mix[:, 4 + 2 * i:6 + 2 * i, :].rearrange("p a b -> p (a b)"),
                                        banks[i][:, :], flat(Y)[:, s], ALU.mult).then_inc(
                    *mark("rwkv_end_vector", "mix1", 4 + 2 * i))
                same(("mix1", 5 + 2 * i), ("mix1", 4 + 2 * i))

        def act_rwkv_end(act):
            for i in range(2):
                s = slice(512 * i, 512 * i + 512)
                act.wait_ge(*at("centred", i))
                nc.scalar.activation(flat(BT)[:, s], flat(Y)[:, s], ACT.Square).then_inc(
                    *mark("rwkv_end_act", "centred squares", i))
            for i in range(2):
                s = slice(512 * i, 512 * i + 512)
                act.wait_ge(*at("variance bank", i))
                nc.scalar.activation(flat(E1)[:, s], banks[6 + i][:, :], ACT.Sqrt, bias=eps[:, 1:2],
                                     scale=1.0 / RW_HD).then_inc(*mark("rwkv_end_act", "variance root", i))

        hid = view(0, FF2T, T)
        uraw = [view(8192 + 516 * i, 2, T + 2) for i in range(4)]
        uacc = [view(10256 + 512 * i, 2, T) for i in range(4)]
        gsil = [view(12304 + 512 * i, 2, T) for i in range(2)]

        def first_group(pe, n, chunks, label, free):
            for b in range(4):
                if free:
                    pe.wait_ge(*at(*free(b)))
            for name, kind, i in chunks:
                chunk_ready(pe, name, kind, i)
            for k in range(KT):
                pe.wait_ge(*at(n, "gained", k))
                for m in range(8):
                    mm = nc.tensor.matmul(halves(m // 2)[:, m % 2, :],
                                          slot(*chunks[m // 4])[:, k, (m % 4) * P:(m % 4 + 1) * P], hg[:, k, :],
                                          start=(k == 0 and m % 2 == 0), stop=(k == KT - 1), skip_group_check=True)
                    if k == KT - 1 and m % 2:
                        mm.then_inc(*mark("projected", label, "bank", m // 2))
            chunk_used(*chunks[0], (label, "bank", 1))
            chunk_used(*chunks[1], (label, "bank", 3))

        def pe_ffn_up(pe):
            first_group(pe, "pre_ffn", [("ffn_w_up", "pair", 0), ("ffn_w_up", "pair", 1)], "up",
                        lambda b: ("mix1", 7))
            norm_total(pe, "pre_ffn", 4, ("post_mix", "added", 7))
            for b in range(4, FFT):
                j = b // 2
                if b % 2 == 0:
                    chunk_ready(pe, "ffn_w_up", "pair", j)
                pe.wait_ge(*at("up scaled", b - 4))
                for i in range(2):
                    mm = wide(pe, ("ffn_w_up", "pair", j), 2 * (b % 2) + i, b % 4, i)
                mm.then_inc(*mark("projected", "up", "bank", b))
                if b % 2:
                    chunk_used("ffn_w_up", "pair", j, ("up", "bank", b))

        def pool_ffn(pool):
            pool.wait_ge(*at("mix1", 7))
            for i in range(4):
                nc.gpsimd.memset(uraw[i][:, :, 0:2], 0.0).then_inc(*mark("ffn_pads", *(("ffn pads",) if i == 3 else ())))

        def dve_ffn(dve):
            norm_reciprocal(dve, "pre_ffn")
            dve.wait_ge(*so_far("norm_rstd"))
            dve.wait_ge(*at("ffn pads"))
            for b in range(FFT):
                r = b % 4
                dve.wait_ge(*at("up", "bank", b))
                nc.vector.tensor_tensor(uraw[r][:, :, 2:T + 2], halves(r), over(rstd[:, :], 2), ALU.mult).then_inc(
                    *mark("up_scaled", "up scaled", b))
                dve.wait_ge(*so_far("up_scaled"))
                if b >= 4 and b % 2 == 0:
                    dve.wait_ge(*at("gate silu", b // 2 - 2, 1))
                tile0 = 2 * (b // 2) + FFT * (b % 2)
                for i in range(2):
                    nc.vector.tensor_scalar(uacc[r][:, i, :], uraw[r][:, i, 2:T + 2],
                                            par("ffn_conv_w", 2 * 2 * FFT + tile0 + i), None, ALU.mult).then_inc(
                        *mark("ffn_conv"))
                for tap in (1, 0):
                    dve.wait_ge(*so_far("ffn_conv"))
                    for i in range(2):
                        nc.vector.scalar_tensor_tensor(uacc[r][:, i, :], uraw[r][:, i, tap:tap + T],
                                                       par("ffn_conv_w", 2 * FFT * tap + tile0 + i), uacc[r][:, i, :],
                                                       ALU.mult, ALU.add).then_inc(*mark("ffn_conv", "conv", tap, b, i))
                if b % 2:
                    dve.wait_ge(*so_far("ffn_conv"))
                    for i in range(2):
                        dve.wait_ge(*at("gate silu", b // 2, i))
                        nc.vector.scalar_tensor_tensor(hid[:, b - 1 + i, :], uacc[r][:, i, :],
                                                       par("ffn_conv_b", FFT + b - 1 + i), gsil[b // 2 % 2][:, i, :],
                                                       ALU.add, ALU.mult).then_inc(*mark("hidden", "hid", b - 1 + i))

        def act_ffn(act):
            for p in range(FFT // 2):
                for i in range(2):
                    act.wait_ge(*at("conv", 0, 2 * p, i))
                    if p >= 2:
                        act.wait_ge(*at("hid", 2 * (p - 2) + i))
                    nc.scalar.activation(gsil[p % 2][:, i, :], uacc[2 * p % 4][:, i, :], ACT.Silu,
                                         bias=par("ffn_conv_b", 2 * p + i)).then_inc(
                        *mark("gate_silu", "gate silu", p, i))

        FR, BCS, EB, EMB, HQ, KF = (view(1024 * i, 4, T) for i in range(6))
        KETOK, VI = view(6144, NC_, HG_D), view(7168, NC_, HG_D)
        GH = view(8192, 4, T)
        AM = [view(9216 + 512 * i, 4, C) for i in range(2)]
        NS = T // HG_CHUNK
        SV = view(10240, NS - 1, 4 * C)
        MQ, MK = view(13824, 4, T), view(14848, 4, T)
        MV = view(15872, NC_, 512)
        SC = view(16896, 4, 2 * T)
        PT = view(18944, 4, 3 * C)
        lb = sb("lb_stat", 64)
        stat = small

        W2 = lambda i: ("w_in_2", "cols", i)

        def pe_project2(pe):
            first_group(pe, "norm_mix", [W2(1), W2(0)], "in2", lambda b: ("up scaled", FFT - 4 + b))
            norm_total(pe, "norm_mix", 4, ("post_ffn", "added", 7))
            def token_major(i, b0, label, waits):
                chunk_ready(pe, *W2(i))
                for c in range(NC_):
                    pe.wait_ge(*at(*waits[c]))
                    for k in range(KT):
                        mm = nc.tensor.matmul(banks[b0 + c][:, :], hg[:, k, c * C:(c + 1) * C], slot(*W2(i))[:, k, :],
                                              start=(k == 0), stop=(k == KT - 1))
                    mm.then_inc(*mark("projected", label, c))
                chunk_used(*W2(i), (label, 1))

            def feature_major(i, b0, label, waits):
                chunk_ready(pe, *W2(i))
                for b in range(2):
                    pe.wait_ge(*at(*waits[b]))
                    for j in range(2):
                        mm = wide(pe, W2(i), 2 * b + j, b0 + b, j)
                    mm.then_inc(*mark("projected", label, b))
                chunk_used(*W2(i), (label, 1))

            token_major(2, 0, "hi bank", [("hf scaled", 0), ("hf scaled", 1)])
            column_rstd(pe, "norm_mix", 5, ("norm_mix", "root"))
            feature_major(3, 2, "hgate bank", [("hq scaled", 0), ("hq scaled", 1)])
            feature_major(4, 0, "mq bank", [("hi out", 0), ("hi out", 1)])
            feature_major(5, 2, "mk bank", [("hgate scaled", 0), ("hgate scaled", 1)])
            token_major(6, 0, "mv bank", [("mq scaled", 0), ("mq scaled", 1)])

        def dve_project2(dve):
            norm_reciprocal(dve, "norm_mix")
            dve.wait_ge(*so_far("norm_rstd"))
            nc.vector.tensor_tensor(lb[:, 8:12], params[:, PARAM_AT["lb_logits_2"]:PARAM_AT["lb_logits_2"] + 4],
                                    params[:, PARAM_AT["lb_logits_2"] + 4:PARAM_AT["lb_logits_2"] + 8],
                                    ALU.subtract).then_inc(*mark("hgrn_vector", "lb logits"))

            def scaled(dst, b0, full, label):
                for b in range(2):
                    dve.wait_ge(*at(*full(b)))
                    nc.vector.tensor_tensor(dst[:, 2 * b:2 * b + 2, :], halves(b0 + b), over(rstd[:, :], 2),
                                            ALU.mult).then_inc(*mark("in2_scaled", label, b))

            scaled(FR, 0, lambda b: ("in2", "bank", b), "hf scaled")
            scaled(HQ, 2, lambda b: ("in2", "bank", 2 + b), "hq scaled")
            dve.wait_ge(*at("lb"))
            nc.vector.tensor_scalar(lb[:, 4:8], lb[:, 0:4], -1.0, 1.0, ALU.mult, ALU.add).then_inc(*mark("hgrn_vector"))
            dve.wait_ge(*so_far("hgrn_vector"))
            dve.wait_ge(*at("f sigmoid"))
            for j in range(4):
                nc.vector.tensor_scalar(FR[:, j, :], FR[:, j, :], lb[:, 4 + j:5 + j], lb[:, j:j + 1], ALU.mult,
                                        ALU.add).then_inc(*mark("hgrn_vector"))
            dve.wait_ge(*so_far("hgrn_vector"))
            nc.vector.tensor_scalar(flat(KF), flat(FR), -1.0, 1.0, ALU.mult, ALU.add).then_inc(
                *mark("hgrn_vector", "f"))
            dve.wait_ge(*at("log f"))
            for j in range(4):
                nc.vector.tensor_tensor_scan(BCS[:, j, :], const("reset32"), EB[:, j, :], 0.0, ALU.mult,
                                             ALU.add).then_inc(*mark("hgrn_vector", *(("b",) if j == 3 else ())))
            scaled(GH, 2, lambda b: ("hgate bank", b), "hgate scaled")
            dve.wait_ge(*at("exp b"))
            nc.vector.tensor_copy(stat[:, 0:32], flat(EB)[:, HG_CHUNK - 1::HG_CHUNK]).then_inc(
                *mark("hgrn_vector", "decays"))
            nc.vector.tensor_tensor(flat(HQ), flat(HQ), flat(EB), ALU.mult).then_inc(*mark("hgrn_vector", "q~"))
            dve.wait_ge(*at("exp -b"))
            nc.vector.tensor_tensor(flat(KF), flat(KF), flat(EMB), ALU.mult).then_inc(*mark("hgrn_vector", "k~"))
            dve.wait_ge(*so_far("hgrn_vector"))
            nc.vector.tensor_tensor(flat(EMB).rearrange("p (n t) -> p n t", t=HG_CHUNK),
                                    flat(KF).rearrange("p (n t) -> p n t", t=HG_CHUNK),
                                    along(stat[:, 0:32], HG_CHUNK), ALU.mult).then_inc(*mark("hgrn_vector", "k end"))
            scaled(MQ, 0, lambda b: ("mq bank", b), "mq scaled")
            scaled(MK, 2, lambda b: ("mk bank", b), "mk scaled")

        def act_project2(act):
            act.wait_ge(*at("lb logits"))
            nc.scalar.activation(lb[:, 0:4], lb[:, 8:12], ACT.Sigmoid).then_inc(*mark("hgrn_act", "lb"))
            act.wait_ge(*at("hf scaled", 1))
            nc.scalar.activation(flat(FR), flat(FR), ACT.Sigmoid).then_inc(*mark("hgrn_act", "f sigmoid"))
            act.wait_ge(*at("f"))
            nc.scalar.preload_act_table_set("natural_log_exp_and_others")
            nc.scalar.activation(flat(EB), flat(FR), ACT.Ln).then_inc(*mark("hgrn_act", "log f"))
            act.wait_ge(*at("norm_mix", "column"))
            nc.scalar.activation(rcol[:, :], banks[5][:, 0:2], ACT.Copy).then_inc(*mark("hgrn_act", "mix column"))
            act.wait_ge(*so_far("hgrn_act"))
            for c in range(NC_):
                act.wait_ge(*at("hi bank", c))
                nc.scalar.activation(VI[:, c, :], banks[c][:, :], ACT.Copy, scale=rcol[:, c:c + 1]).then_inc(
                    *mark("in2_scaled_act", "hi out", c))
            act.wait_ge(*at("b"))
            nc.scalar.activation(flat(EB), flat(BCS), ACT.Exp).then_inc(*mark("hgrn_act", "exp b"))
            nc.scalar.activation(flat(EMB), flat(BCS), ACT.Exp, scale=-1.0).then_inc(*mark("hgrn_act", "exp -b"))
            act.wait_ge(*at("hgate scaled", 1))
            nc.scalar.activation(flat(GH), flat(GH), ACT.Silu).then_inc(*mark("hgrn_act", "hgate"))

        def pe_hgrn(pe):
            pe.wait_ge(*at("mix column"))
            pe.wait_ge(*at("post_ffn", "added", 7))
            pe.wait_ge(*at("k~"))
            for c in range(NC_):
                for j in range(4):
                    mm = nc.tensor.matmul(quarters(4 + c)[:, j, :], KF[:, j, c * C:(c + 1) * C],
                                          HQ[:, j, c * C:(c + 1) * C], start=True, stop=True)
                mm.then_inc(*mark("hgrn_pe", "A bank", c))
            pe.wait_ge(*at("k end"))
            for c in range(NC_):
                for j in range(4):
                    mm = nc.tensor.transpose(quarters(6 + c)[:, j, :], EMB[:, j, c * C:(c + 1) * C], ident)
                mm.then_inc(*mark("hgrn_pe", "k end turned", c))

        def pe_hgrn_states(pe):
            for n in range(NS - 1):
                c, r = n // 4, 32 * (n % 4)
                pe.wait_ge(*at("k end token-major", c))
                pe.wait_ge(*(at("A", n) if n < 2 else at("hgrn state", n - 2)))
                for j in range(4):
                    mm = nc.tensor.matmul(quarters(4 + n % 2)[:, j, :], KETOK[r:r + 32, c, j * C:(j + 1) * C],
                                          VI[r:r + 32, c, j * C:(j + 1) * C], start=True, stop=True,
                                          tile_position=(r, 0))
                mm.then_inc(*mark("hgrn_pe", "hgrn state bank", n))
            for c in range(NC_):
                pe.wait_ge(*at("A", c))
                pe.wait_ge(*at("k end token-major", c))
                for j in range(4):
                    nc.tensor.matmul(halves(6 + j // 2)[:, j % 2, c * C:(c + 1) * C], VI[:, c, j * C:(j + 1) * C],
                                     AM[c][:, j, :], start=(c == 0 and j % 2 == 0), stop=False, skip_group_check=True)
            for n in range(1, NS):
                pe.wait_ge(*at("hgrn state", n - 1))
                for j in range(4):
                    mm = nc.tensor.matmul(halves(6 + j // 2)[:, j % 2, n * HG_CHUNK:(n + 1) * HG_CHUNK],
                                          SV[:, n - 1, j * C:(j + 1) * C],
                                          HQ[:, j, n * HG_CHUNK:(n + 1) * HG_CHUNK], start=False, stop=(n == NS - 1),
                                          skip_group_check=True)
            mm.then_inc(*mark("hgrn_pe", "o bank"))

        def pe_hgrn_norm(pe):
            for i in range(2):
                pe.wait_ge(*at("o squares", i))
                pe.wait_ge(*at("hgrn state", NS - 2))
                mm = nc.tensor.matmul(banks[4 + i][:, :], ones, flat(BCS)[:, 512 * i:512 * i + 512],
                                      start=True, stop=True)
                mm.then_inc(*mark("hgrn_pe", "o total", i))

        def dve_hgrn(dve):
            for c in range(NC_):
                dve.wait_ge(*at("A bank", c))
                nc.vector.tensor_tensor(AM[c], quarters(4 + c), over(const("chunk32"), 4), ALU.mult).then_inc(
                    *mark("hgrn_vector", "A", c))
            for n in range(NS - 1):
                dve.wait_ge(*at("hgrn state bank", n))
                if n:
                    dve.wait_ge(*at("hgrn state", n - 1))
                for j in range(4):
                    b = quarters(4 + n % 2)[:, j, :]
                    o = SV[:, n, j * C:(j + 1) * C]
                    if n == 0:
                        ins = nc.vector.tensor_copy(o, b)
                    else:
                        ins = nc.vector.scalar_tensor_tensor(o, SV[:, n - 1, j * C:(j + 1) * C],
                                                             stat[:, NS * j + n:NS * j + n + 1], b, ALU.mult, ALU.add)
                    ins.then_inc(*mark("hgrn_vector", *(("hgrn state", n) if j == 3 else ())))

        def act_hgrn(act):
            for c in range(NC_):
                act.wait_ge(*at("k end turned", c))
                nc.scalar.activation(KETOK[:, c, :], banks[6 + c][:, :], ACT.Copy).then_inc(
                    *mark("hgrn_act", "k end token-major", c))

        def act_hgrn_end(act):
            act.wait_ge(*at("o bank"))
            for i in range(2):
                nc.scalar.activation(flat(BCS)[:, 512 * i:512 * i + 512], banks[6 + i][:, :], ACT.Square).then_inc(
                    *mark("hgrn_act", "o squares", i))
            for i in range(2):
                act.wait_ge(*at("o total", i))
                nc.scalar.activation(flat(FR)[:, 512 * i:512 * i + 512], banks[4 + i][:, :], ACT.Sqrt,
                                     bias=eps[:, 0:1], scale=1.0 / C).then_inc(*mark("hgrn_act", "o root", i))

        def dve_hgrn_end(dve):
            for i in range(2):
                s = slice(512 * i, 512 * i + 512)
                dve.wait_ge(*at("o root", i))
                nc.vector.reciprocal(flat(FR)[:, s], flat(FR)[:, s]).then_inc(*mark("hgrn_vector"))
                dve.wait_ge(*so_far("hgrn_vector"))
                nc.vector.tensor_tensor(flat(FR)[:, s], banks[6 + i][:, :], flat(FR)[:, s], ALU.mult).then_inc(
                    *mark("hgrn_vector"))
                dve.wait_ge(*so_far("hgrn_vector"))
                dve.wait_ge(*at("hgate"))
                for j in (2 * i, 2 * i + 1):
                    nc.vector.scalar_tensor_tensor(mix[:, j, :], FR[:, j, :], par("hgrn_norm_2", j), GH[:, j, :],
                                                   ALU.mult, ALU.mult).then_inc(*mark("hgrn_vector", "mix2", j))

        def pe_rotary(pe):
            for n, (v, b0, ready, free) in enumerate(((MQ, 2, "mq scaled", "mk scaled"), (MK, 0, "mk scaled", "mv out"))):
                pe.wait_ge(*at(ready, 1))
                pe.wait_ge(*at(free, 1))
                for i in range(2):
                    mm = nc.tensor.matmul(banks[b0 + i][0:ROT, :], const("swap")[0:ROT, 0:ROT],
                                          flat(v)[0:ROT, 512 * i:512 * i + 512], start=True, stop=True)
                mm.then_inc(*mark("moba_pe", "swapped", n))

        def act_moba_values(act):
            for c in range(NC_):
                act.wait_ge(*at("mv bank", c))
                nc.scalar.activation(MV[:, c, :], banks[c][:, :], ACT.Copy, scale=rcol[:, c:c + 1]).then_inc(
                    *mark("in2_scaled_act", "mv out", c))

        def dve_rotary(dve):
            tmp = EB
            for n, (v, b0) in enumerate(((MQ, 2), (MK, 0))):
                dve.wait_ge(*at("swapped", n))
                dve.wait_ge(*(at("k~") if n == 0 else so_far("rotary")))
                for i in range(2):
                    nc.vector.tensor_tensor(tmp[0:ROT, 2 * i:2 * i + 2, :], halves(b0 + i)[0:ROT],
                                            over(const("sin")[0:ROT, :], 2), ALU.mult).then_inc(
                        *mark("rotary", "rotary bank read", n, i))
                dve.wait_ge(*so_far("rotary"))
                nc.vector.tensor_tensor(v[0:ROT], v[0:ROT], over(const("cos")[0:ROT, :], 4), ALU.mult).then_inc(
                    *mark("rotary"))
                dve.wait_ge(*so_far("rotary"))
                nc.vector.tensor_tensor(flat(v)[0:ROT], flat(v)[0:ROT], flat(tmp)[0:ROT], ALU.add).then_inc(
                    *mark("rotary", "rotated", n))

        def pe_moba_scores(pe):
            pe.wait_ge(*at("rotated", 1))
            for j in range(MB_HEADS):
                b = (0, 1, 2, 3)[j]
                nc.tensor.matmul(halves(b)[:, 0, 0:C], MQ[:, j, 0:C], MK[:, j, 0:C], start=True, stop=True)
                mm = nc.tensor.matmul(halves(b)[:, 1, :], MQ[:, j, C:2 * C], MK[:, j, :], start=True, stop=True)
                mm.then_inc(*mark("moba_pe", "moba scores", j))

        def pe_moba_turn(pe):
            for j in range(MB_HEADS):
                pe.wait_ge(*at("moba normal", j, 1))
                nc.tensor.transpose(quarters(j)[:, 0, :], SC[:, j, 0:C], ident)
                nc.tensor.transpose(quarters(j)[:, 1, :], SC[:, j, T:T + C], ident)
                mm = nc.tensor.transpose(quarters(j)[:, 2, :], SC[:, j, T + C:2 * T], ident)
                mm.then_inc(*mark("moba_pe", "moba turned", j))
            for j in range(MB_HEADS):
                pe.wait_ge(*at("moba p", j))
                if j % 2 == 0:
                    pe.wait_ge(*at("moba p", j + 1))
                o = halves(j // 2)[:, j % 2, :]
                nc.tensor.matmul(o, MV[:, 0, j * C:(j + 1) * C], PT[:, j, 0:T], start=(j % 2 == 0), stop=False,
                                 skip_group_check=True)
                mm = nc.tensor.matmul(o[:, C:T], MV[:, 1, j * C:(j + 1) * C], PT[:, j, T:T + C], start=False,
                                      stop=True, skip_group_check=True)
                if j % 2:
                    mm.then_inc(*mark("moba_pe", "moba o", j // 2))

        def dve_moba(dve):
            for j in range(MB_HEADS):
                dve.wait_ge(*at("moba scores", j))
                nc.vector.scalar_tensor_tensor(SC[:, j, 0:C], halves(j)[:, 0, 0:C], MB_HD ** -0.5,
                                               const("causal")[:, C:2 * C], ALU.mult, ALU.add).then_inc(
                    *mark("moba_vector"))
                nc.vector.scalar_tensor_tensor(SC[:, j, T:2 * T], halves(j)[:, 1, :], MB_HD ** -0.5,
                                               const("causal"), ALU.mult, ALU.add).then_inc(
                    *mark("moba_vector", "moba masked", j))
            for j in range(MB_HEADS):
                dve.wait_ge(*at("moba masked", j))
                nc.vector.tensor_reduce(stat[:, 32 + 2 * j:33 + 2 * j], SC[:, j, 0:C], AX.X, ALU.max).then_inc(
                    *mark("moba_vector"))
                nc.vector.tensor_reduce(stat[:, 33 + 2 * j:34 + 2 * j], SC[:, j, T:2 * T], AX.X, ALU.max).then_inc(
                    *mark("moba_vector"))
                dve.wait_ge(*so_far("moba_vector"))
                nc.vector.tensor_scalar(stat[:, 40 + 2 * j:42 + 2 * j], stat[:, 32 + 2 * j:34 + 2 * j], -1.0, None,
                                        ALU.mult).then_inc(*mark("moba_vector", "moba max", j))
            for j in range(MB_HEADS):
                dve.wait_ge(*at("moba exp", j, 1))
                nc.vector.reciprocal(stat[:, 56 + 2 * j:58 + 2 * j], stat[:, 48 + 2 * j:50 + 2 * j]).then_inc(
                    *mark("moba_vector"))
                dve.wait_ge(*so_far("moba_vector"))
                nc.vector.tensor_scalar(SC[:, j, 0:C], SC[:, j, 0:C], stat[:, 56 + 2 * j:57 + 2 * j], None,
                                        ALU.mult).then_inc(*mark("moba_vector"))
                nc.vector.tensor_scalar(SC[:, j, T:2 * T], SC[:, j, T:2 * T], stat[:, 57 + 2 * j:58 + 2 * j], None,
                                        ALU.mult).then_inc(*mark("moba_vector", "moba normal", j, 1))

        def act_moba(act):
            for j in range(MB_HEADS):
                act.wait_ge(*at("moba max", j))
                nc.scalar.activation(SC[:, j, 0:C], SC[:, j, 0:C], ACT.Exp, bias=stat[:, 40 + 2 * j:41 + 2 * j],
                                     accum_out=stat[:, 48 + 2 * j:49 + 2 * j]).then_inc(*mark("moba_act"))
                nc.scalar.activation(SC[:, j, T:2 * T], SC[:, j, T:2 * T], ACT.Exp,
                                     bias=stat[:, 41 + 2 * j:42 + 2 * j],
                                     accum_out=stat[:, 49 + 2 * j:50 + 2 * j]).then_inc(
                    *mark("moba_act", "moba exp", j, 1))
            for j in range(MB_HEADS):
                act.wait_ge(*at("moba turned", j))
                nc.scalar.activation(PT[:, j, :], banks[j][:, 0:3 * C], ACT.Copy).then_inc(
                    *mark("moba_act", "moba p", j))
            for i in range(2):
                act.wait_ge(*at("moba o", i))
                nc.scalar.activation(mix[:, 4 + 2 * i:6 + 2 * i, :], halves(i), ACT.Copy).then_inc(
                    *mark("moba_act", "mix2", 4 + 2 * i))
                same(("mix2", 5 + 2 * i), ("mix2", 4 + 2 * i))

        def dve_residual(dve, label):
            for b in range(4):
                dve.wait_ge(*at(label, "bank", b))
                nc.vector.tensor_tensor(h[:, 2 * b:2 * b + 2, :], halves(4 + b), h[:, 2 * b:2 * b + 2, :],
                                        ALU.add).then_inc(*mark("residual", label, "added", b))

        XQ = view(0, KT, T)
        XS2 = view(2048, 4, 2 * T)
        XPT = view(4096, 4, 2 * T)
        xstat = lb

        def pe_xattn_q(pe):
            first_group(pe, "norm_xattn", [("w_xq_2", "cols", 0), ("w_xq_2", "cols", 1)], "xq",
                        lambda b: ("mix2", 7))
            norm_total(pe, "norm_xattn", 4, ("out2", "added", 3))

        def dve_xattn_q(dve):
            norm_reciprocal(dve, "norm_xattn")
            dve.wait_ge(*so_far("norm_rstd"))
            for b in range(4):
                dve.wait_ge(*at("xq", "bank", b))
                nc.vector.tensor_tensor(XQ[:, 2 * b:2 * b + 2, :], halves(b), over(rstd[:, :], 2),
                                        ALU.mult).then_inc(*mark("xq_scaled", "xq scaled", b))

        def pe_xattn(pe):
            def scores(j):
                pe.wait_ge(*at("xq scaled", j))
                for qb in range(2):
                    for i in range(2):
                        mm = nc.tensor.matmul(halves(j)[:, qb, :], XQ[:, 2 * j + i, qb * C:(qb + 1) * C],
                                              xk[:, 2 * j + i, :], start=(i == 0), stop=(i == 1))
                mm.then_inc(*mark("xattn_pe", "x scores", j))

            def turn(j):
                pe.wait_ge(*at("x normal", j))
                for mt in range(2):
                    for qb in range(2):
                        mm = nc.tensor.transpose(quarters(j)[:, 2 * mt + qb, :],
                                                 XS2[:, j, qb * T + mt * C:qb * T + (mt + 1) * C], ident)
                mm.then_inc(*mark("xattn_pe", "x p turned", j))

            def values(j):
                pe.wait_ge(*at("x p", j))
                if j == 0:
                    pe.wait_ge(*at("norm_xattn", "root"))
                for vt in range(2):
                    for mt in range(2):
                        mm = nc.tensor.matmul(halves(4 + j)[:, vt, :],
                                              xv[:, mt, j * XA_HD + vt * C:j * XA_HD + (vt + 1) * C],
                                              XPT[:, j, mt * T:(mt + 1) * T], start=(mt == 0), stop=(mt == 1))
                mm.then_inc(*mark("xattn_pe", "x o", j))

            for j in range(4):
                scores(j)
            for j in range(4):
                turn(j)
                if j:
                    values(j - 1)
            values(3)

        def dve_xattn(dve):
            for j in range(4):
                dve.wait_ge(*at("x scores", j))
                nc.vector.tensor_reduce(xstat[:, 2 * j:2 * j + 2], halves(j), AX.X, ALU.max).then_inc(
                    *mark("xattn_vector"))
                dve.wait_ge(*so_far("xattn_vector"))
                nc.vector.tensor_scalar(xstat[:, 8 + 2 * j:10 + 2 * j], xstat[:, 2 * j:2 * j + 2], -XA_HD ** -0.5,
                                        None, ALU.mult).then_inc(*mark("xattn_vector", "x max", j))
            for j in range(4):
                dve.wait_ge(*at("x exp", j))
                nc.vector.reciprocal(xstat[:, 24 + 2 * j:26 + 2 * j], xstat[:, 16 + 2 * j:18 + 2 * j]).then_inc(
                    *mark("xattn_vector"))
                dve.wait_ge(*so_far("xattn_vector"))
                for qb in range(2):
                    nc.vector.tensor_scalar(XS2[:, j, qb * T:(qb + 1) * T], XS2[:, j, qb * T:(qb + 1) * T],
                                            xstat[:, 24 + 2 * j + qb:25 + 2 * j + qb], None, ALU.mult).then_inc(
                        *mark("xattn_vector", *(("x normal", j) if qb else ())))

        def act_xattn(act):
            for j in range(4):
                act.wait_ge(*at("x max", j))
                for qb in range(2):
                    nc.scalar.activation(XS2[:, j, qb * T:(qb + 1) * T], halves(j)[:, qb, :], ACT.Exp,
                                         bias=xstat[:, 8 + 2 * j + qb:9 + 2 * j + qb], scale=XA_HD ** -0.5,
                                         accum_out=xstat[:, 16 + 2 * j + qb:17 + 2 * j + qb]).then_inc(
                        *mark("xattn_act", *(("x exp", j) if qb else ())))
            for j in range(4):
                act.wait_ge(*at("x p turned", j))
                nc.scalar.activation(XPT[:, j, :], banks[j][:, :], ACT.Copy).then_inc(*mark("xattn_act", "x p", j))
                if j:
                    x_out(act, j - 1)
            x_out(act, 3)

        def x_out(act, j):
            act.wait_ge(*at("x o", j))
            nc.scalar.activation(mix[:, 2 * j:2 * j + 2, :], halves(4 + j), ACT.Copy).then_inc(
                *mark("xattn_act", "mix3", 2 * j))
            same(("mix3", 2 * j + 1), ("mix3", 2 * j))

        relu = [view(10256 + 512 * i, 2, T) for i in range(4)]

        def pe_mlp(pe):
            first_group(pe, "norm_mlp", [("w_ff1_2", "cols", 0), ("w_ff1_2", "cols", 1)], "ff1",
                        lambda b: ("x p", b))
            norm_total(pe, "norm_mlp", 4, ("xo", "added", 3))
            for b in range(4, FF2T // 2):
                if b % 2 == 0:
                    chunk_ready(pe, "w_ff1_2", "cols", b // 2)
                pe.wait_ge(*at("relu", b - 4))
                for i in range(2):
                    mm = wide(pe, ("w_ff1_2", "cols", b // 2), 2 * (b % 2) + i, b % 4, i)
                mm.then_inc(*mark("projected", "ff1", "bank", b))
                if b % 2:
                    chunk_used("w_ff1_2", "cols", b // 2, ("ff1", "bank", b))

        def dve_mlp(dve):
            norm_reciprocal(dve, "norm_mlp")
            dve.wait_ge(*so_far("norm_rstd"))
            for b in range(FF2T // 2):
                dve.wait_ge(*at("ff1", "bank", b))
                if b >= 4:
                    dve.wait_ge(*at("hid2", 2 * (b - 4)))
                nc.vector.scalar_tensor_tensor(relu[b % 4], halves(b % 4), 0.0, over(rstd[:, :], 2), ALU.max,
                                               ALU.mult).then_inc(*mark("mlp_relu", "relu", b))

        def act_mlp(act):
            for b in range(FF2T // 2):
                act.wait_ge(*at("relu", b))
                nc.scalar.activation(hid[:, 2 * b:2 * b + 2, :], relu[b % 4], ACT.Square).then_inc(
                    *mark("mlp_square", "hid2", 2 * b))
                same(("hid2", 2 * b + 1), ("hid2", 2 * b))

        def dve_final(dve):
            norm_reciprocal(dve, "final")
            dve.wait_ge(*so_far("norm_rstd"))
            for m in range(KT):
                nc.vector.tensor_tensor(mix[:, m, :], hg[:, m, :], rstd[:, :], ALU.mult).then_inc(
                    *mark("final_vector", "normal", m))
            for b in (1, 3):
                dve.wait_ge(*at("out turned", b))
                nc.vector.tensor_copy(xk_tok[:, b // 2, 512 * (b % 2):512 * (b % 2) + 512], banks[b][:, :]).then_inc(
                    *mark("final_vector", "out copied", b))

        xk_tok = xv

        def pe_final(pe):
            norm_total(pe, "final", 4, ("ff2", "added", 3))
            for b in range(4):
                c, half = b // 2, b % 2
                for i in range(4):
                    m = 4 * half + i
                    pe.wait_ge(*at("normal", m))
                    mm = nc.tensor.transpose(quarters(b)[:, i, :], mix[:, m, c * C:(c + 1) * C], ident)
                mm.then_inc(*mark("final_pe", "out turned", b))

        def act_final(act):
            for b in (0, 2):
                act.wait_ge(*at("out turned", b))
                nc.scalar.activation(xk_tok[:, b // 2, 512 * (b % 2):512 * (b % 2) + 512], banks[b][:, :],
                                     ACT.Copy).then_inc(*mark("final_act", "out copied", b))
            for b in range(4):
                act.wait_ge(*at("out copied", b))
                act.dma_start(out[0, (b // 2) * C:(b // 2 + 1) * C, 512 * (b % 2):512 * (b % 2) + 512],
                              xk_tok[:, b // 2, 512 * (b % 2):512 * (b % 2) + 512]).then_inc(
                    *mark("out_stored", *(("out stored",) if b == 3 else ()), by=16))

        @block.gpsimd
        def _(pool):
            pool.dma_start(params[:, :], w["parameters"]).then_inc(*mark("constants_landed", by=16))
            pool.dma_start(consts[:, 3 * P:], w["constants"][:, 3 * P:]).then_inc(
                *mark("constants_landed", "constants landed", by=16))
            sync_lora(pool)
            pool_project1(pool)
            sync_mem(pool)
            pool_rwkv_prepare(pool)
            pool_ssd(pool)
            sync_gate(pool)
            pool_bonus(pool)
            for c in range(NC_):
                pool_rwkv_chunk(pool, c)
            pool_ffn(pool)

        @block.tensor
        def _(pe):
            pe_load(pe)
            pe_project1(pe)
            pe_rwkv_turn(pe)
            pe_mem_turn(pe)
            pe_ssd(pe)
            pe_ssd_norm(pe)
            norm_total(pe, "mem", 6, ("k token-major",))
            column_rstd(pe, "mem", 7, ("mem", "root"))
            for c in range(NC_):
                pe_rwkv_chunk(pe, c)
            pe_rwkv_end(pe)
            narrow(pe, "w_out", KT, mix, lambda k: ("mix1", k), None, "out1",
                   lambda b: ("variance root", 1) if b > 1 else ("centred", b))
            norm_total(pe, "post_mix", 0, ("mix1", 7))
            pe_ffn_up(pe)
            narrow(pe, "ffn_w_down", FFT, hid, lambda k: ("hid", k), None, "down1",
                   lambda b: ("pre_ffn", "root") if b == 0 else ("post_mix", "added", 7))
            norm_total(pe, "post_ffn", 0, ("up scaled", FFT - 1))
            pe_project2(pe)
            pe_hgrn(pe)
            pe_hgrn_states(pe)
            pe_rotary(pe)
            pe_hgrn_norm(pe)
            pe_moba_scores(pe)
            pe_moba_turn(pe)
            narrow(pe, "w_out_2", KT, mix, lambda k: ("mix2", k), None, "out2",
                   lambda b: ("o root", b) if b < 2 else ("mix2", 3))
            pe_xattn_q(pe)
            pe_xattn(pe)
            narrow(pe, "w_xo_2", KT, mix, lambda k: ("mix3", k), None, "xo", lambda b: ("mix3", 2 * b))
            pe_mlp(pe)
            narrow(pe, "w_ff2_2", FF2T, hid, lambda k: ("hid2", k), None, "ff2",
                   lambda b: ("norm_mlp", "root") if b == 0 else ("xo", "added", 3))
            pe_final(pe)

        @block.scalar
        def _(act):
            act.wait_ge(*at("constants landed"))
            act.wait_ge(*at("pads"))
            norm_act(act, "pre_mix", h, "pre_mix_norm", lambda m: ("h", m // 2))
            norm_root(act, "pre_mix", 4)
            act_lora(act)
            act_rwkv_prepare(act)
            act_rwkv_exponentials(act)
            act_rwkv_turn_v(act)
            act_ssd_silu(act)
            act_rwkv_turn(act)
            act_mem_norm(act)
            act_ssd(act)
            norm_root(act, "mem", 6)
            act_mem_column(act)
            for c in range(NC_):
                act_rwkv_chunk(act, c)
            act_rwkv_end(act)
            post_norm_act(act, "post_mix", "out1")
            norm_root(act, "post_mix", 0)
            norm_act(act, "pre_ffn", h, "pre_ffn_norm", lambda m: ("post_mix", "added", m))
            norm_root(act, "pre_ffn", 4)
            act_ffn(act)
            post_norm_act(act, "post_ffn", "down1")
            norm_root(act, "post_ffn", 0)
            norm_act(act, "norm_mix", h, "norm_mix_2", lambda m: ("post_ffn", "added", m))
            norm_root(act, "norm_mix", 4)
            act_project2(act)
            act_hgrn(act)
            act_moba_values(act)
            act_hgrn_end(act)
            act_moba(act)
            norm_act(act, "norm_xattn", h, "norm_xattn_2", lambda m: ("out2", "added", m // 2))
            norm_root(act, "norm_xattn", 4)
            act_xattn(act)
            norm_act(act, "norm_mlp", h, "norm_mlp_2", lambda m: ("xo", "added", m // 2))
            norm_root(act, "norm_mlp", 4)
            act_mlp(act)
            norm_act(act, "final", h, "norm_final_2", lambda m: ("ff2", "added", m // 2))
            norm_root(act, "final", 4)
            act_final(act)

        @block.vector
        def _(dve):
            dve_load(dve)
            norm_sum(dve, "pre_mix")
            dve_project1_rwkv(dve)
            dve_rwkv_prepare(dve)
            dve_ssd_conv(dve, 7, 9)
            dve_rwkv_scaled(dve)
            dve_ssd_conv(dve, 9, 13)
            dve_dt(dve)
            norm_sum(dve, "mem")
            dve_ssd(dve)
            norm_reciprocal(dve, "mem")
            dve.wait_ge(*so_far("norm_rstd"))
            dve_bonus(dve)
            for c in range(NC_):
                dve_rwkv_chunk(dve, c)
            dve_rwkv_end(dve)
            norm_sum_post(dve, "post_mix")
            norm_reciprocal(dve, "post_mix")
            post_norm_apply(dve, "post_mix", "out1", "post_mix_norm")
            norm_sum(dve, "pre_ffn")
            dve_ffn(dve)
            norm_sum_post(dve, "post_ffn")
            norm_reciprocal(dve, "post_ffn")
            post_norm_apply(dve, "post_ffn", "down1", "post_ffn_norm")
            norm_sum(dve, "norm_mix")
            dve_project2(dve)
            dve_hgrn(dve)
            dve_rotary(dve)
            dve_hgrn_end(dve)
            dve_moba(dve)
            dve_residual(dve, "out2")
            norm_sum(dve, "norm_xattn")
            dve_xattn_q(dve)
            dve_xattn(dve)
            dve_residual(dve, "xo")
            norm_sum(dve, "norm_mlp")
            dve_mlp(dve)
            dve_residual(dve, "ff2")
            norm_sum(dve, "final")
            dve_final(dve)

    return steps.steps


_WEIGHTS = ["w_in", "w_out", "ffn_w_up", "ffn_w_down", "w_in_2", "w_out_2", "w_xq_2", "w_xk_2", "w_xv_2",
            "w_xo_2", "w_ff1_2", "w_ff2_2"]
_OTHERS = ["x", "mem_2", "rwkv_w2", "rwkv_a2", "rwkv_g2"]


def kernel(**inputs):
    import concourse.bacc as _bacc
    from concourse.bass_utils import run_bass_kernel_spmd as _run

    arrays = {name: np.ascontiguousarray(np.asarray(inputs[name])[0]) for name in _WEIGHTS}
    arrays |= {name: np.ascontiguousarray(inputs[name]) for name in _OTHERS}
    arrays["parameters"] = parameter_table(inputs)
    arrays["constants"] = constant_table()

    def program(known):
        nc = _bacc.Bacc("TRN2", target_bir_lowering=False, num_devices=1)
        w = {name: nc.dram_tensor(f"in_{name}_dram", a.shape, mybir.dt.from_np(a.dtype),
                                  kind="ExternalInput").ap() for name, a in arrays.items()}
        out = nc.dram_tensor("out_0_dram", (1, T, D), F32, kind="ExternalOutput").ap()
        return nc, build(nc, w, out, known)

    _, counted = program(None)
    nc, _ = program(counted)
    r = _run(nc, [{f"in_{name}_dram": a for name, a in arrays.items()}], core_ids=[0])
    return r.results[0]["out_0_dram"]
```

```python
from contextlib import ExitStack

import numpy as np

import concourse.bass as bass
from concourse import mybir

ALU = mybir.AluOpType
ACT = mybir.ActivationFunctionType
AX = mybir.AxisListType
F32 = mybir.dt.float32
F16 = mybir.dt.float16

P = 128
T = 256
D = 1024
KT = D // P
C = 128
NC_ = T // C
EPS = 1e-6

SSD_D, SSD_HEADS, SSD_GROUPS, SSD_STATE, SSD_CONV = 512, 8, 2, 128, 4
SSD_CONV_DIM = SSD_D + 2 * SSD_GROUPS * SSD_STATE
SSD_COLS = SSD_D + SSD_CONV_DIM + SSD_HEADS
RW_D, RW_HEADS, RW_HD = 512, 8, 64
GN_EPS = 64e-5
DECAY_SCALE = float(np.exp(-0.5))
D_FF = 2816
FFT = D_FF // P
HG_D, HG_HEADS, HG_CHUNK = 512, 4, 32
MB_HEADS, MB_HD, ROT, ROPE_THETA = 4, 128, 32, 500000.0
XA_HEADS, XA_HD = 4, 256
D_FF2 = 4096
FF2T = D_FF2 // P

RING = 4
SLOT = 4096
W_SCALE = 64.0


PARAM_TILES = [
    ("pre_mix_norm", KT), ("post_mix_norm", KT), ("pre_ffn_norm", KT), ("post_ffn_norm", KT),
    ("norm_mix_2", KT), ("norm_xattn_2", KT), ("norm_mem_2", KT), ("norm_mlp_2", KT),
    ("norm_final_2", KT),
    ("ssd_conv_w", 4 * 8), ("ssd_conv_b", 8), ("ssd_norm", 4), ("ssd_d", 4),
    ("ssd_dt_bias", 1), ("ssd_a_log", 1),
    ("rwkv_mu", 14), ("rwkv_w0", 4), ("rwkv_a0", 4), ("rwkv_k_k", 4), ("rwkv_k_a", 4),
    ("rwkv_r_k", 4), ("rwkv_ln_w", 4), ("rwkv_ln_b", 4),
    ("ffn_conv_w", 3 * 2 * FFT), ("ffn_conv_b", 2 * FFT),
    ("lb_logits_2", 8), ("hgrn_norm_2", 4),
]
PARAM_AT = {}
_n = 0
for _name, _tiles in PARAM_TILES:
    PARAM_AT[_name] = _n
    _n += _tiles
PARAM_COLS = _n

LEVELS = (2, 4, 8, 16, 32)
CONST_WIDTHS = [
    ("ident", P), ("ones", P), ("head_ones", P),
    ("incl", P), ("strict", P), ("neg_incl", P), ("neg_strict", P),
    ("pair", P), ("pair_t", P),
    ("levels", 64 * len(LEVELS)),
    ("chunk32", P), ("causal", T), ("swap", P), ("cos", T), ("sin", T),
    ("reset128", T), ("reset32", T),
]
CONST_AT = {}
_n = 0
for _name, _w in CONST_WIDTHS:
    CONST_AT[_name] = (_n, _w)
    _n += _w
CONST_COLS = _n


def constant_table():
    out = np.zeros((P, CONST_COLS), np.float32)

    def put(name, value):
        at, w = CONST_AT[name]
        out[:value.shape[0], at:at + w] = value

    r, c = np.arange(P)[:, None], np.arange(P)[None, :]
    put("ident", np.eye(P))
    put("ones", np.ones((P, P)))
    put("head_ones", (r // RW_HD == c // RW_HD) * 1.0)
    put("incl", (r <= c) * 1.0)
    put("strict", (r < c) * 1.0)
    put("neg_incl", (r <= c) * -1.0)
    put("neg_strict", (r < c) * -1.0)
    put("pair", ((r == c + 1) & (r % 2 == 1)) * -1.0)
    put("pair_t", ((c == r + 1) & (c % 2 == 1)) * 1.0)
    levels = []
    for m in LEVELS:
        mask = ((r // (2 * m) == c // (2 * m)) & (r % (2 * m) >= m) & (c % (2 * m) < m)) * 1.0
        levels.append(mask.reshape(P, P // (2 * m), 2, m)[:, :, 0, :].reshape(P, 64))
    put("levels", np.concatenate(levels, axis=1))
    put("chunk32", ((r <= c) & (r // HG_CHUNK == c // HG_CHUNK)) * 1.0)
    q, k = np.arange(P)[:, None], np.arange(T)[None, :]
    put("causal", np.where(k - P <= q, 0.0, -3e38))
    half = ROT // 2
    swap = np.zeros((P, P))
    for i in range(half):
        swap[i + half, i] = 1.0
        swap[i, i + half] = 1.0
    put("swap", swap)
    inv = np.float32(ROPE_THETA) ** (-np.arange(half, dtype=np.float32) * np.float32(2.0) / np.float32(ROT))
    ang = np.arange(T, dtype=np.float32)[:, None] * inv[None, :].astype(np.float32)
    cos, sin = np.cos(ang).T, np.sin(ang).T
    put("cos", np.concatenate([cos, cos]))
    put("sin", np.concatenate([-sin, sin]))
    t = np.arange(T)[None, :].repeat(P, 0)
    put("reset128", (t % C != 0) * 1.0)
    put("reset32", (t % HG_CHUNK != 0) * 1.0)
    return out


def parameter_table(inputs):
    def tiles(a):
        return np.asarray(a).reshape(-1, P).T

    def column(a):
        out = np.zeros((P, 1), np.float32)
        out[:a.shape[0], 0] = a
        return out

    a = {k: np.asarray(v) for k, v in inputs.items()}
    mu = a["rwkv_mu"][0]
    cols = {name: None for name, _ in PARAM_TILES}
    for name in cols:
        if name == "rwkv_mu":
            k0 = RW_D + 64
            al = 3 * RW_D + 64
            order = [mu[k0:k0 + RW_D], mu[RW_D:k0], mu[al:al + 64], mu[al + 64:], mu[:RW_D],
                     mu[k0 + RW_D:k0 + 2 * RW_D]]
            cols[name] = tiles(np.concatenate(order))
        elif name == "ssd_conv_w":
            cols[name] = np.concatenate([tiles(a[name][0, i]) for i in range(4)], axis=1)
        elif name == "ffn_conv_w":
            cols[name] = np.concatenate([tiles(a[name][0, i]) for i in range(3)], axis=1)
        elif name == "lb_logits_2":
            cols[name] = np.concatenate([tiles(a[name][i]) for i in range(2)], axis=1)
        elif name == "ssd_d":
            cols[name] = tiles(np.repeat(a[name][0], SSD_D // SSD_HEADS))
        elif name in ("ssd_dt_bias", "ssd_a_log"):
            cols[name] = column(a[name][0])
        else:
            cols[name] = tiles(a[name].reshape(-1))
        assert cols[name].shape[1] == dict(PARAM_TILES)[name], name
    return np.ascontiguousarray(np.concatenate(list(cols.values()), axis=1))


def weight_stream():
    out = []
    out += [("w_in", "k", 0), ("w_in", "lora", 0), ("w_in", "r", 0), ("w_in", "v", 0),
            ("w_in", "xs", 0), ("w_in", "bc", 0), ("w_in", "z", 0)]
    out += [("w_xk_2", "cols", i) for i in range(2)] + [("w_xv_2", "cols", i) for i in range(2)]
    out += [("w_out", "rows", i) for i in range(2)]
    out += [("ffn_w_up", "pair", i) for i in range(FFT // 2)]
    out += [("ffn_w_down", "rows", i) for i in range((FFT + 3) // 4)]
    out += [("w_in_2", "cols", i) for i in (1, 0, 2, 3, 4, 5, 6)]
    out += [("w_out_2", "rows", i) for i in (1, 0)]
    out += [("w_xq_2", "cols", i) for i in range(2)]
    out += [("w_xo_2", "rows", i) for i in range(2)]
    out += [("w_ff1_2", "cols", i) for i in range(D_FF2 // 512)]
    out += [("w_ff2_2", "rows", i) for i in range(FF2T // 4)]
    return out


STREAM = weight_stream()
CHUNK_NO = {c: n for n, c in enumerate(STREAM)}
SPLIT = [c for c in STREAM if c[:2] in (("w_in", "r"), ("w_in", "v"), ("w_in", "xs")) or c[0] in ("ffn_w_up", "ffn_w_down", "w_in_2", "w_xq_2", "w_xo_2", "w_ff1_2", "w_ff2_2")]
SPLIT_NO = {c: n for n, c in enumerate(SPLIT)}
SPLIT_FROM = {name: min(n for n, c in enumerate(SPLIT) if c[0] == name) for name in {c[0] for c in SPLIT}}
HIGH_END, BELOW = 16384, 12288


def split_address(n):
    name = SPLIT[n][0]
    i = n - SPLIT_FROM[name]
    if name == "w_in":
        return (7184, 11280, 15376)[i]
    if name == "w_in_2":
        return (8192, BELOW, HIGH_END, 9216, HIGH_END, 9216, HIGH_END)[i]
    if name == "w_xo_2":
        return (8192, 4096)[i]
    if name in ("w_xq_2", "w_ff1_2", "w_ff2_2"):
        return (BELOW, HIGH_END)[i % 2]
    return (HIGH_END, BELOW)[(n - SPLIT_FROM["ffn_w_up"]) % 2]


SPLIT_AT = [split_address(n) for n in range(len(SPLIT))]


def split_before(n):
    return max((m for m in range(n) if abs(SPLIT_AT[m] - SPLIT_AT[n]) < SLOT), default=None)


W_IN_COLS = {"z": 0, "xs": SSD_D, "bc": 2 * SSD_D, "dt": SSD_D + SSD_CONV_DIM,
             "r": SSD_COLS, "w_lo": SSD_COLS + RW_D, "k": SSD_COLS + RW_D + 64,
             "v": SSD_COLS + 2 * RW_D + 64, "a_lo": SSD_COLS + 3 * RW_D + 64}


def chunk_pieces(w, chunk):
    name, kind, i = chunk
    if kind == "rows":
        rows = w[name].rearrange("(k p) n -> p k n", p=P)
        k = rows.shape[1]
        return [(j, rows[:, 4 * i + j:4 * i + j + 2, :]) for j in (0, 2) if 4 * i + j < k]
    cols = w[name].rearrange("(k p) n -> p k n", p=P)
    if kind == "cols":
        return [(0, cols[:, :, 512 * i:512 * i + 512])]
    if kind == "pair":
        return [(0, cols[:, :, 256 * i:256 * i + 256]),
                (256, cols[:, :, D_FF + 256 * i:D_FF + 256 * i + 256])]
    if kind == "lora":
        at = W_IN_COLS
        return [(0, cols[:, :, at["w_lo"]:at["w_lo"] + 64]),
                (64, cols[:, :, at["a_lo"]:at["a_lo"] + 192]),
                (256, cols[:, :, at["dt"]:at["dt"] + SSD_HEADS])]
    return [(0, cols[:, :, W_IN_COLS[kind]:W_IN_COLS[kind] + 512])]


class Ledger:

    def __init__(self, known, sem):
        self.known, self.sem, self.count, self.steps = known, sem, {}, {}

    def mark(self, name, *step, by=1):
        self.count[name] = self.count.get(name, 0) + by
        if step:
            assert step not in self.steps, step
            self.steps[step] = (name, self.count[name])
        return self.sem(name), by

    def same(self, step, as_step):
        self.steps[step] = self.steps[as_step]

    def at(self, *step):
        if self.known is None:
            return self.sem("first_pass"), 1
        name, value = self.known[step]
        assert value > 0
        return self.sem(name), value

    def so_far(self, name):
        return self.sem(name), self.count[name]


def build(nc, w, out, known):
    with ExitStack() as ctx:
        sems = {}

        def sem(name):
            if name not in sems:
                sems[name] = ctx.enter_context(nc.semaphore(name))
            return sems[name]

        steps = Ledger(known, sem)
        mark, at, same, so_far = steps.mark, steps.at, steps.same, steps.so_far

        def sb(name, *dims):
            return ctx.enter_context(nc.sbuf_tensor(name, [P, *dims], F32))

        banks = [ctx.enter_context(nc.psum_tensor(f"bank{i}", [P, 512], F32)) for i in range(8)]

        def halves(b):
            return banks[b][:, :].rearrange("p (i t) -> p i t", i=2)

        def quarters(b):
            return banks[b][:, :].rearrange("p (i t) -> p i t", i=4)

        consts = sb("consts", CONST_COLS)
        params = sb("params", PARAM_COLS)
        ring = sb("ring", RING, SLOT)
        h = sb("h", KT, T)
        hg = sb("hg", KT, T)
        mix = sb("mix", KT, T)
        xk = sb("xk", KT, T)
        xv = sb("xv", NC_, D)
        sqs = sb("sqs", 2, 512)
        ssum = sb("ssum", 512)
        rms = sb("rms", T)
        rstd = sb("rstd", T)
        rcol = sb("rcol", NC_)
        eps = sb("eps", 4)
        ARENA = 20480
        arena = sb("arena", ARENA)

        def const(name):
            a, n = CONST_AT[name]
            return consts[:, a:a + n]

        def par(name, i):
            a = PARAM_AT[name] + i
            return params[:, a:a + 1]

        def view(a, *dims):
            n = int(np.prod(dims))
            assert a + n <= ARENA, (a, dims)
            v = arena[:, a:a + n]
            if len(dims) == 2:
                v = v.rearrange("p (a b) -> p a b", a=dims[0])
            elif len(dims) == 3:
                v = v.rearrange("p (a b c) -> p a b c", a=dims[0], b=dims[1])
            return v

        ident, ones, head_ones = const("ident"), const("ones"), const("head_ones")

        def over(ap, n):
            return ap.unsqueeze(1).broadcast_to([ap.shape[0], n, ap.shape[1]])

        def along(ap, n):
            return ap.unsqueeze(2).broadcast_to([ap.shape[0], ap.shape[1], n])

        raw = view(0, 14, T + 1)
        shf = view(3600, 14, T)
        K_, R_, V_ = shf[:, 0:4, :], shf[:, 6:10, :], shf[:, 10:14, :]
        WA, GLO = shf[:, 4, :], shf[:, 5, :]
        SW, CS, E0 = view(0, 4, T), view(1024, 4, T), view(2048, 4, T)
        A_, KK, E1, E2, BT = (view(7184 + 1024 * i, 4, T) for i in range(5))
        KSQ = mix[:, 0:4, :]
        VTOK = view(0, NC_, RW_D)
        KTOK, BTOK = view(1024, RW_D), view(1536, RW_D)
        P64 = [view(3072 + 256 * i, 4, 64) for i in range(2)]
        SOLVE = 7184 + 5 * 1024
        Y, BONUS = KK, R_
        small = sb("small", 64)
        s0c = view(SOLVE + 7168, 4, 64)
        lora_w = view(SOLVE + 7424, RW_D)
        gate_w = ssum

        def solve_set(i):
            a = SOLVE + 3584 * i
            q = [view(a + 512 * n, 4, C) for n in range(6)]

            def grown(m):
                both = arena[:, a + 512:a + 512 + 2 * (512 + m)].rearrange("p (w x) -> p w x", w=2)
                return both[:, :, 0:512].rearrange("p w (jb two m) -> p w jb two m", two=2, m=m)[:, :, :, 0, :]

            return dict(LT=q[0], X=q[1], XT=q[2], PA=q[3], PB=q[4], ARB=q[5], XX=view(a + 512, 8, C), grown=grown,
                        G=view(a + 3072, 4, 64), U=view(a + 3328, 4, 64))

        sets = [solve_set(0), solve_set(1)]
        rawx = view(SOLVE, 8, T + 3)
        xbc = view(SOLVE + 2080, 8, T)
        EX = [view(SOLVE + 2080 + 512 * i, 4, C) for i in range(2)]
        MT = [view(SOLVE + 3104 + 512 * i, 4, C) for i in range(2)]
        zs = view(SOLVE + 4128, 4, T)
        BTOKS = view(SOLVE + 5152, 2, SSD_STATE)
        dtT, aT, dtmp = view(SOLVE + 7168, T), view(SOLVE + 5664, T), view(SOLVE + 5920, T)
        dtok = view(SOLVE + 6176, NC_, 8)
        atok = view(SOLVE + 6192, NC_, 8)
        cstok = view(SOLVE + 6208, NC_, 8)
        dect = view(SOLVE + 6224, 8)
        acol = view(SOLVE + 6232, 2)
        GT = A_[:, 0:2, :].rearrange("p a (b t) -> p (a b) t", t=C)
        CEX = mix[:, 4:8, :].rearrange("p a (b t) -> p (a b) t", t=C)
        YS = mix[:, 0:4, :]
        XDT = xv[:, 0, :].rearrange("p (c d) -> p c d", c=NC_)
        XDEC, ST = xv[:, 1, 0:SSD_D], xv[:, 1, SSD_D:2 * SSD_D]

        block = ctx.enter_context(nc.Block())

        def slot(name, kind, i=0):
            n = CHUNK_NO[(name, kind, i)]
            s = ring[:, n % RING, :]
            if kind == "rows":
                return s.rearrange("p (k n) -> p k n", k=4)
            if kind == "lora":
                return s[:, 0:8 * 264].rearrange("p (k n) -> p k n", k=KT)
            return s.rearrange("p (k n) -> p k n", k=KT)

        @block.sync
        def _(sp):
            sp.dma_start(consts[:, 0:3 * P], w["constants"][:, 0:3 * P]).then_inc(
                *mark("identity_landed", "identity landed", by=16))
            sp.dma_start(mix[:, :, :].rearrange("p a b -> p (a b)").rearrange("p (c d) -> p c d", c=2),
                         w["x"][0].rearrange("(c p) d -> p c d", p=P)).then_inc(*mark("x_landed", "x landed", by=16))
            for n, chunk in enumerate(STREAM):
                if n >= RING:
                    sp.wait_ge(*at("chunk used", n - RING))
                name, kind, i = chunk
                view_ = slot(name, kind, i)
                pieces = chunk_pieces(w, chunk)
                for j, (a, src) in enumerate(pieces):
                    dst = view_[:, a:a + src.shape[1], :] if kind == "rows" else view_[:, :, a:a + src.shape[2]]
                    last = j == len(pieces) - 1
                    sp.dma_start(dst, src).then_inc(
                        *mark(f"weights_landed_{n % RING}", *(("chunk", n) if last else ()), by=16))
            sp.wait_ge(*at("out stored"))

        def chunk_ready(pe, name, kind, i=0):
            pe.wait_ge(*at("chunk", CHUNK_NO[(name, kind, i)]))

        def chunk_used(name, kind, i, step):
            same(("chunk used", CHUNK_NO[(name, kind, i)]), step)

        def split_view(v):
            return v.bitcast(F16).rearrange("p (w x) -> p w x", w=2)

        hg16 = hg[:, :, :].rearrange("p k t -> p (k t)").bitcast(F16).rearrange("p (k w t) -> p k w t", k=KT, w=2)

        def halves_of(chunk):
            v = split_view(view(SPLIT_AT[SPLIT_NO[chunk]], SLOT))
            k = 4 if chunk[1] == "rows" else KT
            return [v[:, w_, :].rearrange("p (k n) -> p k n", k=k) for w_ in range(2)]

        def quarter(v, chunk, q):
            return v[:, q, :] if chunk[1] == "rows" else v[:, :, q * P:(q + 1) * P]

        def rows_of(chunk):
            return min(4, {"ffn_w_down": FFT, "w_xo_2": KT, "w_ff2_2": FF2T}[chunk[0]] - 4 * chunk[2]) if \
                chunk[1] == "rows" else 4

        def split_high(act, n, qs):
            chunk = SPLIT[n]
            for q in qs:
                if q >= rows_of(chunk):
                    continue
                if q == 0:
                    act.wait_ge(*at("chunk", CHUNK_NO[chunk]))
                    if split_before(n) is not None:
                        act.wait_ge(*at("split used", split_before(n)))
                nc.scalar.activation(quarter(halves_of(chunk)[0], chunk, q), quarter(slot(*chunk), chunk, q), ACT.Copy,
                                     scale=W_SCALE).then_inc(*mark("weights_high", "high", n, q))

        def split_low(dve, n, qs):
            chunk = SPLIT[n]
            for q in qs:
                if q >= rows_of(chunk):
                    continue
                dve.wait_ge(*at("high", n, q))
                nc.vector.scalar_tensor_tensor(quarter(halves_of(chunk)[1], chunk, q), quarter(slot(*chunk), chunk, q),
                                               W_SCALE, quarter(halves_of(chunk)[0], chunk, q), ALU.mult,
                                               ALU.subtract).then_inc(*mark("weights_low", "low", n, q))
                if q == rows_of(chunk) - 1:
                    chunk_used(*chunk, ("low", n, q))

        def split_used(chunk, step):
            same(("split used", SPLIT_NO[chunk]), step)

        def product3(out_, weight, k, cols, src, first, last):
            for i, (a, b) in enumerate(((0, 0), (1, 0), (0, 1))):
                mm = nc.tensor.matmul(out_, weight[a][:, k, cols], src[:, k, b, :], start=(first and i == 0),
                                      stop=(last and i == 2), skip_group_check=True)
            return mm

        mix16 = mix[:, :, :].rearrange("p k t -> p (k t)").bitcast(F16).rearrange("p (k w t) -> p k w t", k=KT, w=2)

        def norm_act(act, n, src, gain, ready, split=False):
            for m in range(KT):
                act.wait_ge(*at(*ready(m)))
                nc.scalar.activation(hg16[:, m, 0, :] if split else hg[:, m, :], src[:, m, :], ACT.Copy,
                                     scale=par(gain, m)).then_inc(*mark("norm_gained", n, "gained", m))
                if m >= 4:
                    act.wait_ge(*at(n, "summed", m // 2 - 2))
                nc.scalar.activation(sqs[:, m // 2 % 2, 256 * (m % 2):256 * (m % 2) + 256], src[:, m, :],
                                     ACT.Square).then_inc(*mark("norm_squares", n, "squares", m))

        def norm_low(dve, n, b, gain):
            for m in (2 * b, 2 * b + 1):
                dve.wait_ge(*at(n, "gained", m))
                nc.vector.scalar_tensor_tensor(hg16[:, m, 1, :], h[:, m, :], par(gain, m), hg16[:, m, 0, :],
                                               ALU.mult, ALU.subtract).then_inc(*mark("norm_low", n, "low", m))

        def norm_part(eng, ops, n, b):
            eng.wait_ge(*at(n, "squares", 2 * b + 1))
            if b == 0:
                ops.tensor_copy(ssum[:, :], sqs[:, 0, :]).then_inc(*mark("norm_summed" if ops is nc.vector else "norm_summed_by_gpsimd", n, "summed", 0))
            else:
                eng.wait_ge(*at(n, "summed", b - 1))
                ops.tensor_tensor(ssum[:, :], ssum[:, :], sqs[:, b % 2, :], ALU.add).then_inc(
                    *mark("norm_summed" if ops is nc.vector else "norm_summed_by_gpsimd", n, "summed", b))

        def pool_norm_sum(pool, n):
            for b in range(4):
                norm_part(pool, nc.gpsimd, n, b)

        def norm_sum(dve, n):
            for b in range(4):
                norm_part(dve, nc.vector, n, b)

        def norm_total(pe, n, bank, free):
            if free:
                pe.wait_ge(*at(*free))
            pe.wait_ge(*at(n, "summed", 3))
            for i in range(2):
                mm = nc.tensor.matmul(banks[bank][:, 0:T], ones, ssum[:, 256 * i:256 * i + 256],
                                      start=(i == 0), stop=(i == 1))
            mm.then_inc(*mark("norm_total", n, "total"))

        def norm_root(act, n, bank, scale=1.0 / D, eps_column=0):
            act.wait_ge(*at(n, "total"))
            nc.scalar.activation(rms[:, :], banks[bank][:, 0:T], ACT.Sqrt, bias=eps[:, eps_column:eps_column + 1],
                                 scale=scale).then_inc(*mark("norm_root", n, "root"))

        def norm_reciprocal(dve, n):
            dve.wait_ge(*at(n, "root"))
            nc.vector.reciprocal(rstd[:, :], rms[:, :]).then_inc(*mark("norm_rstd", n, "rstd"))

        def column_rstd(pe, n, bank, free):
            pe.wait_ge(*at(n, "rstd"))
            pe.wait_ge(*at(*free))
            for c in range(NC_):
                mm = nc.tensor.matmul(banks[bank][:, c:c + 1], rstd[:, c * C:(c + 1) * C], ident[:, 0:1],
                                      start=True, stop=True)
            mm.then_inc(*mark("column_rstd", n, "column"))

        def wide(pe, chunk, j, bank, half):
            if chunk in SPLIT_NO:
                pe.wait_ge(*at("low", SPLIT_NO[chunk], j))
                for k in range(KT):
                    mm = product3(halves(bank)[:, half, :], halves_of(chunk), k, slice(j * P, (j + 1) * P), hg16,
                                  k == 0, k == KT - 1)
                return mm
            s = slot(*chunk)
            for k in range(KT):
                mm = nc.tensor.matmul(halves(bank)[:, half, :], s[:, k, j * P:(j + 1) * P],
                                      hg[:, k, :], start=(k == 0), stop=(k == KT - 1))
            return mm

        def narrow(pe, name, ktiles, src, src_ready, label, free, order=None):
            order = order or range((ktiles + 3) // 4)
            split = (name, "rows", 0) in SPLIT_NO
            for b in range(4):
                if free:
                    pe.wait_ge(*at(*free(b)))

            def product(i, kk, m):
                k = 4 * i + kk
                out_, cols = halves(4 + m // 2)[:, m % 2, :], slice(m * P, (m + 1) * P)
                first = i == order[0] and kk == 0 and m % 2 == 0
                last = i == order[-1] and kk == min(4, ktiles - 4 * i) - 1
                if not split:
                    return nc.tensor.matmul(out_, slot(name, "rows", i)[:, kk, cols], src[:, k, :], start=first,
                                            stop=last, skip_group_check=True)
                for n, (a, b) in enumerate(((0, 0), (1, 0), (0, 1))):
                    mm = nc.tensor.matmul(out_, halves_of((name, "rows", i))[a][:, kk, cols], src[:, k, b, :],
                                          start=(first and n == 0), stop=(last and n == 2), skip_group_check=True)
                return mm

            for i in order:
                if not split:
                    chunk_ready(pe, name, "rows", i)
                n = min(4, ktiles - 4 * i)
                tail = i == order[-1]
                by_rows = n - 2 if tail else n
                for kk in range(n):
                    pe.wait_ge(*at(*src_ready(4 * i + kk)))
                    if split:
                        pe.wait_ge(*at("low", SPLIT_NO[(name, "rows", i)], kk))
                    if kk < by_rows:
                        for m in range(KT):
                            mm = product(i, kk, m)
                used = (label, "bank", 3)
                if not tail:
                    mm.then_inc(*mark("rows_used", label, "rows", i))
                    used = (label, "rows", i)
                else:
                    for m in range(KT):
                        for kk in range(by_rows, n):
                            mm = product(i, kk, m)
                        if m % 2:
                            mm.then_inc(*mark("projected_out", label, "bank", m // 2))
                if split:
                    split_used((name, "rows", i), used)
                else:
                    chunk_used(name, "rows", i, used)

        scaled_f = view(0, 2, 512)

        def post_norm_act(act, n, label):
            for b in range(4):
                act.wait_ge(*at(label, "bank", b))
                if b >= 2:
                    act.wait_ge(*at(n, "summed", b - 2))
                nc.scalar.activation(sqs[:, b % 2, :], banks[4 + b][:, :], ACT.Square).then_inc(
                    *mark("norm_squares", n, "squares", 2 * b + 1))

        def post_norm_apply(dve, n, label, gain, following, following_gain):
            dve.wait_ge(*at(n, "rstd"))
            for b in range(4):
                for m in (2 * b, 2 * b + 1):
                    nc.vector.scalar_tensor_tensor(scaled_f[:, b % 2, 256 * (m % 2):256 * (m % 2) + 256],
                                                   halves(4 + b)[:, m % 2, :], par(gain, m), rstd[:, :],
                                                   ALU.mult, ALU.mult).then_inc(*mark("post_scaled", n, "scaled", m))
                for m in (2 * b, 2 * b + 1):
                    dve.wait_ge(*at(n, "scaled", m))
                    nc.vector.tensor_tensor(h[:, m, :], h[:, m, :],
                                            scaled_f[:, b % 2, 256 * (m % 2):256 * (m % 2) + 256],
                                            ALU.add).then_inc(*mark("residual", n, "added", m))
                norm_low(dve, following, b, following_gain)

        PROJ = [("k", 4), ("lora", 2), ("r", 4), ("v", 4), ("xs", 4), ("bc", 4), ("z", 4)]
        TILE_OF = [(kind, j) for kind, n in PROJ for j in range(n)]
        PBANKS = len(TILE_OF) // 2

        def pe_load(pe):
            pe.wait_ge(*at("x landed"))
            pe.wait_ge(*at("identity landed"))
            xt = mix[:, :, :].rearrange("p a b -> p (a b)").rearrange("p (c d) -> p c d", c=2)
            for b in range(4):
                for m in (2 * b, 2 * b + 1):
                    for c in range(NC_):
                        mm = nc.tensor.transpose(halves(4 + b)[:, m % 2, c * C:(c + 1) * C],
                                                 xt[:, c, m * P:(m + 1) * P], ident)
                mm.then_inc(*mark("x_turned", "x turned", b))

        def dve_load(dve):
            for b in range(4):
                dve.wait_ge(*at("x turned", b))
                nc.vector.tensor_copy(h[:, 2 * b:2 * b + 2, :], halves(4 + b)).then_inc(*mark("h_written", "h", b))

        def pe_project1(pe):
            for i, (kind, j) in enumerate(TILE_OF):
                b = i // 2
                if j == 0 and ("w_in", kind, 0) not in SPLIT_NO:
                    chunk_ready(pe, "w_in", kind)
                if i % 2 == 0 and b >= 4:
                    pe.wait_ge(*at("proj1 out", b - 4))
                if ("w_in", kind, 0) in SPLIT_NO:
                    pe.wait_ge(*at("low", SPLIT_NO[("w_in", kind, 0)], j))
                    pe.wait_ge(*at("pre_mix", "low", KT - 1))
                for k in range(KT):
                    if i == 0:
                        pe.wait_ge(*at("pre_mix", "gained", k))
                    if ("w_in", kind, 0) in SPLIT_NO:
                        mm = product3(halves(b % 4)[:, i % 2, :], halves_of(("w_in", kind, 0)), k,
                                      slice(j * P, (j + 1) * P), pre16, k == 0, k == KT - 1)
                        continue
                    mm = nc.tensor.matmul(halves(b % 4)[:, i % 2, :], slot("w_in", kind)[:, k, j * P:(j + 1) * P],
                                          hg[:, k, :], start=(k == 0), stop=(k == KT - 1))
                if i % 2:
                    mm.then_inc(*mark("proj1", "proj1", b))
                if i == 0:
                    norm_total(pe, "pre_mix", 4, ("h", 3))
                if i == 7:
                    pe_mem_turn(pe, (0, 1))
                if i == 9:
                    pe_mem_turn(pe, (2, 3))
                if i == 15:
                    pe_lora(pe)
                if i == 19:
                    pe_head_norm(pe)
                if i == 21:
                    pe_rwkv_turn_v(pe)
                if kind == "lora" and j == 1:
                    for k in range(KT):
                        mm = nc.tensor.matmul(banks[5][0:SSD_HEADS, 0:T], slot("w_in", "lora")[:, k, 256:264],
                                              hg[:, k, :], start=(k == 0), stop=(k == KT - 1))
                    mm.then_inc(*mark("proj1_dt", "proj1 dt"))
                    chunk_used("w_in", "lora", 0, ("proj1 dt",))
                elif j == dict(PROJ)[kind] - 1:
                    if ("w_in", kind, 0) in SPLIT_NO:
                        split_used(("w_in", kind, 0), ("proj1", b))
                    else:
                        chunk_used("w_in", kind, 0, ("proj1", b))

        pre16 = xv[:, :, :].rearrange("p c d -> p (c d)").bitcast(F16).rearrange("p (k w t) -> p k w t", k=KT, w=2)

        def act_pre_high(act):
            for m in range(KT):
                nc.scalar.activation(pre16[:, m, 0, :], h[:, m, :], ACT.Copy, scale=par("pre_mix_norm", m)).then_inc(
                    *mark("pre_high", "pre_mix", "high", m))

        def dve_pre_low(dve):
            for m in range(KT):
                dve.wait_ge(*at("pre_mix", "high", m))
                nc.vector.scalar_tensor_tensor(pre16[:, m, 1, :], h[:, m, :], par("pre_mix_norm", m), pre16[:, m, 0, :],
                                               ALU.mult, ALU.subtract).then_inc(*mark("pre_low", "pre_mix", "low", m))

        def evacuate1(dst, b):
            if ("w_in", TILE_OF[2 * b][0], 0) in SPLIT_NO:
                return nc.vector.scalar_tensor_tensor(dst, halves(b % 4), 1.0 / W_SCALE, over(rstd[:, :], 2), ALU.mult,
                                                      ALU.mult)
            return nc.vector.tensor_tensor(dst, halves(b % 4), over(rstd[:, :], 2), ALU.mult)

        def dve_project1_rwkv(dve):
            norm_reciprocal(dve, "pre_mix")
            dve.wait_ge(*so_far("norm_rstd"))
            for b in range(7):
                dve.wait_ge(*at("proj1", b))
                if b == 0:
                    dve.wait_ge(*at("pads"))
                evacuate1(raw[:, 2 * b:2 * b + 2, 1:T + 1], b).then_inc(*mark("proj1_scaled", "proj1 out", b))
                if b == 0:
                    dve_pre_low(dve)
                if b == 3:
                    dve_mem_norm(dve)
                if b in (0, 2, 4):
                    split_low(dve, b // 2, range(4))
                if b == 2:
                    dve.wait_ge(*at("proj1 dt"))
                    nc.vector.tensor_tensor(dtT[0:8, :], banks[5][0:8, 0:T], rstd[0:8, :], ALU.mult).then_inc(
                        *mark("dt_raw", "dt raw"))
            for b in range(7):
                dve.wait_ge(*at("shift difference", b))
                for i in (2 * b, 2 * b + 1):
                    nc.vector.scalar_tensor_tensor(shf[:, i, :], shf[:, i, :], par("rwkv_mu", i),
                                                   raw[:, i, 1:T + 1], ALU.mult, ALU.add).then_inc(
                        *mark("shifted", "shifted", i))

        def pool_project1(pool):
            nc.gpsimd.memset(raw[:, :, 0:1], 0.0)
            nc.gpsimd.memset(eps[:, 0:1], EPS)
            nc.gpsimd.memset(eps[:, 1:2], GN_EPS)
            nc.gpsimd.memset(eps[:, 2:3], 1.0)
            nc.gpsimd.memset(eps[:, 3:4], EPS * W_SCALE ** 2).then_inc(*mark("pads", "pads"))
            for b in range(7):
                pool.wait_ge(*at("proj1 out", b))
                nc.gpsimd.tensor_tensor(shf[:, 2 * b:2 * b + 2, :], raw[:, 2 * b:2 * b + 2, 0:T],
                                        raw[:, 2 * b:2 * b + 2, 1:T + 1], ALU.subtract).then_inc(
                    *mark("shift_difference", "shift difference", b))
            pool.wait_ge(*at("proj1", 6))
            nc.gpsimd.memset(rawx[:, :, 0:3], 0.0).then_inc(*mark("rawx_pads", "rawx pads"))

        def dve_ssd_conv(dve, first, last):
            for b in range(first, last):
                dve.wait_ge(*at("proj1", b))
                if b < 11:
                    n = b - 7
                    dve.wait_ge(*at("rawx pads"))
                    evacuate1(rawx[:, 2 * n:2 * n + 2, 3:T + 3], b).then_inc(*mark("proj1_scaled", "proj1 out", b))
                    dve.wait_ge(*so_far("proj1_scaled"))
                    for i in (2 * n, 2 * n + 1):
                        nc.vector.tensor_scalar(xbc[:, i, :], rawx[:, i, 3:T + 3], par("ssd_conv_w", 24 + i),
                                                par("ssd_conv_b", i), ALU.mult, ALU.add).then_inc(*mark("ssd_conv"))
                    for tap in (2, 1, 0):
                        dve.wait_ge(*so_far("ssd_conv"))
                        for i in (2 * n, 2 * n + 1):
                            nc.vector.scalar_tensor_tensor(xbc[:, i, :], rawx[:, i, tap:tap + T],
                                                           par("ssd_conv_w", 8 * tap + i), xbc[:, i, :],
                                                           ALU.mult, ALU.add).then_inc(
                                *mark("ssd_conv", "ssd conv", tap, i))
                else:
                    n = b - 11
                    nc.vector.tensor_tensor(zs[:, 2 * n:2 * n + 2, :], halves(b % 4), over(rstd[:, :], 2),
                                            ALU.mult).then_inc(*mark("proj1_scaled", "proj1 out", b))

        def act_ssd_silu(act):
            act.wait_ge(*at("dt raw"))
            nc.scalar.activation(dtT[0:8, :], dtT[0:8, :], ACT.Identity, bias=par("ssd_dt_bias", 0)[0:8, :]).then_inc(
                *mark("dt_act", "dt biased"))
            act.wait_ge(*so_far("dt_act"))
            nc.scalar.activation(dtmp[0:8, :], dtT[0:8, :], ACT.Abs).then_inc(*mark("dt_act"))
            nc.scalar.preload_act_table_set("natural_log_exp_and_others")
            nc.scalar.activation(acol[0:8, 0:1], par("ssd_a_log", 0)[0:8, :], ACT.Exp).then_inc(*mark("dt_act"))
            act.wait_ge(*so_far("dt_act"))
            nc.scalar.activation(dtmp[0:8, :], dtmp[0:8, :], ACT.Exp, scale=-1.0).then_inc(*mark("dt_act", "dt exp"))
            act.wait_ge(*at("dt one plus"))
            nc.scalar.activation(rms[0:8, :], aT[0:8, :], ACT.Ln).then_inc(*mark("dt_act", "dt log"))
            for i in range(8):
                act.wait_ge(*at("ssd conv", 0, i))
                nc.scalar.activation(rawx[:, i, 3:T + 3], xbc[:, i, :], ACT.Silu).then_inc(
                    *mark("ssd_silu", "ssd silu", i))

        def act_z_silu(act):
            for n in range(2):
                act.wait_ge(*at("proj1 out", 11 + n))
                nc.scalar.activation(zs[:, 2 * n:2 * n + 2, :], zs[:, 2 * n:2 * n + 2, :], ACT.Silu).then_inc(
                    *mark("z_silu", "z silu", n))

        def dve_dt(dve):
            dve.wait_ge(*at("dt exp"))
            nc.vector.tensor_scalar(aT[0:8, :], dtmp[0:8, :], 1.0, None, ALU.add).then_inc(
                *mark("dt_vector", "dt one plus"))
            dve.wait_ge(*so_far("dt_vector"))
            nc.vector.scalar_tensor_tensor(dtmp[0:8, :], aT[0:8, :], -1.0, dtmp[0:8, :], ALU.add,
                                           ALU.subtract).then_inc(*mark("dt_vector"))
            dve.wait_ge(*so_far("dt_vector"))
            nc.vector.scalar_tensor_tensor(dtT[0:8, :], dtT[0:8, :], 0.0, dtmp[0:8, :], ALU.max,
                                           ALU.subtract).then_inc(*mark("dt_vector"))
            dve.wait_ge(*so_far("dt_vector"))
            dve.wait_ge(*at("dt log"))
            nc.vector.tensor_tensor(dtT[0:8, :], dtT[0:8, :], rms[0:8, :], ALU.add).then_inc(*mark("dt_vector"))
            dve.wait_ge(*so_far("dt_vector"))
            nc.vector.tensor_scalar(aT[0:8, :], dtT[0:8, :], acol[0:8, 0:1], -1.0, ALU.mult, ALU.mult).then_inc(
                *mark("dt_vector", "dt done"))

        XS = lambda i: rawx[:, i, 3:T + 3]

        def pe_ssd(pe):
            pe.wait_ge(*at("mem", "low", 7))
            pe.wait_ge(*at("k token-major"))
            pe.wait_ge(*at("dt done"))
            for c in range(NC_):
                nc.tensor.transpose(banks[4][:, 8 * c:8 * c + 8], dtT[0:8, c * C:(c + 1) * C], ident[0:8, 0:8])
                mm = nc.tensor.transpose(banks[4][:, 16 + 8 * c:24 + 8 * c], aT[0:8, c * C:(c + 1) * C],
                                         ident[0:8, 0:8])
            mm.then_inc(*mark("ssd_pe", "ssd dt turned"))
            for c in range(NC_):
                for i in range(4):
                    if c == 0:
                        pe.wait_ge(*at("ssd silu", i))
                    mm = nc.tensor.transpose(quarters(5 + c)[:, i, :], XS(i)[:, c * C:(c + 1) * C], ident)
                mm.then_inc(*mark("ssd_pe", "ssd x turned", c))
            for g in range(2):
                pe.wait_ge(*at("ssd silu", 4 + g))
                mm = nc.tensor.transpose(quarters(7)[:, g, :], XS(4 + g)[:, 0:C], ident)
            mm.then_inc(*mark("ssd_pe", "ssd b turned"))
            pe.wait_ge(*at("ssd dt token-major"))
            for c in range(NC_):
                mm = nc.tensor.matmul(banks[4][:, 32 + 8 * c:40 + 8 * c], const("incl"), atok[:, c, :],
                                      start=True, stop=True)
            mm.then_inc(*mark("ssd_pe", "ssd cumulative"))
            pe.wait_ge(*at("mem", "root"))
            for g in range(2):
                pe.wait_ge(*at("ssd silu", 6 + g))
                for c in range(NC_):
                    mm = nc.tensor.matmul(quarters(0)[:, 2 * g + c, :], XS(4 + g)[:, c * C:(c + 1) * C],
                                          XS(6 + g)[:, c * C:(c + 1) * C], start=True, stop=True)
            mm.then_inc(*mark("ssd_pe", "ssd bc"))
            for c in range(NC_):
                for g in range(2):
                    b = (1, 2, 3, 7)[2 * c + g]
                    if b == 7:
                        pe.wait_ge(*at("ssd b token-major"))
                    for i in range(4):
                        mm = nc.tensor.matmul(quarters(b)[:, i, :],
                                              atok[:, c, 4 * g + i:4 * g + i + 1].broadcast_to([P, P]),
                                              const("incl"), start=True, stop=True)
                    mm.then_inc(*mark("ssd_pe", "ssd sums", c, g))
            pe.wait_ge(*at("ssd decayed"))
            pe.wait_ge(*at("ssd cumulative column"))
            for g in range(2):
                mm = nc.tensor.matmul(banks[4][:, 256 * g:256 * g + 256], BTOKS[:, g, :],
                                      XDEC[:, 256 * g:256 * g + 256], start=True, stop=True)
            mm.then_inc(*mark("ssd_pe", "ssd state"))
            for c in range(NC_):
                for g in range(2):
                    pe.wait_ge(*at("ssd mt", c, g))
                    if c == 1:
                        pe.wait_ge(*at("ssd cex", g))
                        pe.wait_ge(*at("ssd state out"))
                    elif g == 0:
                        pe.wait_ge(*at("ssd x token-major", 1))
                    for i in range(4):
                        hd = 4 * g + i
                        o = halves(5 + g)[64 * (hd % 2):64 * (hd % 2) + 64, (hd // 2) % 2, c * C:(c + 1) * C]
                        mm = nc.tensor.matmul(o, XDT[:, c, 64 * hd:64 * hd + 64], MT[g][:, i, :],
                                              start=True, stop=(c == 0), skip_group_check=True)
                        if c == 1:
                            mm = nc.tensor.matmul(o, ST[:, 64 * hd:64 * hd + 64], CEX[:, hd, :],
                                                  start=False, stop=True, skip_group_check=True)
                    mm.then_inc(*mark("ssd_pe", "ssd y", c, g))

        def dve_ssd(dve):
            dve.wait_ge(*at("ssd dt turned"))
            nc.vector.tensor_copy(view(SOLVE + 6176, 32), banks[4][:, 0:32]).then_inc(
                *mark("ssd_vector", "ssd dt token-major"))
            dve.wait_ge(*so_far("ssd_vector"))
            for c in range(NC_):
                dve.wait_ge(*at("ssd x turned", c))
                nc.vector.tensor_tensor(XDT[:, c, :].rearrange("p (h d) -> p h d", h=8),
                                        banks[5 + c][:, :].rearrange("p (h d) -> p h d", h=8),
                                        along(dtok[:, c, :], 64), ALU.mult).then_inc(
                    *mark("ssd_vector", "ssd x token-major", c))
            dve.wait_ge(*at("ssd b turned"))
            nc.vector.tensor_copy(BTOKS, quarters(7)[:, 0:2, :]).then_inc(*mark("ssd_vector", "ssd b token-major"))
            mem_low(dve, 0)
            dve.wait_ge(*at("ssd cumulative"))
            nc.vector.tensor_copy(cstok.rearrange("p c h -> p (c h)"), banks[4][:, 32:48]).then_inc(
                *mark("ssd_vector", "ssd cumulative column"))
            dve.wait_ge(*at("ssd bc"))
            nc.vector.tensor_tensor(GT, quarters(0), over(const("incl"), 4), ALU.mult).then_inc(*mark("ssd_vector"))
            for c in range(NC_):
                for g in range(2):
                    b = (1, 2, 3, 7)[2 * c + g]
                    dve.wait_ge(*at("ssd sums", c, g))
                    dve.wait_ge(*so_far("ssd_vector"))
                    if c == 0:
                        nc.vector.tensor_tensor(dect[:, 4 * g:4 * g + 4], quarters(b)[:, :, C - 1],
                                                cstok[:, 0, 4 * g:4 * g + 4], ALU.subtract).then_inc(
                            *mark("ssd_vector", "ssd decay exponent", g))
                    else:
                        dve.wait_ge(*at("ssd cexp", g))
                        dve.wait_ge(*at("ssd cex", g))
                    if c == 0 and g == 0:
                        dve.wait_ge(*at("ssd silu", 7))
                    for i in range(4):
                        hd = 4 * g + i
                        nc.vector.tensor_scalar(EX[g][:, i, :], quarters(b)[:, i, :], cstok[:, c, hd:hd + 1], 0.0,
                                                ALU.subtract, ALU.min).then_inc(
                            *mark("ssd_vector", "ssd exponent", c, g, i))
                    if c == 0 and g == 1:
                        dve.wait_ge(*at("ssd decay"))
                        nc.vector.tensor_tensor(XDEC.rearrange("p (h d) -> p h d", h=8),
                                                XDT[:, 0, :].rearrange("p (h d) -> p h d", h=8),
                                                along(dect, 64), ALU.mult).then_inc(*mark("ssd_vector", "ssd decayed"))
                    if c == 0 and g == 1:
                        for gg in range(2):
                            dve.wait_ge(*at("ssd decays", 0, gg))
                            nc.vector.tensor_tensor(MT[gg], EX[gg], over(GT[:, 2 * gg, :], 4), ALU.mult).then_inc(
                                *mark("ssd_vector", "ssd mt", 0, gg))
            dve.wait_ge(*at("ssd state"))
            nc.vector.tensor_copy(ST, banks[4][:, :]).then_inc(*mark("ssd_vector", "ssd state out"))
            for gg in range(2):
                dve.wait_ge(*at("ssd decays", 1, gg))
                dve.wait_ge(*at("ssd y", 0, gg))
                nc.vector.tensor_tensor(MT[gg], EX[gg], over(GT[:, 2 * gg + 1, :], 4), ALU.mult).then_inc(
                    *mark("ssd_vector", "ssd mt", 1, gg))
            for g in range(2):
                dve.wait_ge(*at("ssd y", 1, g))
                for j in range(2):
                    i = 2 * g + j
                    nc.vector.scalar_tensor_tensor(YS[:, i, :], XS(i), par("ssd_d", i), halves(5 + g)[:, j, :],
                                                   ALU.mult, ALU.add).then_inc(*mark("ssd_vector"))
                dve.wait_ge(*so_far("ssd_vector"))
                dve.wait_ge(*at("z silu", g))
                nc.vector.tensor_tensor(YS[:, 2 * g:2 * g + 2, :], YS[:, 2 * g:2 * g + 2, :],
                                        zs[:, 2 * g:2 * g + 2, :], ALU.mult).then_inc(
                    *mark("ssd_vector", "ssd gated", g))
            norm_reciprocal(dve, "mem")
            for g in range(2):
                dve.wait_ge(*at("ssd group root", g))
                nc.vector.reciprocal(GT[:, 2 * g:2 * g + 2, :].rearrange("p a b -> p (a b)"),
                                     zs[:, 2 * g, :]).then_inc(*mark("ssd_vector"))
                dve.wait_ge(*so_far("ssd_vector"))
                for j in range(2):
                    i = 2 * g + j
                    nc.vector.scalar_tensor_tensor(mix[:, i, :], YS[:, i, :], par("ssd_norm", i),
                                                   GT[:, 2 * g:2 * g + 2, :].rearrange("p a b -> p (a b)"),
                                                   ALU.mult, ALU.mult).then_inc(*mark("ssd_vector", "mix1", i))

        def act_ssd(act):
            for g in range(2):
                act.wait_ge(*at("ssd decay exponent", g))
            nc.scalar.activation(dect, dect, ACT.Exp).then_inc(*mark("ssd_act", "ssd decay"))
            for g in range(2):
                act.wait_ge(*at("ssd exponent", 0, g, 3))
                nc.scalar.activation(EX[g], EX[g], ACT.Exp).then_inc(*mark("ssd_act", "ssd decays", 0, g))
            for g in range(2):
                act.wait_ge(*at("ssd sums", 1, g))
                nc.scalar.activation(CEX[:, 4 * g:4 * g + 4, :], quarters((3, 7)[g]), ACT.Exp).then_inc(
                    *mark("ssd_act", "ssd cexp", g))
            for g in range(2):
                act.wait_ge(*at("ssd exponent", 1, g, 3))
                nc.scalar.activation(EX[g], EX[g], ACT.Exp).then_inc(*mark("ssd_act", "ssd decays", 1, g))
            act_mem_move(act)
            for g in range(2):
                act.wait_ge(*at("ssd gated", g))
                nc.scalar.activation(xbc[:, 2 * g:2 * g + 2, :], YS[:, 2 * g:2 * g + 2, :], ACT.Square).then_inc(
                    *mark("ssd_act", "ssd squares", g))
            for g in range(2):
                act.wait_ge(*at("ssd group total", g))
                nc.scalar.activation(zs[:, 2 * g, :], banks[g][:, 0:T], ACT.Sqrt, bias=eps[:, 0:1],
                                     scale=1.0 / 256).then_inc(*mark("ssd_act", "ssd group root", g))

        def pool_ssd(pool):
            for g in range(2):
                pool.wait_ge(*at("ssd cexp", g))
                nc.gpsimd.tensor_tensor(CEX[:, 4 * g:4 * g + 4, :], CEX[:, 4 * g:4 * g + 4, :],
                                        over(XS(6 + g)[:, C:2 * C], 4), ALU.mult).then_inc(
                    *mark("ssd_pool", "ssd cex", g))

        def pe_ssd_norm(pe):
            for g in range(2):
                pe.wait_ge(*at("ssd squares", g))
                pe.wait_ge(*at("ssd exponent", 0, 1, 3))
                for j in range(2):
                    mm = nc.tensor.matmul(banks[g][:, 0:T], ones, xbc[:, 2 * g + j, :], start=(j == 0), stop=(j == 1))
                mm.then_inc(*mark("ssd_pe", "ssd group total", g))

        def load_mem(pool):
            pool.wait_ge(*at("x turned", 3))
            pool.dma_start(mix[:, :, :].rearrange("p a b -> p (a b)").rearrange("p (c d) -> p c d", c=2),
                         w["mem_2"][0].rearrange("(c p) d -> p c d", p=P)).then_inc(
                *mark("mem_landed", "mem landed", by=16))

        mem16 = xk[:, :, :].rearrange("p k t -> p (k t)").bitcast(F16).rearrange("p (k w t) -> p k w t", k=KT, w=2)

        def pe_mem_turn(pe, bs):
            xt = mix[:, :, :].rearrange("p a b -> p (a b)").rearrange("p (c d) -> p c d", c=2)
            for b in bs:
                if b == 0:
                    pe.wait_ge(*at("mem landed"))
                    pe.wait_ge(*at("pre_mix", "root"))
                elif b == 1:
                    pe.wait_ge(*at("dt raw"))
                else:
                    pe.wait_ge(*at("mem", "low", 2 * b - 3))
                for m in (2 * b, 2 * b + 1):
                    for c in range(NC_):
                        mm = nc.tensor.transpose(halves(4 + b % 2)[:, m % 2, c * C:(c + 1) * C],
                                                 xt[:, c, m * P:(m + 1) * P], ident)
                mm.then_inc(*mark("mem_turned", "mem turned", b))

        def act_mem_norm(act):
            for m in range(KT):
                act.wait_ge(*at("mem turned", m // 2))
                if m >= 4:
                    act.wait_ge(*at("mem", "summed", m // 2 - 2))
                if m == 0:
                    act.wait_ge(*at("pre_mix", "summed", 3))
                src = halves(4 + m // 2 % 2)[:, m % 2, :]
                nc.scalar.activation(sqs[:, m // 2 % 2, 256 * (m % 2):256 * (m % 2) + 256], src,
                                     ACT.Square).then_inc(*mark("norm_squares", "mem", "squares", m))
                nc.scalar.activation(mem16[:, m, 0, :], src, ACT.Copy, scale=par("norm_mem_2", m)).then_inc(
                    *mark("norm_gained", "mem", "gained", m))

        def dve_mem_norm(dve):
            for b in range(4):
                for m in (2 * b, 2 * b + 1):
                    dve.wait_ge(*at("mem", "gained", 2 * b + 1))
                    nc.vector.scalar_tensor_tensor(mem16[:, m, 1, :], halves(4 + b % 2)[:, m % 2, :],
                                                   par("norm_mem_2", m), mem16[:, m, 0, :], ALU.mult,
                                                   ALU.subtract).then_inc(*mark("norm_low", "mem", "low", m))
                norm_part(dve, nc.vector, "mem", b)

        def act_mem_move(act):
            act.wait_ge(*at("proj1", PBANKS - 1))
            for i in range(2):
                act.wait_ge(*at("mem", "low", 4 * i + 3))
                nc.scalar.activation(hg16[:, 4 * i:4 * i + 4], mem16[:, 4 * i:4 * i + 4], ACT.Copy).then_inc(
                    *mark("mem_moved", "mem moved", i))

        MEM_CHUNKS = [("w_xk_2", "cols", 0), ("w_xk_2", "cols", 1), ("w_xv_2", "cols", 0), ("w_xv_2", "cols", 1)]
        MEM_QUARTERS = 16
        mem_w = [v.bitcast(F16).rearrange("p (w k n) -> p w k n", w=2, k=KT) for v in
                 (sqs[:, :, :].rearrange("p a b -> p (a b)"), mix[:, 4:8, :].rearrange("p a b -> p (a b)"))]

        def mem_source(n):
            return slot(*MEM_CHUNKS[n // 4])[:, :, (n % 4) * P:(n % 4 + 1) * P]

        def mem_high(act, n):
            if n >= MEM_QUARTERS:
                return
            if n % 4 == 0:
                act.wait_ge(*at("chunk", CHUNK_NO[MEM_CHUNKS[n // 4]]))
            if n < 2:
                act.wait_ge(*(at("mem", "summed", 3) if n == 0 else at("ssd y", 1, 1)))
            else:
                act.wait_ge(*at("mem quarter used", n - 2))
            nc.scalar.activation(mem_w[n % 2][:, 0], mem_source(n), ACT.Copy, scale=W_SCALE).then_inc(
                *mark("mem_weights_high", "mem weights high", n))

        def mem_low(dve, n):
            if n >= MEM_QUARTERS:
                return
            dve.wait_ge(*at("mem weights high", n))
            nc.vector.scalar_tensor_tensor(mem_w[n % 2][:, 1], mem_source(n), W_SCALE, mem_w[n % 2][:, 0], ALU.mult,
                                           ALU.subtract).then_inc(*mark("mem_weights_low", "mem weights low", n))
            if n % 4 == 3:
                chunk_used(*MEM_CHUNKS[n // 4], ("mem weights low", n))

        def pe_mem_part(pe, part):
            n, second = part // 2, part % 2
            if not second:
                pe.wait_ge(*at("mem weights low", n))
            if part == 0:
                pe.wait_ge(*at("mem moved", 1))
                pe.wait_ge(*at("mem column"))
            w_ = mem_w[n % 2]
            if n < 8:
                b = 6 + (n // 2) % 2
                if n >= 4 and part % 4 == 0:
                    pe.wait_ge(*at("keys", n // 2 - 2))
                for k in range(4 * second, 4 * second + 4):
                    for i, (a, x) in enumerate(((0, 0), (1, 0), (0, 1))):
                        mm = nc.tensor.matmul(halves(b)[:, n % 2, :], w_[:, a, k, :], hg16[:, k, x, :],
                                              start=(k == 0 and i == 0), stop=(k == KT - 1 and i == 2))
                step = ("keys bank", n // 2) if part % 4 == 3 else ("mem part", part)
            else:
                c, half = second, (n - 8) // 4
                if n % 4 == 0:
                    pe.wait_ge(*(at("keys", 2 + c) if half == 0 else at("values", c)))
                for k in range(KT):
                    for i, (x, a) in enumerate(((0, 0), (1, 0), (0, 1))):
                        mm = nc.tensor.matmul(quarters(6 + c)[:, n % 4, :], hg16[:, k, x, c * C:(c + 1) * C],
                                              w_[:, a, k, :], start=(k == 0 and i == 0), stop=(k == KT - 1 and i == 2))
                step = ("values bank", 2 * half + c) if n % 4 == 3 else ("mem part", part)
            mm.then_inc(*mark("mem_pe", *step))
            if second:
                same(("mem quarter used", n), step)

        def dve_mem_keys(dve, b):
            dve.wait_ge(*at("keys bank", b))
            nc.vector.tensor_tensor(xk[:, 2 * b:2 * b + 2, :], halves(6 + b % 2), over(rstd[:, :], 2),
                                    ALU.mult).then_inc(*mark("mem_keys", "keys", b))

        def act_mem_column(act):
            act.wait_ge(*at("mem", "column"))
            nc.scalar.activation(rcol[:, :], banks[7][:, 0:2], ACT.Copy).then_inc(*mark("mem_act", "mem column"))

        def act_mem_values(act, n):
            if n == 0:
                act.wait_ge(*so_far("mem_act"))
            half, c = n // 2, n % 2
            act.wait_ge(*at("values bank", n))
            nc.scalar.activation(xv[:, c, 512 * half:512 * half + 512], banks[6 + n % 2][:, :], ACT.Copy,
                                 scale=rcol[:, c:c + 1]).then_inc(*mark("mem_act", "values", n))

        def act_lora(act):
            act.wait_ge(*at("shifted", 4))
            nc.scalar.activation(WA[0:64, :], WA[0:64, :], ACT.Tanh).then_inc(*mark("lora_in", "lora tanh"))
            act.wait_ge(*at("shifted", 5))
            nc.scalar.activation(GLO, GLO, ACT.Sigmoid).then_inc(*mark("lora_in", "lora gate"))

        def load_lora(pool):
            pool.dma_start(lora_w[0:64, 0:RW_D], w["rwkv_w2"][0]).then_inc(*mark("lora_weights", by=16))
            pool.dma_start(lora_w[64:128, 0:RW_D], w["rwkv_a2"][0]).then_inc(
                *mark("lora_weights", "lora weights", by=16))

        def load_gate(pool):
            pool.wait_ge(*at("mem", "total"))
            pool.dma_start(gate_w[:, :], w["rwkv_g2"][0]).then_inc(*mark("gate_weights", "gate weights", by=16))

        def pe_lora(pe):
            pe.wait_ge(*at("lora weights"))
            pe.wait_ge(*at("lora tanh"))
            pe.wait_ge(*at("h", 3))
            for j in range(4):
                mm = nc.tensor.matmul(halves(6 + j // 2)[:, j % 2, :], lora_w[0:64, j * P:(j + 1) * P], WA[0:64, :],
                                      start=True, stop=True)
                if j % 2:
                    mm.then_inc(*mark("lora_pe", "decay lora", j // 2))
            pe.wait_ge(*at("mem", "low", 7))
            for j in range(4):
                mm = nc.tensor.matmul(halves(4 + j // 2)[:, j % 2, :], lora_w[64:128, j * P:(j + 1) * P],
                                      WA[64:128, :], start=True, stop=True)
                if j % 2:
                    mm.then_inc(*mark("lora_pe", "rate lora", j // 2))

        def pe_head_norm(pe):
            pe.wait_ge(*at("decay sigmoid", 3))
            pe.wait_ge(*at("k squares"))
            for i in range(2):
                mm = nc.tensor.matmul(banks[6 + i][:, :], head_ones, flat(KSQ)[:, 512 * i:512 * i + 512],
                                      start=True, stop=True)
                mm.then_inc(*mark("lora_pe", "k sums", i))

        def flat(v):
            return v.rearrange("p a b -> p (a b)")

        KP = K_

        def act_rwkv_prepare(act):
            act.wait_ge(*at("shifted", 13))
            for j in range(4):
                act.wait_ge(*at("decay lora", j // 2))
                nc.scalar.activation(SW[:, j, :], halves(6 + j // 2)[:, j % 2, :], ACT.Sigmoid,
                                     bias=par("rwkv_w0", j)).then_inc(*mark("rwkv_act", "decay sigmoid", j))
            for j in range(4):
                act.wait_ge(*at("rate lora", j // 2))
                nc.scalar.activation(A_[:, j, :], halves(4 + j // 2)[:, j % 2, :], ACT.Sigmoid,
                                     bias=par("rwkv_a0", j)).then_inc(*mark("rwkv_act", "rate", j))
            act.wait_ge(*at("kk"))
            nc.scalar.activation(flat(KSQ), flat(KK), ACT.Square).then_inc(*mark("rwkv_act", "k squares"))

        def act_rwkv_exponentials(act):
            for i in range(2):
                act.wait_ge(*at("k sums", i))
                nc.scalar.activation(flat(KSQ)[:, 512 * i:512 * i + 512], banks[6 + i][:, :], ACT.Sqrt).then_inc(
                    *mark("rwkv_act", "k norms", i))
            act.wait_ge(*at("cumulative"))
            nc.scalar.activation(flat(E1), flat(CS), ACT.Exp, scale=-DECAY_SCALE).then_inc(*mark("rwkv_act", "E1"))
            nc.scalar.activation(flat(E2), flat(CS), ACT.Exp, scale=DECAY_SCALE).then_inc(*mark("rwkv_act", "E2"))
            act.wait_ge(*at("cumulative before"))
            nc.scalar.activation(flat(E0), flat(E0), ACT.Exp, scale=-DECAY_SCALE).then_inc(*mark("rwkv_act", "E0"))
            act.wait_ge(*at("state exponent"))
            nc.scalar.activation(small[:, 8:12], small[:, 4:8], ACT.Exp, scale=-DECAY_SCALE).then_inc(
                *mark("rwkv_act", "state factor"))

        def dve_rwkv_prepare(dve):
            dve.wait_ge(*at("shifted", 13))
            for j in range(4):
                nc.vector.tensor_scalar(KK[:, j, :], K_[:, j, :], par("rwkv_k_k", j), None, ALU.mult).then_inc(
                    *mark("rwkv_vector", *(("kk",) if j == 3 else ())))
            for j in range(4):
                dve.wait_ge(*at("decay sigmoid", j))
                nc.vector.tensor_tensor_scan(CS[:, j, :], const("reset128"), SW[:, j, :], 0.0, ALU.mult,
                                             ALU.add).then_inc(*mark("rwkv_vector"))
            dve.wait_ge(*so_far("rwkv_vector"))
            cs4 = flat(CS).rearrange("p (j c t) -> p j c t", j=4, c=NC_)
            nc.vector.tensor_copy(small[:, 12:20].rearrange("p (j c) -> p j c", c=2), cs4[:, :, :, C // 2 - 1]).then_inc(
                *mark("rwkv_vector", "middles"))
            dve.wait_ge(*so_far("rwkv_vector"))
            mid = small[:, 12:20].rearrange("p (j c) -> p j c", c=2)
            nc.vector.tensor_tensor(small[:, 4:8], cs4[:, :, 0, C - 1], mid[:, :, 0], ALU.subtract).then_inc(
                *mark("rwkv_vector"))
            dve.wait_ge(*so_far("rwkv_vector"))
            nc.vector.tensor_tensor(small[:, 4:8], small[:, 4:8], mid[:, :, 1], ALU.add).then_inc(
                *mark("rwkv_vector", "state exponent"))
            jc = flat(CS).rearrange("p (jc t) -> p jc t", t=C)
            nc.vector.tensor_tensor(jc, jc, along(small[:, 12:20], C), ALU.subtract).then_inc(
                *mark("rwkv_vector", "cumulative"))
            nc.vector.tensor_scalar(small[:, 0:4], params[:, PARAM_AT["rwkv_k_a"]:PARAM_AT["rwkv_k_a"] + 4], -1.0,
                                    1.0, ALU.mult, ALU.add).then_inc(*mark("rwkv_vector"))
            dve.wait_ge(*so_far("rwkv_vector"))
            for j in range(4):
                dve.wait_ge(*at("rate", j))
                nc.vector.tensor_scalar(BT[:, j, :], A_[:, j, :], par("rwkv_k_a", j), small[:, j:j + 1],
                                        ALU.mult, ALU.add).then_inc(*mark("rwkv_vector"))
            dve.wait_ge(*so_far("rwkv_vector"))
            nc.vector.tensor_tensor(flat(KP), flat(K_), flat(BT), ALU.mult).then_inc(*mark("rwkv_vector", "k prime"))

        def dve_rwkv_scaled(dve):
            dve.wait_ge(*at("k norms", 1))
            nc.vector.tensor_scalar(flat(KSQ), flat(KSQ), 1e-12, None, ALU.max).then_inc(*mark("rwkv_vector"))
            dve.wait_ge(*so_far("rwkv_vector"))
            nc.vector.reciprocal(flat(KSQ), flat(KSQ)).then_inc(*mark("rwkv_vector"))
            dve.wait_ge(*so_far("rwkv_vector"))
            nc.vector.tensor_tensor(flat(KK), flat(KK), flat(KSQ), ALU.mult).then_inc(*mark("rwkv_vector", "kk unit"))
            dve.wait_ge(*so_far("rwkv_vector"))
            nc.vector.tensor_tensor(flat(BT), flat(KK), flat(A_), ALU.mult).then_inc(*mark("rwkv_vector"))
            dve.wait_ge(*so_far("rwkv_vector"))
            dve.wait_ge(*at("E2"))
            nc.vector.tensor_tensor(flat(BT), flat(BT), flat(E2), ALU.mult).then_inc(*mark("rwkv_vector", "BT"))
            dve.wait_ge(*at("E0"))
            nc.vector.tensor_tensor(flat(E0), flat(E0), flat(KK), ALU.mult).then_inc(*mark("rwkv_vector", "AT"))
            dve.wait_ge(*so_far("rwkv_vector"))
            nc.vector.tensor_tensor(flat(E2), flat(E2), flat(KP), ALU.mult).then_inc(*mark("rwkv_vector", "KT"))

        AT_, RT_, KT_ = E0, E1, E2

        def pool_rwkv_prepare(pool):
            pool.wait_ge(*at("cumulative"))
            pool.wait_ge(*at("decay sigmoid", 3))
            nc.gpsimd.tensor_tensor(flat(E0), flat(CS), flat(SW), ALU.subtract).then_inc(
                *mark("rwkv_pool", "cumulative before"))
            pool.wait_ge(*at("E1"))
            nc.gpsimd.tensor_tensor(flat(E1), flat(E1), flat(R_), ALU.mult).then_inc(*mark("rwkv_pool", "RT"))

        def pe_rwkv_turn_v(pe):
            pe.wait_ge(*at("rate", 3))
            for c in range(NC_):
                for j in range(4):
                    mm = nc.tensor.transpose(quarters(4 + c)[:, j, :], V_[:, j, c * C:(c + 1) * C], ident)
                mm.then_inc(*mark("rwkv_pe", "v turned", c))

        def pe_rwkv_turn(pe):
            pe.wait_ge(*at("k norms", 1))
            for n, (src, step) in enumerate(((BT, "BT"), (KT_, "KT"))):
                pe.wait_ge(*at(step))
                for j in range(4):
                    mm = nc.tensor.transpose(quarters(6 + n)[:, j, :], src[:, j, 0:C], ident)
                mm.then_inc(*mark("rwkv_pe", ("b turned", "k turned")[n]))

        def act_rwkv_turn_v(act):
            for c in range(NC_):
                act.wait_ge(*at("v turned", c))
                if c == 0:
                    act.wait_ge(*at("cumulative before"))
                nc.scalar.activation(VTOK[:, c, :], banks[4 + c][:, :], ACT.Copy).then_inc(
                    *mark("rwkv_act", "v token-major", c))

        def act_rwkv_turn(act):
            act.wait_ge(*at("b turned"))
            act.wait_ge(*so_far("rwkv_act"))
            nc.scalar.activation(BTOK, banks[6][:, :], ACT.Copy, scale=-1.0).then_inc(*mark("rwkv_act", "b token-major"))
            act.wait_ge(*at("k turned"))
            nc.scalar.activation(KTOK, banks[7][:, :], ACT.Copy).then_inc(*mark("rwkv_act", "k token-major"))

        def product(pe, g, c, bank, left, right):
            for j in range(4):
                lo = 64 * g
                mm = nc.tensor.matmul(quarters(bank)[:, j, :], left[lo:lo + 64, j, c * C:(c + 1) * C],
                                      right[lo:lo + 64, j, c * C:(c + 1) * C], start=True, stop=True)
            return mm

        def pe_rwkv_chunk(pe, c):
            def fill(n):
                pe_mem_part(pe, 16 * c + n)

            if c == 0:
                pe.wait_ge(*at("k token-major"))
                pe.wait_ge(*at("AT"))
                pe.wait_ge(*at("ssd group root", 1))
                pe.wait_ge(*at("ssd gated", 1))
            for g in range(2):
                b = 3 * g
                if c == 1:
                    pe.wait_ge(*at("y out", 0, g))
                    pe.wait_ge(*at("state out", g))
                product(pe, g, c, b, BT, AT_).then_inc(*mark("solve_pe", "LT bank", c, g))
                product(pe, g, c, b + 1, AT_, BT).then_inc(*mark("solve_pe", "L bank", c, g))
            fill(0)
            for n, m in enumerate(LEVELS):
                B = P // (2 * m)
                for g in range(2):
                    st = sets[g]
                    pe.wait_ge(*at("X", c, g, n))
                    for j in range(4):
                        x = st["X"][:, j, :].rearrange("p (b two m) -> p b two m", b=B, two=2)[:, :, 0, :]
                        mm = nc.tensor.matmul(banks[3 * g][:, 64 * j:64 * j + 64], st["LT"][:, j, :], x,
                                              start=True, stop=True)
                    mm.then_inc(*mark("solve_pe", "P bank", c, g, n))
                fill(1 + 2 * n)
                for g in range(2):
                    st = sets[g]
                    p = st["PA"] if n % 2 == 0 else st["PB"]
                    pe.wait_ge(*at("P", c, g, n))
                    for j in range(4):
                        x = p[:, j, :].rearrange("p (b two m) -> p b two m", b=B, two=2)[:, :, 0, :]
                        mm = nc.tensor.matmul(banks[3 * g + 1][:, 64 * j:64 * j + 64], st["XT"][:, j, :], x,
                                              start=True, stop=True)
                    for j in range(4):
                        x = st["XT"][:, j, :].rearrange("p (b two m) -> p b two m", b=B, two=2)[:, :, 1, :]
                        mm = nc.tensor.matmul(banks[3 * g + 1][:, 256 + 64 * j:320 + 64 * j], p[:, j, :], x,
                                              start=True, stop=True)
                    mm.then_inc(*mark("solve_pe", "dX bank", c, g, n))
                fill(2 + 2 * n)
            n = len(LEVELS)
            for g in range(2):
                st = sets[g]
                pe.wait_ge(*at("X", c, g, n))
                for j in range(4):
                    mm = nc.tensor.matmul(banks[3 * g][64:128, 64 * j:64 * j + 64], st["LT"][0:64, j, 64:128],
                                          st["X"][0:64, j, 0:64], start=True, stop=True)
                mm.then_inc(*mark("solve_pe", "P64 bank", c, g))
            for g in range(2):
                product(pe, g, c, 3 * g + 1, KT_, AT_).then_inc(*mark("solve_pe", "AK bank", c, g))
            fill(11)
            for g in range(2):
                st = sets[g]
                pe.wait_ge(*at("P64", c, g))
                for j in range(4):
                    mm = nc.tensor.matmul(banks[3 * g + 2][0:64, 64 * j:64 * j + 64], P64[g][64:128, j, :],
                                          st["XT"][64:128, j, 64:128], start=True, stop=True)
                mm.then_inc(*mark("solve_pe", "dXT64 bank", c, g))
            for g in range(2):
                if c == 0 and g == 0:
                    pe.wait_ge(*at("RT"))
                product(pe, g, c, 3 * g, KT_, RT_).then_inc(*mark("solve_pe", "RK bank", c, g))
            fill(12)
            for g in range(2):
                st = sets[g]
                lo = 64 * g
                pe.wait_ge(*at("AK", c, g))
                for j in range(4):
                    hd = 2 * j + g
                    mm = nc.tensor.matmul(banks[3 * g + 1][:, 64 * j:64 * j + 64], st["LT"][:, j, :],
                                          VTOK[:, c, 64 * hd:64 * hd + 64], start=True, stop=(c == 0))
                    if c:
                        mm = nc.tensor.matmul(banks[3 * g + 1][:, 64 * j:64 * j + 64],
                                              AT_[lo:lo + 64, j, C:2 * C], s0c[lo:lo + 64, j, :],
                                              start=False, stop=True)
                mm.then_inc(*mark("solve_pe", "G bank", c, g))
            for g in range(2):
                pe.wait_ge(*at("XT64", c, g))
                product(pe, g, c, 3 * g + 2, BT, RT_).then_inc(*mark("solve_pe", "RB bank", c, g))
            fill(13)
            for g in range(2):
                st = sets[g]
                pe.wait_ge(*at("G", c, g))
                for j in range(4):
                    mm = nc.tensor.matmul(banks[3 * g + 1][:, 256 + 64 * j:320 + 64 * j], st["XT"][:, j, :],
                                          st["G"][:, j, :], start=True, stop=True)
                mm.then_inc(*mark("solve_pe", "U bank", c, g))
            fill(14)
            for g in range(2):
                st = sets[g]
                lo = 64 * g
                pe.wait_ge(*at("U", c, g))
                pe.wait_ge(*at("RK", c, g))
                pe.wait_ge(*at("RB", c, g))
                if c == 0:
                    for j in range(4):
                        hd = 2 * j + g
                        o = banks[3 * g + 2][lo:lo + 64, 64 * j:64 * j + 64]
                        nc.tensor.matmul(o, KTOK[:, 64 * hd:64 * hd + 64], VTOK[:, 0, 64 * hd:64 * hd + 64],
                                         start=True, stop=False)
                        mm = nc.tensor.matmul(o, BTOK[:, 64 * hd:64 * hd + 64], st["U"][:, j, :],
                                              start=False, stop=True)
                    mm.then_inc(*mark("solve_pe", "state bank", g))
                for j in range(4):
                    hd = 2 * j + g
                    o = quarters(3 * g)[lo:lo + 64, j, :]
                    nc.tensor.matmul(o, VTOK[:, c, 64 * hd:64 * hd + 64], st["X"][:, j, :], start=True, stop=False)
                    mm = nc.tensor.matmul(o, st["U"][:, j, :], st["ARB"][:, j, :], start=False, stop=(c == 0))
                    if c:
                        mm = nc.tensor.matmul(o, s0c[lo:lo + 64, j, :], RT_[lo:lo + 64, j, C:2 * C],
                                              start=False, stop=True)
                mm.then_inc(*mark("solve_pe", "y bank", c, g))
            fill(15)

        def dve_rwkv_chunk(dve, c):
            for g in range(2):
                st = sets[g]
                b = 3 * g
                dve.wait_ge(*at("LT bank", c, g))
                if c:
                    dve.wait_ge(*at("y bank", 0, g))
                nc.vector.tensor_tensor(st["LT"], quarters(b), over(const("neg_strict"), 4), ALU.mult).then_inc(
                    *mark("solve_vector", "LT", c, g))
                dve.wait_ge(*at("L bank", c, g))
                nc.vector.tensor_tensor(st["X"], quarters(b + 1), over(const("pair"), 4), ALU.mult).then_inc(
                    *mark("solve_vector"))
                dve.wait_ge(*at("LT", c, g))
                nc.vector.tensor_tensor(st["XT"], st["LT"], over(const("pair_t"), 4), ALU.mult).then_inc(
                    *mark("solve_vector"))
                dve.wait_ge(*so_far("solve_vector"))
                both = st["XX"]
                nc.vector.tensor_tensor(both, both, over(ident, 8), ALU.add).then_inc(
                    *mark("solve_vector", "X", c, g, 0))
            if c == 0:
                mem_low(dve, 1)
            for n, m in enumerate(LEVELS):
                B = P // (2 * m)
                mask = const("levels")[:, 64 * n:64 * n + 64].rearrange("p (b m) -> p b m", b=B)
                for g in range(2):
                    st = sets[g]
                    p = (st["PA"] if n % 2 == 0 else st["PB"]).rearrange("p j (b two m) -> p j b two m", b=B, two=2)
                    dve.wait_ge(*at("P bank", c, g, n))
                    dve.wait_ge(*at("P zeroed", c, g, n))
                    nc.vector.tensor_tensor(p[:, :, :, 0, :],
                                            banks[3 * g][:, 0:256].rearrange("p (j b m) -> p j b m", j=4, b=B),
                                            mask.unsqueeze(1).broadcast_to([P, 4, B, m]), ALU.mult).then_inc(
                        *mark("solve_vector", "P", c, g, n))
                for g in range(2):
                    grown = sets[g]["grown"](m)
                    dve.wait_ge(*at("dX bank", c, g, n))
                    nc.vector.tensor_tensor(grown, banks[3 * g + 1][:, :].rearrange("p (w jb m) -> p w jb m", w=2, m=m),
                                            grown, ALU.add).then_inc(*mark("solve_vector", "X", c, g, n + 1))
                mem_low(dve, 8 * c + n + 2)
                if c == 0 and n in (1, 3):
                    dve_mem_keys(dve, n // 2)
            for g in range(2):
                dve.wait_ge(*at("P64 bank", c, g))
                nc.vector.tensor_copy(P64[g][64:128, :, :],
                                      banks[3 * g][64:128, 0:256].rearrange("p (j m) -> p j m", j=4)).then_inc(
                    *mark("solve_vector", "P64", c, g))
            mem_low(dve, 8 * c + 7)
            for g in range(2):
                dve.wait_ge(*at("AK bank", c, g))
                nc.vector.tensor_tensor(sets[g]["LT"], quarters(3 * g + 1), over(const("strict"), 4),
                                        ALU.mult).then_inc(*mark("solve_vector", "AK", c, g))
            for g in range(2):
                dve.wait_ge(*at("dXT64 bank", c, g))
                nc.vector.tensor_copy(sets[g]["XT"][0:64, :, 64:128],
                                      banks[3 * g + 2][0:64, 0:256].rearrange("p (j m) -> p j m", j=4)).then_inc(
                    *mark("solve_vector", "XT64", c, g))
            for g in range(2):
                dve.wait_ge(*at("RK bank", c, g))
                nc.vector.tensor_tensor(sets[g]["X"], quarters(3 * g), over(const("incl"), 4), ALU.mult).then_inc(
                    *mark("solve_vector", "RK", c, g))
            if c == 0:
                dve_mem_keys(dve, 2)
            for g in range(2):
                dve.wait_ge(*at("RB bank", c, g))
                nc.vector.tensor_tensor(sets[g]["ARB"], quarters(3 * g + 2), over(const("neg_incl"), 4),
                                        ALU.mult).then_inc(*mark("solve_vector", "RB", c, g))
            mem_low(dve, 8 * c + 8)
            if c == 0:
                for g in range(2):
                    lo = 64 * g
                    dve.wait_ge(*at("state bank", g))
                    dve.wait_ge(*at("state factor"))
                    nc.vector.tensor_tensor(s0c[lo:lo + 64], banks[3 * g + 2][lo:lo + 64, 0:256].rearrange(
                        "p (j m) -> p j m", j=4), along(small[lo:lo + 64, 8:12], 64), ALU.mult).then_inc(
                        *mark("solve_vector", "state out", g))
                dve_mem_keys(dve, 3)
            mem_low(dve, 8 * c + 9)

        def act_rwkv_chunk(act, c):
            for n in range(8 * c + 2, 8 * c + 8):
                if n == 14:
                    act_mem_values(act, 0)
                    act_mem_values(act, 1)
                mem_high(act, n)
            for g in range(2):
                st = sets[g]
                act.wait_ge(*at("G bank", c, g))
                nc.scalar.activation(st["G"], banks[3 * g + 1][:, 0:256].rearrange("p (j m) -> p j m", j=4),
                                     ACT.Copy).then_inc(*mark("solve_act", "G", c, g))
            mem_high(act, 8 * c + 8)
            for g in range(2):
                st = sets[g]
                act.wait_ge(*at("U bank", c, g))
                nc.scalar.activation(st["U"], banks[3 * g + 1][:, 256:512].rearrange("p (j m) -> p j m", j=4),
                                     ACT.Copy).then_inc(*mark("solve_act", "U", c, g))
            for g in range(2):
                lo = 64 * g
                act.wait_ge(*at("y bank", c, g))
                nc.scalar.activation(Y[lo:lo + 64, :, c * C:(c + 1) * C], quarters(3 * g)[lo:lo + 64],
                                     ACT.Copy).then_inc(*mark("solve_act", "y out", c, g))
            mem_high(act, 8 * c + 9)
            if c:
                act_mem_values(act, 2)
                act_mem_values(act, 3)

        def pool_rwkv_chunk(pool, c):
            for n in range(len(LEVELS)):
                for g in range(2):
                    p = sets[g]["PA"] if n % 2 == 0 else sets[g]["PB"]
                    if n >= 2:
                        pool.wait_ge(*at("dX bank", c, g, n - 2))
                    elif c:
                        pool.wait_ge(*at("dX bank", 0, g, 4 - n))
                    else:
                        pool.wait_ge(*at("mix1", 3))
                    nc.gpsimd.memset(p, 0.0).then_inc(*mark("solve_pool", "P zeroed", c, g, n))

        def pe_rwkv_end(pe):
            pe.wait_ge(*at("lora gate"))
            pe.wait_ge(*at("gate weights"))
            for g in range(2):
                pe.wait_ge(*at("y out", 1, g))
                pe.wait_ge(*at("RB", 1, g))
            pe.wait_ge(*at("values", 3))
            for j in range(4):
                mm = nc.tensor.matmul(halves(j // 2)[:, j % 2, :], gate_w[:, j * P:(j + 1) * P], GLO,
                                      start=True, stop=True)
            mm.then_inc(*mark("rwkv_end_pe", "gate bank"))
            for i in range(2):
                mm = nc.tensor.matmul(banks[4 + i][:, :], head_ones, flat(Y)[:, 512 * i:512 * i + 512],
                                      start=True, stop=True)
                mm.then_inc(*mark("rwkv_end_pe", "mean bank", i))
            pe.wait_ge(*at("bonus products"))
            for i in range(2):
                mm = nc.tensor.matmul(banks[2 + i][:, :], head_ones, flat(A_)[:, 512 * i:512 * i + 512],
                                      start=True, stop=True)
            mm.then_inc(*mark("rwkv_end_pe", "bonus bank"))
            for i in range(2):
                pe.wait_ge(*at("centred squares", i))
                mm = nc.tensor.matmul(banks[6 + i][:, :], head_ones, flat(BT)[:, 512 * i:512 * i + 512],
                                      start=True, stop=True)
                mm.then_inc(*mark("rwkv_end_pe", "variance bank", i))

        def pool_bonus(pool):
            pool.wait_ge(*at("k prime"))
            pool.wait_ge(*at("BT"))
            pool.wait_ge(*at("mix1", 3))
            nc.gpsimd.tensor_tensor(flat(A_), flat(R_), flat(KP), ALU.mult).then_inc(*mark("rwkv_pool", "rk"))

        def dve_bonus(dve):
            dve.wait_ge(*at("rk"))
            for j in range(4):
                nc.vector.tensor_scalar(A_[:, j, :], A_[:, j, :], par("rwkv_r_k", j), None, ALU.mult).then_inc(
                    *mark("bonus_vector", *(("bonus products",) if j == 3 else ())))

        def dve_rwkv_end(dve):
            for i in range(2):
                dve.wait_ge(*at("mean bank", i))
                nc.vector.scalar_tensor_tensor(flat(Y)[:, 512 * i:512 * i + 512], banks[4 + i][:, :], -1.0 / RW_HD,
                                               flat(Y)[:, 512 * i:512 * i + 512], ALU.mult, ALU.add).then_inc(
                    *mark("rwkv_end_vector", "centred", i))
            dve.wait_ge(*at("bonus bank"))
            for i in range(2):
                nc.vector.tensor_tensor(flat(BONUS)[:, 512 * i:512 * i + 512], banks[2 + i][:, :],
                                        flat(V_)[:, 512 * i:512 * i + 512], ALU.mult).then_inc(
                    *mark("rwkv_end_vector", "bonus", i))
            for i in range(2):
                s = slice(512 * i, 512 * i + 512)
                dve.wait_ge(*at("variance root", i))
                nc.vector.reciprocal(flat(E1)[:, s], flat(E1)[:, s]).then_inc(*mark("rwkv_end_vector"))
                dve.wait_ge(*so_far("rwkv_end_vector"))
                nc.vector.tensor_tensor(flat(Y)[:, s], flat(Y)[:, s], flat(E1)[:, s], ALU.mult).then_inc(
                    *mark("rwkv_end_vector"))
                dve.wait_ge(*so_far("rwkv_end_vector"))
                for j in (2 * i, 2 * i + 1):
                    nc.vector.tensor_scalar(Y[:, j, :], Y[:, j, :], par("rwkv_ln_w", j), par("rwkv_ln_b", j),
                                            ALU.mult, ALU.add).then_inc(*mark("rwkv_end_vector"))
                dve.wait_ge(*so_far("rwkv_end_vector"))
                nc.vector.tensor_tensor(flat(Y)[:, s], flat(Y)[:, s], flat(BONUS)[:, s], ALU.add).then_inc(
                    *mark("rwkv_end_vector"))
                dve.wait_ge(*so_far("rwkv_end_vector"))
                nc.vector.tensor_tensor(mix[:, 4 + 2 * i:6 + 2 * i, :].rearrange("p a b -> p (a b)"),
                                        banks[i][:, :], flat(Y)[:, s], ALU.mult).then_inc(
                    *mark("rwkv_end_vector", "mix1", 4 + 2 * i))
                same(("mix1", 5 + 2 * i), ("mix1", 4 + 2 * i))

        def act_rwkv_end(act):
            for i in range(2):
                s = slice(512 * i, 512 * i + 512)
                act.wait_ge(*at("centred", i))
                nc.scalar.activation(flat(BT)[:, s], flat(Y)[:, s], ACT.Square).then_inc(
                    *mark("rwkv_end_act", "centred squares", i))
            for i in range(2):
                s = slice(512 * i, 512 * i + 512)
                act.wait_ge(*at("variance bank", i))
                nc.scalar.activation(flat(E1)[:, s], banks[6 + i][:, :], ACT.Sqrt, bias=eps[:, 1:2],
                                     scale=1.0 / RW_HD).then_inc(*mark("rwkv_end_act", "variance root", i))

        def hidden16(tiles):
            return view(0, tiles * T).bitcast(F16).rearrange("p (k w t) -> p k w t", k=tiles, w=2)

        hid = hidden16(FFT)
        uraw = [view(5632 + 516 * i, 2, T + 2) for i in range(4)]
        uacc = [view(7696 + 512 * i, 2, T) for i in range(4)]
        gsil = [view(9744 + 512 * i, 2, T) for i in range(2)]
        hidf = [view(10768 + 512 * i, 2, T) for i in range(2)]

        def first_group(pe, n, chunks, label, free, h_done):
            for b in range(2):
                pe.wait_ge(*at(*free(b)))
            pe.wait_ge(*at("low", SPLIT_NO[chunks[0]], 3))
            for k in range(KT):
                pe.wait_ge(*at(n, "low", k))
                for m in range(4):
                    mm = product3(halves(m // 2)[:, m % 2, :], halves_of(chunks[0]), k, slice(m * P, (m + 1) * P),
                                  hg16, k == 0 and m % 2 == 0, k == KT - 1)
                    if k == KT - 1 and m % 2:
                        mm.then_inc(*mark("projected", label, "bank", m // 2))
            split_used(chunks[0], (label, "bank", 1))
            norm_total(pe, n, 4, h_done)
            for b in (2, 3):
                pe.wait_ge(*at(*free(b)))
                for i in range(2):
                    mm = wide(pe, chunks[1], 2 * (b - 2) + i, b, i)
                mm.then_inc(*mark("projected", label, "bank", b))
            split_used(chunks[1], (label, "bank", 3))

        def pe_ffn_up(pe):
            first_group(pe, "pre_ffn", [("ffn_w_up", "pair", 0), ("ffn_w_up", "pair", 1)], "up",
                        lambda b: ("mix1", 7), ("post_mix", "added", 7))
            for b in range(4, FFT):
                j = b // 2
                pe.wait_ge(*at("up scaled", b - 4))
                for i in range(2):
                    mm = wide(pe, ("ffn_w_up", "pair", j), 2 * (b % 2) + i, b % 4, i)
                mm.then_inc(*mark("projected", "up", "bank", b))
                if b % 2:
                    split_used(("ffn_w_up", "pair", j), ("up", "bank", b))

        def pool_ffn(pool):
            pool.wait_ge(*at("mix1", 7))
            for i in range(4):
                nc.gpsimd.memset(uraw[i][:, :, 0:2], 0.0).then_inc(*mark("ffn_pads", *(("ffn pads",) if i == 3 else ())))

        def dve_ffn(dve):
            norm_reciprocal(dve, "pre_ffn")
            dve.wait_ge(*so_far("norm_rstd"))
            dve.wait_ge(*at("ffn pads"))
            for b in range(FFT):
                r = b % 4
                dve.wait_ge(*at("up", "bank", b))
                nc.vector.tensor_tensor(uraw[r][:, :, 2:T + 2], halves(r), over(rstd[:, :], 2), ALU.mult).then_inc(
                    *mark("up_scaled", "up scaled", b))
                dve.wait_ge(*so_far("up_scaled"))
                tile0 = 2 * (b // 2) + FFT * (b % 2)
                n, q = split_turn(SPLIT_1, b)
                split_low(dve, n, q[:1])
                for tap in (1, 0):
                    for i in range(2):
                        dve.wait_ge(*at("conv", tap + 1, b, i))
                        nc.vector.scalar_tensor_tensor(uacc[r][:, i, :], uraw[r][:, i, tap:tap + T],
                                                       par("ffn_conv_w", 2 * FFT * tap + tile0 + i), uacc[r][:, i, :],
                                                       ALU.mult, ALU.add).then_inc(*mark("ffn_conv", "conv", tap, b, i))
                split_low(dve, n, q[1:])
                if b % 2:
                    for i in range(2):
                        dve.wait_ge(*at("conv", 0, b, i))
                        dve.wait_ge(*at("gate silu", b // 2, i))
                        if b >= 5:
                            dve.wait_ge(*at("hid", b - 5 + i))
                        nc.vector.scalar_tensor_tensor(hidf[b // 2 % 2][:, i, :], uacc[r][:, i, :],
                                                       par("ffn_conv_b", FFT + b - 1 + i), gsil[b // 2 % 2][:, i, :],
                                                       ALU.add, ALU.mult).then_inc(
                            *mark("hidden", "hidden float", b - 1 + i))
            split_low(dve, n, (2, 3))
            for n in range(n + 1, SPLIT_FROM["w_in_2"]):
                split_low(dve, n, range(4))

        SPLIT_1, SPLIT_2 = SPLIT_FROM["ffn_w_up"], SPLIT_FROM["w_ff1_2"]

        def split_turn(start, b):
            return start + (b + 1) // 2 + 1, ((0, 1) if b % 2 else (2, 3)) if b else ()

        def act_ffn(act):
            for b in range(FFT):
                r, p = b % 4, b // 2
                n, q = split_turn(SPLIT_1, b)
                split_high(act, n, q[:1])
                act.wait_ge(*at("up scaled", b))
                if b >= 4:
                    act.wait_ge(*(at("hidden float", b - 4) if b % 2 else at("gate silu", p - 2, 1)))
                for i in range(2):
                    nc.scalar.activation(uacc[r][:, i, :], uraw[r][:, i, 2:T + 2], ACT.Copy,
                                         scale=par("ffn_conv_w", 2 * 2 * FFT + 2 * p + FFT * (b % 2) + i)).then_inc(
                        *mark("ffn_tap", "conv", 2, b, i))
                split_high(act, n, q[1:])
                for i in range(2):
                    if b % 2 == 0:
                        act.wait_ge(*at("conv", 0, b, i))
                        if p >= 2:
                            act.wait_ge(*at("hidden float", 2 * (p - 2) + i))
                        nc.scalar.activation(gsil[p % 2][:, i, :], uacc[r][:, i, :], ACT.Silu,
                                             bias=par("ffn_conv_b", 2 * p + i)).then_inc(
                            *mark("gate_silu", "gate silu", p, i))
                    else:
                        act.wait_ge(*at("hidden float", b - 1 + i))
                        nc.scalar.activation(hid[:, b - 1 + i, 0, :], hidf[p % 2][:, i, :], ACT.Copy).then_inc(
                            *mark("hidden_high", "hid high", b - 1 + i))
            split_high(act, n, (2, 3))
            for n in range(n + 1, SPLIT_FROM["w_in_2"]):
                split_high(act, n, range(4))

        def pool_hidden(pool):
            for m in range(FFT):
                pool.wait_ge(*at("hid high", m))
                nc.gpsimd.tensor_tensor(hid[:, m, 1, :], hidf[m // 2 % 2][:, m % 2, :], hid[:, m, 0, :],
                                        ALU.subtract).then_inc(*mark("hidden_low", "hid", m))

        FR, BCS, EB, EMB, HQ, KF = (view(1024 * i, 4, T) for i in range(6))
        KETOK, VI = view(1024, NC_, HG_D), view(7168, NC_, HG_D)
        GH = view(8192, 4, T)
        AM = [view(9216 + 512 * i, 4, C) for i in range(2)]
        NS = T // HG_CHUNK
        SV = view(10240, NS - 1, 4 * C)
        MQ, MK = view(13824, 4, T), view(14848, 4, T)
        MV = view(6144, NC_, 512)
        SC = view(16896, 4, 2 * T)
        PT = view(18944, 4, 3 * C)
        lb = sb("lb_stat", 64)
        stat = small

        W2 = lambda i: ("w_in_2", "cols", i)

        def pe_project2(pe):
            first_group(pe, "norm_mix", [W2(1), W2(0)], "in2", lambda b: ("up scaled", FFT - 4 + b),
                        ("post_ffn", "added", 7))
            def token_major(i, b0, label, waits):
                pe.wait_ge(*at("low", SPLIT_NO[W2(i)], 3))
                w_ = halves_of(W2(i))
                for c in range(NC_):
                    pe.wait_ge(*at(*waits[c]))
                    for k in range(KT):
                        for n, (a, b) in enumerate(((0, 0), (1, 0), (0, 1))):
                            mm = nc.tensor.matmul(banks[b0 + c][:, :], hg16[:, k, b, c * C:(c + 1) * C], w_[a][:, k, :],
                                                  start=(k == 0 and n == 0), stop=(k == KT - 1 and n == 2))
                    mm.then_inc(*mark("projected", label, c))
                split_used(W2(i), (label, 1))

            def feature_major(i, b0, label, waits):
                for b in range(2):
                    pe.wait_ge(*at(*waits[b]))
                    for j in range(2):
                        mm = wide(pe, W2(i), 2 * b + j, b0 + b, j)
                    mm.then_inc(*mark("projected", label, b))
                split_used(W2(i), (label, 1))

            token_major(2, 0, "hi bank", [("hf scaled", 0), ("hf scaled", 1)])
            column_rstd(pe, "norm_mix", 5, ("norm_mix", "root"))
            feature_major(3, 2, "hgate bank", [("hq scaled", 0), ("hq scaled", 1)])
            feature_major(4, 0, "mq bank", [("hi out", 0), ("hi out", 1)])
            feature_major(5, 2, "mk bank", [("hgate scaled", 0), ("hgate scaled", 1)])
            pe_hgrn(pe)
            pe_rotary(pe)
            token_major(6, 0, "mv bank", [("mq scaled", 0), ("mq scaled", 1)])

        def dve_project2(dve):
            norm_reciprocal(dve, "norm_mix")
            dve.wait_ge(*so_far("norm_rstd"))
            nc.vector.tensor_tensor(lb[:, 8:12], params[:, PARAM_AT["lb_logits_2"]:PARAM_AT["lb_logits_2"] + 4],
                                    params[:, PARAM_AT["lb_logits_2"] + 4:PARAM_AT["lb_logits_2"] + 8],
                                    ALU.subtract).then_inc(*mark("hgrn_vector", "lb logits"))

            def scaled(dst, b0, full, label):
                for b in range(2):
                    dve.wait_ge(*at(*full(b)))
                    nc.vector.tensor_tensor(dst[:, 2 * b:2 * b + 2, :], halves(b0 + b), over(rstd[:, :], 2),
                                            ALU.mult).then_inc(*mark("in2_scaled", label, b))

            N2 = SPLIT_FROM["w_in_2"]
            split_low(dve, N2 + 2, (0, 1))
            scaled(FR, 0, lambda b: ("in2", "bank", b), "hf scaled")
            split_low(dve, N2 + 2, (2, 3))
            scaled(HQ, 2, lambda b: ("in2", "bank", 2 + b), "hq scaled")
            split_low(dve, N2 + 3, range(4))
            dve.wait_ge(*at("lb"))
            nc.vector.tensor_scalar(lb[:, 4:8], lb[:, 0:4], -1.0, 1.0, ALU.mult, ALU.add).then_inc(*mark("hgrn_vector"))
            dve.wait_ge(*so_far("hgrn_vector"))
            dve.wait_ge(*at("f sigmoid"))
            for j in range(4):
                nc.vector.tensor_scalar(FR[:, j, :], FR[:, j, :], lb[:, 4 + j:5 + j], lb[:, j:j + 1], ALU.mult,
                                        ALU.add).then_inc(*mark("hgrn_vector"))
            dve.wait_ge(*so_far("hgrn_vector"))
            nc.vector.tensor_scalar(flat(KF), flat(FR), -1.0, 1.0, ALU.mult, ALU.add).then_inc(
                *mark("hgrn_vector", "f"))
            dve.wait_ge(*at("log f"))
            for j in range(4):
                nc.vector.tensor_tensor_scan(BCS[:, j, :], const("reset32"), EB[:, j, :], 0.0, ALU.mult,
                                             ALU.add).then_inc(*mark("hgrn_vector", *(("b",) if j == 3 else ())))
            split_low(dve, N2 + 4, range(4))
            scaled(GH, 2, lambda b: ("hgate bank", b), "hgate scaled")
            dve.wait_ge(*at("exp b"))
            nc.vector.tensor_copy(stat[:, 0:32], flat(EB)[:, HG_CHUNK - 1::HG_CHUNK]).then_inc(
                *mark("hgrn_vector", "decays"))
            nc.vector.tensor_tensor(flat(HQ), flat(HQ), flat(EB), ALU.mult).then_inc(*mark("hgrn_vector", "q~"))
            dve.wait_ge(*at("exp -b"))
            nc.vector.tensor_tensor(flat(KF), flat(KF), flat(EMB), ALU.mult).then_inc(*mark("hgrn_vector", "k~"))
            dve.wait_ge(*so_far("hgrn_vector"))
            nc.vector.tensor_tensor(flat(EMB).rearrange("p (n t) -> p n t", t=HG_CHUNK),
                                    flat(KF).rearrange("p (n t) -> p n t", t=HG_CHUNK),
                                    along(stat[:, 0:32], HG_CHUNK), ALU.mult).then_inc(*mark("hgrn_vector", "k end"))
            split_low(dve, N2 + 5, range(4))
            scaled(MQ, 0, lambda b: ("mq bank", b), "mq scaled")
            split_low(dve, N2 + 6, range(4))
            scaled(MK, 2, lambda b: ("mk bank", b), "mk scaled")

        def act_project2(act):
            act.wait_ge(*at("lb logits"))
            nc.scalar.activation(lb[:, 0:4], lb[:, 8:12], ACT.Sigmoid).then_inc(*mark("hgrn_act", "lb"))
            N2 = SPLIT_FROM["w_in_2"]
            split_high(act, N2 + 2, range(4))
            act.wait_ge(*at("hf scaled", 1))
            nc.scalar.activation(flat(FR), flat(FR), ACT.Sigmoid).then_inc(*mark("hgrn_act", "f sigmoid"))
            split_high(act, N2 + 3, range(4))
            act.wait_ge(*at("f"))
            nc.scalar.preload_act_table_set("natural_log_exp_and_others")
            nc.scalar.activation(flat(EB), flat(FR), ACT.Ln).then_inc(*mark("hgrn_act", "log f"))
            act.wait_ge(*at("norm_mix", "column"))
            nc.scalar.activation(rcol[:, :], banks[5][:, 0:2], ACT.Copy).then_inc(*mark("hgrn_act", "mix column"))
            act.wait_ge(*so_far("hgrn_act"))
            for c in range(NC_):
                act.wait_ge(*at("hi bank", c))
                nc.scalar.activation(VI[:, c, :], banks[c][:, :], ACT.Copy, scale=rcol[:, c:c + 1]).then_inc(
                    *mark("in2_scaled_act", "hi out", c))
            split_high(act, N2 + 4, range(4))
            act.wait_ge(*at("b"))
            nc.scalar.activation(flat(EB), flat(BCS), ACT.Exp).then_inc(*mark("hgrn_act", "exp b"))
            nc.scalar.activation(flat(EMB), flat(BCS), ACT.Exp, scale=-1.0).then_inc(*mark("hgrn_act", "exp -b"))
            split_high(act, N2 + 5, range(4))
            act.wait_ge(*at("hgate scaled", 1))
            nc.scalar.activation(flat(GH), flat(GH), ACT.Silu).then_inc(*mark("hgrn_act", "hgate"))
            split_high(act, N2 + 6, range(4))

        def pe_hgrn(pe):
            pe.wait_ge(*at("mix column"))
            pe.wait_ge(*at("post_ffn", "added", 7))
            pe.wait_ge(*at("k~"))
            for c in range(NC_):
                for j in range(4):
                    mm = nc.tensor.matmul(quarters(4 + c)[:, j, :], KF[:, j, c * C:(c + 1) * C],
                                          HQ[:, j, c * C:(c + 1) * C], start=True, stop=True)
                mm.then_inc(*mark("hgrn_pe", "A bank", c))
            pe.wait_ge(*at("k end"))
            for c in range(NC_):
                for j in range(4):
                    mm = nc.tensor.transpose(quarters(6 + c)[:, j, :], EMB[:, j, c * C:(c + 1) * C], ident)
                mm.then_inc(*mark("hgrn_pe", "k end turned", c))

        def pe_hgrn_states(pe):
            for n in range(NS - 1):
                c, r = n // 4, 32 * (n % 4)
                pe.wait_ge(*at("k end token-major", c))
                pe.wait_ge(*(at("A", n) if n < 2 else at("hgrn state", n - 2)))
                for j in range(4):
                    mm = nc.tensor.matmul(quarters(4 + n % 2)[:, j, :], KETOK[r:r + 32, c, j * C:(j + 1) * C],
                                          VI[r:r + 32, c, j * C:(j + 1) * C], start=True, stop=True,
                                          tile_position=(r, 0))
                mm.then_inc(*mark("hgrn_pe", "hgrn state bank", n))

        def pe_hgrn_out(pe):
            for c in range(NC_):
                pe.wait_ge(*at("A", c))
                pe.wait_ge(*at("k end token-major", c))
                for j in range(4):
                    nc.tensor.matmul(halves(6 + j // 2)[:, j % 2, c * C:(c + 1) * C], VI[:, c, j * C:(j + 1) * C],
                                     AM[c][:, j, :], start=(c == 0 and j % 2 == 0), stop=False, skip_group_check=True)
            for n in range(1, NS):
                pe.wait_ge(*at("hgrn state", n - 1))
                for j in range(4):
                    mm = nc.tensor.matmul(halves(6 + j // 2)[:, j % 2, n * HG_CHUNK:(n + 1) * HG_CHUNK],
                                          SV[:, n - 1, j * C:(j + 1) * C],
                                          HQ[:, j, n * HG_CHUNK:(n + 1) * HG_CHUNK], start=False, stop=(n == NS - 1),
                                          skip_group_check=True)
            mm.then_inc(*mark("hgrn_pe", "o bank"))

        def pe_hgrn_norm(pe):
            for i in range(2):
                pe.wait_ge(*at("o squares", i))
                pe.wait_ge(*at("hgrn state", NS - 2))
                mm = nc.tensor.matmul(banks[4 + i][:, :], ones, flat(BCS)[:, 512 * i:512 * i + 512],
                                      start=True, stop=True)
                mm.then_inc(*mark("hgrn_pe", "o total", i))

        def dve_hgrn(dve):
            for c in range(NC_):
                dve.wait_ge(*at("A bank", c))
                nc.vector.tensor_tensor(AM[c], quarters(4 + c), over(const("chunk32"), 4), ALU.mult).then_inc(
                    *mark("hgrn_vector", "A", c))

        def dve_hgrn_states(dve):
            for n in range(NS - 1):
                dve.wait_ge(*at("hgrn state bank", n))
                if n:
                    dve.wait_ge(*at("hgrn state", n - 1))
                for j in range(4):
                    b = quarters(4 + n % 2)[:, j, :]
                    o = SV[:, n, j * C:(j + 1) * C]
                    if n == 0:
                        ins = nc.vector.tensor_copy(o, b)
                    else:
                        ins = nc.vector.scalar_tensor_tensor(o, SV[:, n - 1, j * C:(j + 1) * C],
                                                             stat[:, NS * j + n:NS * j + n + 1], b, ALU.mult, ALU.add)
                    ins.then_inc(*mark("hgrn_vector", *(("hgrn state", n) if j == 3 else ())))

        def act_hgrn(act):
            for c in range(NC_):
                act.wait_ge(*at("k end turned", c))
                nc.scalar.activation(KETOK[:, c, :], banks[6 + c][:, :], ACT.Copy).then_inc(
                    *mark("hgrn_act", "k end token-major", c))

        def act_hgrn_end(act):
            act.wait_ge(*at("o bank"))
            for i in range(2):
                nc.scalar.activation(flat(BCS)[:, 512 * i:512 * i + 512], banks[6 + i][:, :], ACT.Square).then_inc(
                    *mark("hgrn_act", "o squares", i))
            for i in range(2):
                nc.scalar.activation(flat(EMB)[:, 512 * i:512 * i + 512], banks[6 + i][:, :], ACT.Copy).then_inc(
                    *mark("hgrn_act", "o copied", i))
            for i in range(2):
                act.wait_ge(*at("o total", i))
                nc.scalar.activation(flat(FR)[:, 512 * i:512 * i + 512], banks[4 + i][:, :], ACT.Sqrt,
                                     bias=eps[:, 0:1], scale=1.0 / C).then_inc(*mark("hgrn_act", "o root", i))

        def dve_hgrn_end(dve):
            for i in range(2):
                s = slice(512 * i, 512 * i + 512)
                dve.wait_ge(*at("o root", i))
                nc.vector.reciprocal(flat(FR)[:, s], flat(FR)[:, s]).then_inc(*mark("hgrn_vector"))
                dve.wait_ge(*so_far("hgrn_vector"))
                nc.vector.tensor_tensor(flat(FR)[:, s], flat(EMB)[:, s], flat(FR)[:, s], ALU.mult).then_inc(
                    *mark("hgrn_vector"))
                dve.wait_ge(*so_far("hgrn_vector"))
                dve.wait_ge(*at("hgate"))
                for j in (2 * i, 2 * i + 1):
                    nc.vector.scalar_tensor_tensor(mix[:, j, :], FR[:, j, :], par("hgrn_norm_2", j), GH[:, j, :],
                                                   ALU.mult, ALU.mult).then_inc(*mark("hgrn_vector", "mix2", j))

        def pe_rotary(pe):
            for n, (v, b0, ready, free) in enumerate(((MQ, 2, "mq scaled", "mk scaled"),
                                                      (MK, 6, "mk scaled", "k end token-major"))):
                pe.wait_ge(*at(ready, 1))
                pe.wait_ge(*at(free, 1))
                for i in range(2):
                    mm = nc.tensor.matmul(banks[b0 + i][0:ROT, :], const("swap")[0:ROT, 0:ROT],
                                          flat(v)[0:ROT, 512 * i:512 * i + 512], start=True, stop=True)
                mm.then_inc(*mark("moba_pe", "swapped", n))

        def act_moba_values(act):
            for c in range(NC_):
                act.wait_ge(*at("mv bank", c))
                nc.scalar.activation(MV[:, c, :], banks[c][:, :], ACT.Copy, scale=rcol[:, c:c + 1]).then_inc(
                    *mark("in2_scaled_act", "mv out", c))

        def dve_rotary(dve):
            tmp = EB
            for n, (v, b0) in enumerate(((MQ, 2), (MK, 6))):
                dve.wait_ge(*at("swapped", n))
                dve.wait_ge(*(at("k~") if n == 0 else so_far("rotary")))
                for i in range(2):
                    nc.vector.tensor_tensor(tmp[0:ROT, 2 * i:2 * i + 2, :], halves(b0 + i)[0:ROT],
                                            over(const("sin")[0:ROT, :], 2), ALU.mult).then_inc(
                        *mark("rotary", "rotary bank read", n, i))
                dve.wait_ge(*so_far("rotary"))
                nc.vector.tensor_tensor(v[0:ROT], v[0:ROT], over(const("cos")[0:ROT, :], 4), ALU.mult).then_inc(
                    *mark("rotary"))
                dve.wait_ge(*so_far("rotary"))
                nc.vector.tensor_tensor(flat(v)[0:ROT], flat(v)[0:ROT], flat(tmp)[0:ROT], ALU.add).then_inc(
                    *mark("rotary", "rotated", n))

        def pe_moba_scores(pe):
            pe.wait_ge(*at("rotated", 1))
            pe.wait_ge(*at("mv out", 1))
            for j in range(MB_HEADS):
                b = j
                nc.tensor.matmul(halves(b)[:, 0, 0:C], MQ[:, j, 0:C], MK[:, j, 0:C], start=True, stop=True)
                mm = nc.tensor.matmul(halves(b)[:, 1, :], MQ[:, j, C:2 * C], MK[:, j, :], start=True, stop=True)
                mm.then_inc(*mark("moba_pe", "moba scores", j))

        def pe_moba_turn(pe):
            for j in range(MB_HEADS):
                pe.wait_ge(*at("moba normal", j, 1))
                nc.tensor.transpose(quarters(j)[:, 0, :], SC[:, j, 0:C], ident)
                nc.tensor.transpose(quarters(j)[:, 1, :], SC[:, j, T:T + C], ident)
                mm = nc.tensor.transpose(quarters(j)[:, 2, :], SC[:, j, T + C:2 * T], ident)
                mm.then_inc(*mark("moba_pe", "moba turned", j))

        def pe_moba_out(pe):
            for j in range(MB_HEADS):
                pe.wait_ge(*at("moba p", j))
                if j % 2 == 0:
                    pe.wait_ge(*at("moba p", j + 1))
                o = halves(j // 2)[:, j % 2, :]
                nc.tensor.matmul(o, MV[:, 0, j * C:(j + 1) * C], PT[:, j, 0:T], start=(j % 2 == 0), stop=False,
                                 skip_group_check=True)
                mm = nc.tensor.matmul(o[:, C:T], MV[:, 1, j * C:(j + 1) * C], PT[:, j, T:T + C], start=False,
                                      stop=True, skip_group_check=True)
                if j % 2:
                    mm.then_inc(*mark("moba_pe", "moba o", j // 2))

        def dve_moba(dve):
            for j in range(MB_HEADS):
                dve.wait_ge(*at("moba scores", j))
                nc.vector.scalar_tensor_tensor(SC[:, j, 0:C], halves(j)[:, 0, 0:C], MB_HD ** -0.5,
                                               const("causal")[:, C:2 * C], ALU.mult, ALU.add).then_inc(
                    *mark("moba_vector"))
                nc.vector.scalar_tensor_tensor(SC[:, j, T:2 * T], halves(j)[:, 1, :], MB_HD ** -0.5,
                                               const("causal"), ALU.mult, ALU.add).then_inc(
                    *mark("moba_vector", "moba masked", j))
            for j in range(MB_HEADS):
                dve.wait_ge(*at("moba masked", j))
                nc.vector.tensor_reduce(stat[:, 32 + 2 * j:33 + 2 * j], SC[:, j, 0:C], AX.X, ALU.max).then_inc(
                    *mark("moba_vector"))
                nc.vector.tensor_reduce(stat[:, 33 + 2 * j:34 + 2 * j], SC[:, j, T:2 * T], AX.X, ALU.max).then_inc(
                    *mark("moba_vector"))
                dve.wait_ge(*so_far("moba_vector"))
                nc.vector.tensor_scalar(stat[:, 40 + 2 * j:42 + 2 * j], stat[:, 32 + 2 * j:34 + 2 * j], -1.0, None,
                                        ALU.mult).then_inc(*mark("moba_vector", "moba max", j))
            for j in range(MB_HEADS):
                dve.wait_ge(*at("moba exp", j, 1))
                nc.vector.reciprocal(stat[:, 56 + 2 * j:58 + 2 * j], stat[:, 48 + 2 * j:50 + 2 * j]).then_inc(
                    *mark("moba_vector"))
                dve.wait_ge(*so_far("moba_vector"))
                nc.vector.tensor_scalar(SC[:, j, 0:C], SC[:, j, 0:C], stat[:, 56 + 2 * j:57 + 2 * j], None,
                                        ALU.mult).then_inc(*mark("moba_vector"))
                nc.vector.tensor_scalar(SC[:, j, T:2 * T], SC[:, j, T:2 * T], stat[:, 57 + 2 * j:58 + 2 * j], None,
                                        ALU.mult).then_inc(*mark("moba_vector", "moba normal", j, 1))

        def act_moba(act):
            for j in range(MB_HEADS):
                act.wait_ge(*at("moba max", j))
                nc.scalar.activation(SC[:, j, 0:C], SC[:, j, 0:C], ACT.Exp, bias=stat[:, 40 + 2 * j:41 + 2 * j],
                                     accum_out=stat[:, 48 + 2 * j:49 + 2 * j]).then_inc(*mark("moba_act"))
                nc.scalar.activation(SC[:, j, T:2 * T], SC[:, j, T:2 * T], ACT.Exp,
                                     bias=stat[:, 41 + 2 * j:42 + 2 * j],
                                     accum_out=stat[:, 49 + 2 * j:50 + 2 * j]).then_inc(
                    *mark("moba_act", "moba exp", j, 1))

        def act_moba_out(act):
            for j in range(MB_HEADS):
                act.wait_ge(*at("moba turned", j))
                nc.scalar.activation(PT[:, j, :], banks[j][:, 0:3 * C], ACT.Copy).then_inc(
                    *mark("moba_act", "moba p", j))
            for i in range(2):
                act.wait_ge(*at("moba o", i))
                nc.scalar.activation(mix[:, 4 + 2 * i:6 + 2 * i, :], halves(i), ACT.Copy).then_inc(
                    *mark("moba_act", "mix2", 4 + 2 * i))
                same(("mix2", 5 + 2 * i), ("mix2", 4 + 2 * i))

        def dve_residual(dve, label, scale, following, following_gain):
            for b in range(4):
                dve.wait_ge(*at(label, "bank", b))
                nc.vector.scalar_tensor_tensor(h[:, 2 * b:2 * b + 2, :], halves(4 + b), scale,
                                               h[:, 2 * b:2 * b + 2, :], ALU.mult, ALU.add).then_inc(
                    *mark("residual", label, "added", b))
                if b and following_gain:
                    norm_low(dve, following, b - 1, following_gain)
                elif b:
                    norm_part(dve, nc.vector, following, b - 1)
            if following_gain:
                norm_low(dve, following, 3, following_gain)
            else:
                norm_part(dve, nc.vector, following, 3)

        XQ = view(0, KT, T)
        XS2 = view(2048, 4, 2 * T)
        XPT = view(0, 4, 2 * T)
        xstat = lb

        def pe_xattn_q(pe):
            first_group(pe, "norm_xattn", [("w_xq_2", "cols", 0), ("w_xq_2", "cols", 1)], "xq",
                        lambda b: ("mix2", 7), ("out2", "added", 3))

        def dve_xattn_q(dve):
            norm_reciprocal(dve, "norm_xattn")
            dve.wait_ge(*so_far("norm_rstd"))
            for b in range(4):
                dve.wait_ge(*at("xq", "bank", b))
                nc.vector.tensor_tensor(XQ[:, 2 * b:2 * b + 2, :], halves(b), over(rstd[:, :], 2),
                                        ALU.mult).then_inc(*mark("xq_scaled", "xq scaled", b))

        def pe_xattn(pe):
            def scores(j):
                pe.wait_ge(*at("xq scaled", j))
                for qb in range(2):
                    for i in range(2):
                        mm = nc.tensor.matmul(halves(j)[:, qb, :], XQ[:, 2 * j + i, qb * C:(qb + 1) * C],
                                              xk[:, 2 * j + i, :], start=(i == 0), stop=(i == 1))
                mm.then_inc(*mark("xattn_pe", "x scores", j))

            def turn(j):
                pe.wait_ge(*at("x normal", j))
                for mt in range(2):
                    for qb in range(2):
                        mm = nc.tensor.transpose(quarters(j)[:, 2 * mt + qb, :],
                                                 XS2[:, j, qb * T + mt * C:qb * T + (mt + 1) * C], ident)
                mm.then_inc(*mark("xattn_pe", "x p turned", j))

            def values(j):
                pe.wait_ge(*at("x p", j))
                if j == 0:
                    pe.wait_ge(*at("norm_xattn", "root"))
                for vt in range(2):
                    for mt in range(2):
                        mm = nc.tensor.matmul(halves(4 + j)[:, vt, :],
                                              xv[:, mt, j * XA_HD + vt * C:j * XA_HD + (vt + 1) * C],
                                              XPT[:, j, mt * T:(mt + 1) * T], start=(mt == 0), stop=(mt == 1))
                mm.then_inc(*mark("xattn_pe", "x o", j))

            for j in range(4):
                scores(j)
            for j in range(4):
                turn(j)
                if j:
                    values(j - 1)
            values(3)

        def dve_xattn(dve):
            for j in range(4):
                dve.wait_ge(*at("x scores", j))
                nc.vector.tensor_reduce(xstat[:, 2 * j:2 * j + 2], halves(j), AX.X, ALU.max).then_inc(
                    *mark("xattn_vector"))
                dve.wait_ge(*so_far("xattn_vector"))
                nc.vector.tensor_scalar(xstat[:, 8 + 2 * j:10 + 2 * j], xstat[:, 2 * j:2 * j + 2], -XA_HD ** -0.5,
                                        None, ALU.mult).then_inc(*mark("xattn_vector", "x max", j))
            for j in range(4):
                dve.wait_ge(*at("x exp", j))
                nc.vector.reciprocal(xstat[:, 24 + 2 * j:26 + 2 * j], xstat[:, 16 + 2 * j:18 + 2 * j]).then_inc(
                    *mark("xattn_vector"))
                dve.wait_ge(*so_far("xattn_vector"))
                for qb in range(2):
                    nc.vector.tensor_scalar(XS2[:, j, qb * T:(qb + 1) * T], XS2[:, j, qb * T:(qb + 1) * T],
                                            xstat[:, 24 + 2 * j + qb:25 + 2 * j + qb], None, ALU.mult).then_inc(
                        *mark("xattn_vector", *(("x normal", j) if qb else ())))

        def act_xattn(act):
            for j in range(4):
                act.wait_ge(*at("x max", j))
                for qb in range(2):
                    nc.scalar.activation(XS2[:, j, qb * T:(qb + 1) * T], halves(j)[:, qb, :], ACT.Exp,
                                         bias=xstat[:, 8 + 2 * j + qb:9 + 2 * j + qb], scale=XA_HD ** -0.5,
                                         accum_out=xstat[:, 16 + 2 * j + qb:17 + 2 * j + qb]).then_inc(
                        *mark("xattn_act", *(("x exp", j) if qb else ())))
            for j in range(4):
                act.wait_ge(*at("x p turned", j))
                nc.scalar.activation(XPT[:, j, :], banks[j][:, :], ACT.Copy).then_inc(*mark("xattn_act", "x p", j))
                if j:
                    x_out(act, j - 1)
            x_out(act, 3)

        def x_out(act, j):
            act.wait_ge(*at("x o", j))
            nc.scalar.activation(mix16[:, 2 * j:2 * j + 2, 0, :], halves(4 + j), ACT.Copy).then_inc(
                *mark("xattn_act", "mix3 high", j))

        def dve_x_out(dve):
            for j in range(4):
                dve.wait_ge(*at("mix3 high", j))
                nc.vector.tensor_tensor(mix16[:, 2 * j:2 * j + 2, 1, :], halves(4 + j), mix16[:, 2 * j:2 * j + 2, 0, :],
                                        ALU.subtract).then_inc(*mark("mix3_low", "mix3", 2 * j))
                same(("mix3", 2 * j + 1), ("mix3", 2 * j))

        relu = [view(8192 + 512 * i, 2, T) for i in range(4)]
        squared = [view(10240 + 512 * i, 2, T) for i in range(2)]
        hid2 = hidden16(FF2T)

        def pe_mlp(pe):
            first_group(pe, "norm_mlp", [("w_ff1_2", "cols", 0), ("w_ff1_2", "cols", 1)], "ff1",
                        lambda b: ("x p", b), ("xo", "added", 3))
            for b in range(4, FF2T // 2):
                pe.wait_ge(*at("relu", b - 4))
                for i in range(2):
                    mm = wide(pe, ("w_ff1_2", "cols", b // 2), 2 * (b % 2) + i, b % 4, i)
                mm.then_inc(*mark("projected", "ff1", "bank", b))
                if b % 2:
                    split_used(("w_ff1_2", "cols", b // 2), ("ff1", "bank", b))

        def dve_mlp(dve):
            def low(b):
                dve.wait_ge(*at("hid2 high", b))
                nc.vector.tensor_tensor(hid2[:, 2 * b:2 * b + 2, 1, :], squared[b % 2], hid2[:, 2 * b:2 * b + 2, 0, :],
                                        ALU.subtract).then_inc(*mark("mlp_low", "hid2", 2 * b))
                same(("hid2", 2 * b + 1), ("hid2", 2 * b))

            norm_reciprocal(dve, "norm_mlp")
            dve.wait_ge(*so_far("norm_rstd"))
            for b in range(FF2T // 2):
                dve.wait_ge(*at("ff1", "bank", b))
                if b >= 4:
                    dve.wait_ge(*at("squared", b - 4))
                nc.vector.scalar_tensor_tensor(relu[b % 4], halves(b % 4), 0.0, over(rstd[:, :], 2), ALU.max,
                                               ALU.mult).then_inc(*mark("mlp_relu", "relu", b))
                n, q = split_turn(SPLIT_2, b)
                split_low(dve, n, q)
                if b:
                    low(b - 1)
            low(b)
            split_low(dve, n, (2, 3))
            for n in range(n + 1, len(SPLIT)):
                split_low(dve, n, range(4))

        def act_mlp(act):
            for b in range(FF2T // 2):
                n, q = split_turn(SPLIT_2, b)
                split_high(act, n, q)
                act.wait_ge(*at("relu", b))
                if b >= 2:
                    act.wait_ge(*at("hid2", 2 * (b - 2)))
                nc.scalar.activation(squared[b % 2], relu[b % 4], ACT.Square).then_inc(
                    *mark("mlp_square", "squared", b))
                act.wait_ge(*so_far("mlp_square"))
                nc.scalar.activation(hid2[:, 2 * b:2 * b + 2, 0, :], squared[b % 2], ACT.Copy).then_inc(
                    *mark("mlp_high", "hid2 high", b))
            split_high(act, n, (2, 3))
            for n in range(n + 1, len(SPLIT)):
                split_high(act, n, range(4))

        out_tok = xv

        def pe_final(pe):
            for half in range(2):
                for c in range(NC_):
                    for i in range(4):
                        m = 4 * half + i
                        pe.wait_ge(*at("final", "gained", m))
                        mm = nc.tensor.transpose(quarters(2 * half + c)[:, i, :], hg[:, m, c * C:(c + 1) * C], ident)
                    mm.then_inc(*mark("final_pe", "out turned", 2 * half + c))
            pe.wait_ge(*at("final", "summed", 3))
            pe.wait_ge(*at("ff2", "added", 3))
            for c in range(NC_):
                for i in range(2):
                    mm = nc.tensor.matmul(banks[4][:, c:c + 1], ssum[:, 256 * i + c * C:256 * i + (c + 1) * C],
                                          ones[:, 0:1], start=(i == 0), stop=(i == 1))
            mm.then_inc(*mark("final_pe", "final", "total"))

        def dve_final(dve):
            dve.wait_ge(*at("final root"))
            nc.vector.reciprocal(rcol[:, :], rms[:, 0:NC_]).then_inc(*mark("final_vector", "final column"))
            dve.wait_ge(*so_far("final_vector"))
            for b in (0, 2):
                dve.wait_ge(*at("out turned", b))
                c, half = b % 2, b // 2
                nc.vector.tensor_scalar(out_tok[:, c, 512 * half:512 * half + 512], banks[b][:, :], rcol[:, c:c + 1],
                                        None, ALU.mult).then_inc(*mark("final_vector", "out written", b))

        def act_final(act):
            act.wait_ge(*at("final", "total"))
            nc.scalar.activation(rms[:, 0:NC_], banks[4][:, 0:NC_], ACT.Sqrt, bias=eps[:, 0:1],
                                 scale=1.0 / D).then_inc(*mark("final_act", "final root"))
            act.wait_ge(*at("final column"))
            for b in (1, 3):
                act.wait_ge(*at("out turned", b))
                c, half = b % 2, b // 2
                nc.scalar.activation(out_tok[:, c, 512 * half:512 * half + 512], banks[b][:, :], ACT.Copy,
                                     scale=rcol[:, c:c + 1]).then_inc(*mark("final_act", "out written", b))
            for b in (1, 0, 3, 2):
                act.wait_ge(*at("out written", b))
                c, half = b % 2, b // 2
                act.dma_start(out[0, c * C:(c + 1) * C, 512 * half:512 * half + 512],
                              out_tok[:, c, 512 * half:512 * half + 512]).then_inc(
                    *mark("out_stored", *(("out stored",) if b == 2 else ()), by=16))

        @block.gpsimd
        def _(pool):
            pool.wait_ge(*at("x landed"))
            pool.dma_start(consts[:, 3 * P:], w["constants"][:, 3 * P:]).then_inc(
                *mark("constants_landed", "constants landed", by=16))
            load_lora(pool)
            load_mem(pool)
            pool_project1(pool)
            pool_rwkv_prepare(pool)
            pool_ssd(pool)
            load_gate(pool)
            pool_bonus(pool)
            for c in range(NC_):
                pool_rwkv_chunk(pool, c)
            pool_ffn(pool)
            pool_norm_sum(pool, "pre_ffn")
            pool_hidden(pool)
            for n in ("norm_mix", "norm_xattn", "norm_mlp"):
                pool_norm_sum(pool, n)

        @block.tensor
        def _(pe):
            pe_load(pe)
            pe_project1(pe)
            pe_rwkv_turn(pe)
            norm_total(pe, "mem", 0, ("proj1 out", 12))
            pe_ssd(pe)
            pe_ssd_norm(pe)
            column_rstd(pe, "mem", 7, ("mem", "root"))
            for c in range(NC_):
                pe_rwkv_chunk(pe, c)
            pe_rwkv_end(pe)
            narrow(pe, "w_out", KT, mix, lambda k: ("mix1", k), "out1",
                   lambda b: ("variance root", 1) if b > 1 else ("centred", b))
            norm_total(pe, "post_mix", 0, ("mix1", 7))
            pe_ffn_up(pe)
            narrow(pe, "ffn_w_down", FFT, hid, lambda k: ("hid", k), "down1",
                   lambda b: ("pre_ffn", "root") if b == 0 else ("post_mix", "added", 7))
            norm_total(pe, "post_ffn", 0, ("up scaled", FFT - 1))
            pe_project2(pe)
            pe_hgrn_states(pe)
            pe_moba_scores(pe)
            pe_hgrn_out(pe)
            pe_moba_turn(pe)
            pe_hgrn_norm(pe)
            pe_moba_out(pe)
            narrow(pe, "w_out_2", KT, mix, lambda k: ("mix2", k), "out2",
                   lambda b: ("o root", b) if b < 2 else ("o copied", b - 2), order=(1, 0))
            pe_xattn_q(pe)
            pe_xattn(pe)
            narrow(pe, "w_xo_2", KT, mix16, lambda k: ("mix3", k), "xo", lambda b: ("mix3", 2 * b))
            pe_mlp(pe)
            narrow(pe, "w_ff2_2", FF2T, hid2, lambda k: ("hid2", k), "ff2",
                   lambda b: ("norm_mlp", "root") if b == 0 else ("xo", "added", 3))
            pe_final(pe)

        @block.scalar
        def _(act):
            act.dma_start(params[:, :], w["parameters"]).then_inc(*mark("parameters_landed", "parameters landed", by=16))
            act.wait_ge(*at("parameters landed"))
            act.wait_ge(*at("pads"))
            norm_act(act, "pre_mix", h, "pre_mix_norm", lambda m: ("h", m // 2))
            norm_root(act, "pre_mix", 4)
            act_pre_high(act)
            for n in range(2):
                split_high(act, n, range(4))
            act_mem_norm(act)
            split_high(act, 2, range(4))
            act.wait_ge(*at("constants landed"))
            act_lora(act)
            act_rwkv_prepare(act)
            act_rwkv_exponentials(act)
            act_rwkv_turn_v(act)
            act_ssd_silu(act)
            act_rwkv_turn(act)
            act_z_silu(act)
            act.wait_ge(*at("dt done"))
            norm_root(act, "mem", 0, W_SCALE ** 2 / D, 3)
            mem_high(act, 0)
            act_ssd(act)
            act_mem_column(act)
            mem_high(act, 1)
            for c in range(NC_):
                act_rwkv_chunk(act, c)
            act_rwkv_end(act)
            for n in range(SPLIT_1, SPLIT_1 + 2):
                split_high(act, n, range(4))
            post_norm_act(act, "post_mix", "out1")
            norm_root(act, "post_mix", 0)
            norm_act(act, "pre_ffn", h, "pre_ffn_norm", lambda m: ("post_mix", "added", m), split=True)
            norm_root(act, "pre_ffn", 4, W_SCALE ** 2 / D, 3)
            act_ffn(act)
            act.wait_ge(*at("hid", FFT - 1))
            split_high(act, SPLIT_FROM["w_in_2"], range(4))
            post_norm_act(act, "post_ffn", "down1")
            norm_root(act, "post_ffn", 0, eps_column=3)
            norm_act(act, "norm_mix", h, "norm_mix_2", lambda m: ("post_ffn", "added", m), split=True)
            split_high(act, SPLIT_FROM["w_in_2"] + 1, range(4))
            norm_root(act, "norm_mix", 4, W_SCALE ** 2 / D, 3)
            act_project2(act)
            act_hgrn(act)
            act_moba_values(act)
            act_moba(act)
            act_hgrn_end(act)
            act_moba_out(act)
            for n in range(2):
                split_high(act, SPLIT_FROM["w_xq_2"] + n, range(4))
            norm_act(act, "norm_xattn", h, "norm_xattn_2", lambda m: ("out2", "added", m // 2), split=True)
            norm_root(act, "norm_xattn", 4, W_SCALE ** 2 / D, 3)
            for n in range(2):
                split_high(act, SPLIT_FROM["w_xo_2"] + n, range(4))
            act_xattn(act)
            for n in range(SPLIT_2, SPLIT_2 + 2):
                split_high(act, n, range(4))
            norm_act(act, "norm_mlp", h, "norm_mlp_2", lambda m: ("xo", "added", m // 2), split=True)
            norm_root(act, "norm_mlp", 4, W_SCALE ** 2 / D, 3)
            act_mlp(act)
            norm_act(act, "final", h, "norm_final_2", lambda m: ("ff2", "added", m // 2))
            act_final(act)

        @block.vector
        def _(dve):
            dve_load(dve)
            norm_sum(dve, "pre_mix")
            dve_project1_rwkv(dve)
            dve_rwkv_prepare(dve)
            dve_ssd_conv(dve, 7, 9)
            dve_rwkv_scaled(dve)
            dve_dt(dve)
            dve_ssd_conv(dve, 9, 13)
            dve_ssd(dve)
            dve.wait_ge(*so_far("norm_rstd"))
            for c in range(NC_):
                dve_rwkv_chunk(dve, c)
                if c == 0:
                    dve_bonus(dve)
            dve_rwkv_end(dve)
            for n in range(SPLIT_1, SPLIT_1 + 2):
                split_low(dve, n, range(4))
            norm_sum(dve, "post_mix")
            norm_reciprocal(dve, "post_mix")
            post_norm_apply(dve, "post_mix", "out1", "post_mix_norm", "pre_ffn", "pre_ffn_norm")
            dve_ffn(dve)
            dve.wait_ge(*at("hid", FFT - 1))
            split_low(dve, SPLIT_FROM["w_in_2"], range(4))
            norm_sum(dve, "post_ffn")
            norm_reciprocal(dve, "post_ffn")
            post_norm_apply(dve, "post_ffn", "down1", "post_ffn_norm", "norm_mix", "norm_mix_2")
            split_low(dve, SPLIT_FROM["w_in_2"] + 1, range(4))
            dve_project2(dve)
            dve_hgrn(dve)
            dve_rotary(dve)
            dve_hgrn_states(dve)
            dve_moba(dve)
            dve_hgrn_end(dve)
            for n in range(2):
                split_low(dve, SPLIT_FROM["w_xq_2"] + n, range(4))
            dve_residual(dve, "out2", 1.0, "norm_xattn", "norm_xattn_2")
            split_low(dve, SPLIT_FROM["w_xo_2"], range(4))
            dve_xattn_q(dve)
            dve_xattn(dve)
            split_low(dve, SPLIT_FROM["w_xo_2"] + 1, range(4))
            dve_x_out(dve)
            for n in range(SPLIT_2, SPLIT_2 + 2):
                split_low(dve, n, range(4))
            dve_residual(dve, "xo", 1.0 / W_SCALE, "norm_mlp", "norm_mlp_2")
            dve_mlp(dve)
            dve_residual(dve, "ff2", 1.0 / W_SCALE, "final", None)
            dve_final(dve)

    return steps.steps


_WEIGHTS = ["w_in", "w_out", "ffn_w_up", "ffn_w_down", "w_in_2", "w_out_2", "w_xq_2", "w_xk_2", "w_xv_2",
            "w_xo_2", "w_ff1_2", "w_ff2_2"]
_OTHERS = ["x", "mem_2", "rwkv_w2", "rwkv_a2", "rwkv_g2"]


def kernel(**inputs):
    import concourse.bacc as _bacc
    from concourse.bass_utils import run_bass_kernel_spmd as _run

    arrays = {name: np.ascontiguousarray(np.asarray(inputs[name])[0]) for name in _WEIGHTS}
    arrays |= {name: np.ascontiguousarray(inputs[name]) for name in _OTHERS}
    arrays["parameters"] = parameter_table(inputs)
    arrays["constants"] = constant_table()

    def program(known):
        nc = _bacc.Bacc("TRN2", target_bir_lowering=False, num_devices=1)
        w = {name: nc.dram_tensor(f"in_{name}_dram", a.shape, mybir.dt.from_np(a.dtype),
                                  kind="ExternalInput").ap() for name, a in arrays.items()}
        out = nc.dram_tensor("out_0_dram", (1, T, D), F32, kind="ExternalOutput").ap()
        return nc, build(nc, w, out, known)

    _, counted = program(None)
    nc, _ = program(counted)
    r = _run(nc, [{f"in_{name}_dram": a for name, a in arrays.items()}], core_ids=[0])
    return r.results[0]["out_0_dram"]
```
